# Optimizing a Trainium2 kernel written in Bass

```python
import math
import jax, jax.numpy as jnp
from jax import lax
import numpy as np

D_MODEL = 1024
BATCH = 1
SEQ = 512
DEPTH = 2
DEC_BATCH = 8
DEC_SEQ = 8
PAST_LEN = 1024
PAGE_SIZE = 128

N_A = DEPTH // 2
N_B = DEPTH - N_A
DN_HEADS = 6
DN_DK = 128
DN_DV = 128
DN_CONV = 4
DN_CHUNK = 64
DN_QKV = DN_HEADS * (2 * DN_DK + DN_DV)
DN_WIDTH = DN_HEADS * DN_DV
SB_HEADS = 12
SB_DH = 64
SB_WIDTH = SB_HEADS * SB_DH
SB_BIAS_INIT = -9.0
Q_BLOCK = 128
N_MEM = 256
MEM_HEADS = 4
MEM_DH = 64
MEM_WIDTH = MEM_HEADS * MEM_DH
D_FF = 2816
FFN_CONV = 3
EPS = 1e-6
A_DN_COLS = DN_QKV + DN_WIDTH + 2 * DN_HEADS
A_IN_COLS = A_DN_COLS + MEM_WIDTH
A_MIX = DN_WIDTH + MEM_WIDTH
B_IN_COLS = SB_WIDTH + MEM_WIDTH
B_MIX = SB_WIDTH + MEM_WIDTH

kernel_name = "yoco_deltanet_stickbreaking_decoder_step"

def rms_norm(x, gain):
    xf = x.astype(jnp.float32)
    y = xf * lax.rsqrt(jnp.mean(xf * xf, axis=-1, keepdims=True) + EPS)
    return (y * gain.astype(jnp.float32)).astype(x.dtype)

def l2_normalize(x):
    xf = x.astype(jnp.float32)
    return xf * lax.rsqrt(jnp.sum(xf * xf, axis=-1, keepdims=True) + EPS)

def causal_conv(x, state, w, b=None):
    width, t = w.shape[0], x.shape[1]
    xp = jnp.concatenate([state.astype(x.dtype), x], axis=1)
    y = xp[:, 0:t] * w[0]
    for i in range(1, width):
        y = y + xp[:, i:i + t] * w[i]
    if b is not None:
        y = y + b
    return y, xp[:, xp.shape[1] - (width - 1):]

def gated_delta_rule(q, k, v, beta, g, s0):
    bsz, t, nh, dk = q.shape
    dv = v.shape[-1]
    c = min(DN_CHUNK, t)
    n = -(-t // c)
    pad = n * c - t

    def prep(a):
        a = jnp.pad(a, [(0, 0), (0, pad)] + [(0, 0)] * (a.ndim - 2))
        a = a.reshape((bsz, n, c) + a.shape[2:])
        return jnp.moveaxis(a, 3, 1)

    q, k, v, beta, g = (prep(a) for a in (q * dk ** -0.5, k, v, beta, g))
    gc = jnp.cumsum(g, axis=-1)
    idx = jnp.arange(c)
    tril = idx[:, None] >= idx[None, :]
    strict = idx[:, None] > idx[None, :]
    gamma = jnp.exp(jnp.where(tril, gc[..., :, None] - gc[..., None, :], -jnp.inf))
    kb = k * beta[..., None]
    low = jnp.where(strict, jnp.einsum('bhncd,bhnsd->bhncs', kb, k) * gamma, 0.0)
    rhs = jnp.concatenate([v * beta[..., None], kb * jnp.exp(gc)[..., None]], axis=-1)
    sol = lax.linalg.triangular_solve(jnp.eye(c, dtype=low.dtype) + low, rhs,
                                      left_side=True, lower=True)
    u, w = sol[..., :dv], sol[..., dv:]
    attn = jnp.einsum('bhncd,bhnsd->bhncs', q, k) * gamma
    q_dec = q * jnp.exp(gc)[..., None]
    g_last = gc[..., -1]
    k_dec = k * jnp.exp(g_last[..., None] - gc)[..., None]

    def step(s, xs):
        u_c, w_c, attn_c, qd_c, kd_c, gl_c = xs
        v_new = u_c - jnp.einsum('bhcd,bhde->bhce', w_c, s)
        o = jnp.einsum('bhcd,bhde->bhce', qd_c, s) + jnp.einsum('bhcs,bhse->bhce', attn_c, v_new)
        s = s * jnp.exp(gl_c)[..., None, None] + jnp.einsum('bhcd,bhce->bhde', kd_c, v_new)
        return s, o

    xs = tuple(jnp.moveaxis(a, 2, 0) for a in (u, w, attn, q_dec, k_dec, g_last))
    s_final, o = lax.scan(step, s0, xs)
    o = jnp.transpose(o, (1, 0, 3, 2, 4)).reshape(bsz, n * c, nh, dv)[:, :t]
    return o, s_final

def deltanet_mixer(proj, conv_state, s0, conv_w, a_log, dt_bias, o_gain):
    bsz, t = proj.shape[:2]
    qkv, conv_new = causal_conv(proj[..., :DN_QKV], conv_state, conv_w)
    qkv = jax.nn.silu(qkv)
    hk = DN_HEADS * DN_DK
    q = l2_normalize(qkv[..., :hk].reshape(bsz, t, DN_HEADS, DN_DK))
    k = l2_normalize(qkv[..., hk:2 * hk].reshape(bsz, t, DN_HEADS, DN_DK))
    v = qkv[..., 2 * hk:].reshape(bsz, t, DN_HEADS, DN_DV).astype(jnp.float32)
    z = proj[..., DN_QKV:DN_QKV + DN_WIDTH].reshape(bsz, t, DN_HEADS, DN_DV).astype(jnp.float32)
    b_in = proj[..., DN_QKV + DN_WIDTH:DN_QKV + DN_WIDTH + DN_HEADS].astype(jnp.float32)
    a_in = proj[..., DN_QKV + DN_WIDTH + DN_HEADS:A_DN_COLS].astype(jnp.float32)
    beta = jax.nn.sigmoid(b_in)
    g = -jnp.exp(a_log.astype(jnp.float32)) * jax.nn.softplus(a_in + dt_bias.astype(jnp.float32))
    o, s_new = gated_delta_rule(q, k, v, beta, g, s0.astype(jnp.float32))
    o = rms_norm(o, o_gain) * jax.nn.silu(z)
    return o.reshape(bsz, t, DN_WIDTH).astype(proj.dtype), conv_new, s_new.astype(s0.dtype)

def memory_kv(mem, mem_norm, w_mem_kv):
    mn = rms_norm(mem[None], mem_norm[:, None, None, :])
    kv = jnp.einsum('lbmd,lde->lbme', mn, w_mem_kv)
    shp = kv.shape[:3] + (MEM_HEADS, MEM_DH)
    return kv[..., :MEM_WIDTH].reshape(shp), kv[..., MEM_WIDTH:].reshape(shp)

def memory_attend(q, mk, mv):
    bsz, t = q.shape[:2]
    qh = q.reshape(bsz, t, MEM_HEADS, MEM_DH)
    s = jnp.einsum('bthd,bmhd->bhtm', qh, mk).astype(jnp.float32) * (MEM_DH ** -0.5)
    p = jax.nn.softmax(s, axis=-1).astype(mv.dtype)
    return jnp.einsum('bhtm,bmhd->bthd', p, mv).reshape(bsz, t, MEM_WIDTH)

def conv_ffn(x, state, w_up, conv_w, conv_b, w_down):
    h, state_new = causal_conv(x @ w_up, state, conv_w, conv_b)
    y = jax.nn.gelu(h[..., :D_FF], approximate=True) * h[..., D_FF:]
    return y @ w_down, state_new

def stick_breaking_block(q, k, v, bias, q_pos, k_pos):
    z = jnp.einsum('bqhd,bkhd->bhqk', q, k).astype(jnp.float32) * (SB_DH ** -0.5)
    z = z + bias.astype(jnp.float32)[None, :, None, None]
    mask = k_pos[None, :] < q_pos[:, None]
    log_keep = jnp.where(mask, jax.nn.log_sigmoid(-z), 0.0)
    incl = lax.cumsum(log_keep, axis=3, reverse=True)
    excl = jnp.concatenate([incl[..., 1:], jnp.zeros_like(incl[..., :1])], axis=-1)
    wts = jnp.where(mask, jnp.exp(jax.nn.log_sigmoid(z) + excl), 0.0)
    return jnp.einsum('bhqk,bkhd->bqhd', wts.astype(v.dtype), v)

def stick_breaking(q, k, v, bias, q_pos, k_pos):
    bsz, tq = q.shape[:2]
    qb = min(Q_BLOCK, tq)
    n = -(-tq // qb)
    pad = n * qb - tq
    qp = jnp.pad(q, ((0, 0), (0, pad), (0, 0), (0, 0))).reshape(bsz, n, qb, SB_HEADS, SB_DH)
    qp = jnp.transpose(qp, (1, 0, 2, 3, 4))
    pp = jnp.pad(q_pos, (0, pad)).reshape(n, qb)
    out = lax.map(lambda a: stick_breaking_block(a[0], k, v, bias, a[1], k_pos), (qp, pp))
    return jnp.transpose(out, (1, 0, 2, 3, 4)).reshape(bsz, n * qb, SB_HEADS, SB_DH)[:, :tq]

def run_trunk(x, q_pos, mem_k, mem_v, dn_conv0, dn_s0, ffn_conv0, k_past, v_past, k_pos_past,
              norm_mix_pre, norm_mix_post, norm_ffn_pre, norm_ffn_post,
              w_in_a, w_out_a, dn_conv_w, dn_a_log, dn_dt_bias, dn_o_gain,
              kv_norm, w_kv, w_in_b, w_out_b, sb_bias,
              ffn_w_up, ffn_conv_w, ffn_conv_b, ffn_w_down):
    bsz, t = x.shape[:2]
    h = x
    dn_s_new, dn_conv_new, ffn_conv_new = [], [], []
    k_new = v_new = k_all = v_all = k_pos = None
    for l in range(DEPTH):
        xn = rms_norm(h, norm_mix_pre[l])
        if l < N_A:
            proj = xn @ w_in_a[l]
            dn_out, c_new, s_new = deltanet_mixer(proj[..., :A_DN_COLS], dn_conv0[l], dn_s0[l],
                                                  dn_conv_w[l], dn_a_log[l], dn_dt_bias[l], dn_o_gain[l])
            dn_conv_new.append(c_new)
            dn_s_new.append(s_new)
            mem_out = memory_attend(proj[..., A_DN_COLS:], mem_k[l], mem_v[l])
            mix = jnp.concatenate([dn_out, mem_out], axis=-1) @ w_out_a[l]
        else:
            j = l - N_A
            proj = xn @ w_in_b[j]
            q = proj[..., :SB_WIDTH].reshape(bsz, t, SB_HEADS, SB_DH)
            sb_out = stick_breaking(q, k_all, v_all, sb_bias[j], q_pos, k_pos).reshape(bsz, t, SB_WIDTH)
            mem_out = memory_attend(proj[..., SB_WIDTH:], mem_k[l], mem_v[l])
            mix = jnp.concatenate([sb_out, mem_out], axis=-1) @ w_out_b[j]
        h = h + rms_norm(mix, norm_mix_post[l])
        f, fc_new = conv_ffn(rms_norm(h, norm_ffn_pre[l]), ffn_conv0[l], ffn_w_up[l],
                             ffn_conv_w[l], ffn_conv_b[l], ffn_w_down[l])
        ffn_conv_new.append(fc_new)
        h = h + rms_norm(f, norm_ffn_post[l])
        if l == N_A - 1:
            kv = rms_norm(h, kv_norm) @ w_kv
            k_new = kv[..., :SB_WIDTH].reshape(bsz, t, SB_HEADS, SB_DH)
            v_new = kv[..., SB_WIDTH:].reshape(bsz, t, SB_HEADS, SB_DH)
            k_all = jnp.concatenate([k_past.astype(k_new.dtype), k_new], axis=1)
            v_all = jnp.concatenate([v_past.astype(v_new.dtype), v_new], axis=1)
            k_pos = jnp.concatenate([k_pos_past, q_pos])
    return (h, jnp.stack(dn_s_new), jnp.stack(dn_conv_new), jnp.stack(ffn_conv_new), k_new, v_new)

def setup_inputs(seed: int = 0) -> dict:
    key = jax.random.key(seed)
    ks = iter(jax.random.split(key, 48))
    f32 = jnp.float32

    def nrm(shape, scale=1.0):
        return jax.random.normal(next(ks), shape, f32) * scale

    def gain(shape):
        return 1.0 + nrm(shape, 0.02)

    n_pages = PAST_LEN // PAGE_SIZE
    n_used = DEC_BATCH * n_pages
    n_phys = n_used + max(1, n_used // 4)
    page_table = jax.random.permutation(next(ks), n_phys)[:n_used].reshape(DEC_BATCH, n_pages).astype(jnp.int32)
    dt = jnp.exp(jax.random.uniform(next(ks), (N_A, DN_HEADS), f32,
                                    minval=math.log(1e-3), maxval=math.log(1e-1)))
    return {
        "x_prompt": nrm((BATCH, SEQ, D_MODEL)),
        "x_sample": nrm((DEC_BATCH, DEC_SEQ, D_MODEL)),
        "mem_prompt": nrm((BATCH, N_MEM, D_MODEL)),
        "cache_k": nrm((n_phys, PAGE_SIZE, SB_HEADS, SB_DH)),
        "cache_v": nrm((n_phys, PAGE_SIZE, SB_HEADS, SB_DH)),
        "page_table": page_table,
        "cache_mem_k": nrm((DEPTH, DEC_BATCH, N_MEM, MEM_HEADS, MEM_DH)),
        "cache_mem_v": nrm((DEPTH, DEC_BATCH, N_MEM, MEM_HEADS, MEM_DH)),
        "state_dn": nrm((N_A, DEC_BATCH, DN_HEADS, DN_DK, DN_DV), 0.1),
        "state_dn_conv": nrm((N_A, DEC_BATCH, DN_CONV - 1, DN_QKV)),
        "state_ffn_conv": nrm((DEPTH, DEC_BATCH, FFN_CONV - 1, 2 * D_FF)),
        "norm_mix_pre": gain((DEPTH, D_MODEL)),
        "norm_mix_post": gain((DEPTH, D_MODEL)),
        "norm_ffn_pre": gain((DEPTH, D_MODEL)),
        "norm_ffn_post": gain((DEPTH, D_MODEL)),
        "w_in_a": nrm((N_A, D_MODEL, A_IN_COLS), D_MODEL ** -0.5),
        "w_out_a": nrm((N_A, A_MIX, D_MODEL), A_MIX ** -0.5),
        "dn_conv_w": nrm((N_A, DN_CONV, DN_QKV), DN_CONV ** -0.5),
        "dn_a_log": jnp.log(jax.random.uniform(next(ks), (N_A, DN_HEADS), f32, minval=1.0, maxval=16.0)),
        "dn_dt_bias": dt + jnp.log(-jnp.expm1(-dt)),
        "dn_o_gain": gain((N_A, DN_DV)),
        "kv_norm": gain((D_MODEL,)),
        "w_kv": nrm((D_MODEL, 2 * SB_WIDTH), D_MODEL ** -0.5),
        "w_in_b": nrm((N_B, D_MODEL, B_IN_COLS), D_MODEL ** -0.5),
        "w_out_b": nrm((N_B, B_MIX, D_MODEL), B_MIX ** -0.5),
        "sb_bias": SB_BIAS_INIT + nrm((N_B, SB_HEADS), 0.5),
        "mem_norm": gain((DEPTH, D_MODEL)),
        "w_mem_kv": nrm((DEPTH, D_MODEL, 2 * MEM_WIDTH), D_MODEL ** -0.5),
        "ffn_w_up": nrm((DEPTH, D_MODEL, 2 * D_FF), D_MODEL ** -0.5),
        "ffn_conv_w": nrm((DEPTH, FFN_CONV, 2 * D_FF), FFN_CONV ** -0.5),
        "ffn_conv_b": nrm((DEPTH, 2 * D_FF), 0.01),
        "ffn_w_down": nrm((DEPTH, D_FF, D_MODEL), D_FF ** -0.5),
    }

def reference(x_prompt, x_sample, mem_prompt, cache_k, cache_v, page_table, cache_mem_k, cache_mem_v,
              state_dn, state_dn_conv, state_ffn_conv,
              norm_mix_pre, norm_mix_post, norm_ffn_pre, norm_ffn_post,
              w_in_a, w_out_a, dn_conv_w, dn_a_log, dn_dt_bias, dn_o_gain,
              kv_norm, w_kv, w_in_b, w_out_b, sb_bias, mem_norm, w_mem_kv,
              ffn_w_up, ffn_conv_w, ffn_conv_b, ffn_w_down):
    weights = (norm_mix_pre, norm_mix_post, norm_ffn_pre, norm_ffn_post,
               w_in_a, w_out_a, dn_conv_w, dn_a_log, dn_dt_bias, dn_o_gain,
               kv_norm, w_kv, w_in_b, w_out_b, sb_bias,
               ffn_w_up, ffn_conv_w, ffn_conv_b, ffn_w_down)
    bp, tp = x_prompt.shape[:2]
    dtp = x_prompt.dtype
    mem_k_p, mem_v_p = memory_kv(mem_prompt, mem_norm, w_mem_kv)
    y_prompt, dn_s_p, dn_c_p, ffn_c_p, k_p, v_p = run_trunk(
        x_prompt, jnp.arange(tp, dtype=jnp.int32), mem_k_p, mem_v_p,
        jnp.zeros((N_A, bp, DN_CONV - 1, DN_QKV), dtp),
        jnp.zeros((N_A, bp, DN_HEADS, DN_DK, DN_DV), dtp),
        jnp.zeros((DEPTH, bp, FFN_CONV - 1, 2 * D_FF), dtp),
        jnp.zeros((bp, 0, SB_HEADS, SB_DH), dtp), jnp.zeros((bp, 0, SB_HEADS, SB_DH), dtp),
        jnp.zeros((0,), jnp.int32), *weights)
    bs, ts = x_sample.shape[:2]
    past_len = page_table.shape[1] * cache_k.shape[1]
    k_past = cache_k[page_table].reshape(bs, past_len, SB_HEADS, SB_DH)
    v_past = cache_v[page_table].reshape(bs, past_len, SB_HEADS, SB_DH)
    y_sample, dn_s_s, dn_c_s, ffn_c_s, k_s, v_s = run_trunk(
        x_sample, past_len + jnp.arange(ts, dtype=jnp.int32), cache_mem_k, cache_mem_v,
        state_dn_conv, state_dn, state_ffn_conv,
        k_past, v_past, jnp.arange(past_len, dtype=jnp.int32), *weights)
    return (y_prompt, y_sample, dn_s_p, dn_c_p, ffn_c_p, k_p, v_p, mem_k_p, mem_v_p,
            dn_s_s, dn_c_s, ffn_c_s, k_s, v_s)


_drawn_inputs = setup_inputs


def setup_inputs(seed=0):
    import zlib

    import numpy as np

    out = dict(_drawn_inputs(seed))
    spreads = {}
    factors = {'norm_ffn_post': 3.559,
     'dn_o_gain': 3.332,
     'kv_norm': 2.726,
     'mem_norm': 2.902,
     'ffn_conv_b': 5.122}
    for name, (base, spread) in spreads.items():
        noise = np.random.default_rng([zlib.crc32(name.encode()), seed]).standard_normal(out[name].shape)
        drawn = base * np.exp(spread * noise) if base else spread * noise
        out[name] = __import__('jax').numpy.asarray(drawn.astype(out[name].dtype))
    for name, factor in factors.items():
        out[name] = (out[name] * factor).astype(out[name].dtype)
    return out
```

```python
from contextlib import ExitStack

import numpy as np
import concourse.bass as bass
from concourse import mybir
from concourse.alu_op_type import AluOpType as ALU

ACT = mybir.ActivationFunctionType
F32 = mybir.dt.float32
I32 = mybir.dt.int32
AX_X = mybir.AxisListType.X

P = 128
D_MODEL = 1024
KD = D_MODEL // P
SEQ = 512
DEC_B, DEC_T = 8, 8
NS = DEC_B * DEC_T
NT = SEQ + NS
HALF = NT // 2
DN_H = 6
QKV = 3 * DN_H
DN_TAPS, FF_TAPS = 4, 3
FF = 2816 // P
SB_H, DH = 12, 64
SBC = SB_H * DH // P
MEMC = 2
N_MEM = 256
PAGES = 8
NC = PAGES + 1
QC = 2 * DEC_T
ZW = PAGES * P + NS
SLOT = FF // 2 * P
NEG = -1.0e30
EPS = 1e-6
EXP_LN = "natural_log_exp_and_others"
NCH = SEQ // P
LEVELS = 7
LEVELS_S = 3


class Steps:

    def __init__(self, sem, names):
        self.sem, self.names, self.n, self.next = sem, names, len(names), 0

    def mark(self, name):
        assert self.names[self.next % self.n] == name, (name, self.names[self.next % self.n])
        self.next += 1
        return 1

    def at(self, name, turn=0):
        return (turn + 1) * self.n + self.names.index(name) + 1


def constants():
    s, t = np.arange(P)[:, None], np.arange(P)[None, :]
    same8 = s // 8 == t // 8
    f = lambda m: m.astype(np.float32)
    neg = lambda m: np.where(m, 0.0, NEG).astype(np.float32)
    levels = [f((s >> (l + 1) == t >> (l + 1)) & (((t >> l) & 1) == 1) & (((s >> l) & 1) == 0))
              for l in range(LEVELS)]
    common = np.concatenate([np.ones((P, P), np.float32), f(s == t)], 1)
    dn = np.concatenate(levels + [f(s <= t), neg(s <= t), f(same8 & (s <= t)), neg(same8 & (s <= t)), f(same8)], 1)
    b, col = np.arange(DEC_B)[None, :, None], np.arange(NS)[None, None, :]
    new = neg((col // DEC_T == b) & (col % DEC_T < s[:, :, None] % DEC_T)).reshape(P, -1)
    sb = np.concatenate([f(s >= t), neg(s < t), np.zeros((P, SEQ - P), np.float32), new], 1)
    return common, dn, sb


UNIT_PLAN = [("mem0", 4), ("mem1", 4), ("in_a", QKV + DN_H + MEMC), ("out_a", KD), ("up0", 2 * FF), ("down0", 2 * KD),
             ("kv", 2 * SBC), ("in_b", SBC + MEMC), ("out_b", KD), ("up1", 2 * FF), ("down1", 2 * KD)]
UNIT0 = {}
_u = 0
for _name, _n in UNIT_PLAN:
    UNIT0[_name] = _u
    _u += _n
UNITS = dict(UNIT_PLAN)
W8 = [n for n, _ in UNIT_PLAN if not n.startswith("down")]
W8_ROW = {}
_r = 0
for _name in W8:
    W8_ROW[_name] = _r
    _r += UNITS[_name]
W8_ROWS = _r
GAINS = ["mem0", "mem1", "mix_pre0", "mix_post0", "ffn_pre0", "ffn_post0", "kv", "mix_pre1", "mix_post1",
         "ffn_pre1", "ffn_post1"]


def build(nc, d):
    with ExitStack() as ctx:
        def sb(name, *shape, dt=F32):
            return ctx.enter_context(nc.sbuf_tensor(name, list(shape), dt))

        def sem(name):
            return ctx.enter_context(nc.semaphore(name))

        PB = ctx.enter_context(nc.psum_tensor("PB", [P, 8, 512], F32))
        hT = sb("hT", P, KD, NT)
        xnT = sb("xnT", P, KD, NT)
        mixT = sb("mixT", P, KD, NT)
        big = sb("big", P, (QKV + DN_H) * NT)
        ring = sb("ring", P, 2, SLOT)
        kvr = sb("kvr", P, SBC * NT + NCH * SBC * P + SBC * P)
        membuf = sb("membuf", P, 4096)
        mkv = sb("mkv", P, 2, 2, 2, N_MEM)
        mq = sb("mq", P, MEMC, NT)
        qmblk = sb("qmblk", P, MEMC, DEC_B, 4 * DEC_T)
        qblk = sb("qblk", P, SBC, DEC_B, QC)
        common = sb("common", P, 2 * P)
        pconst = sb("pconst", P, 12 * P)
        gains = sb("gains", P, len(GAINS), KD)
        dnw = sb("dnw", P, QKV, DN_TAPS)
        ffw = sb("ffw", P, 2, 2 * FF, FF_TAPS + 1)
        cstate = sb("cstate", P, 2 * FF * DEC_B * 2)
        cnew = sb("cnew", P, 2 * FF * (DEC_B + 1) * 2)
        rstd = sb("rstd", P, NT)
        wba = sb("wba", P, KD, 2 * DN_H)
        tok = sb("tok", P, 9, NCH + 1, DN_H)
        small = sb("small", P, 48)
        sbias = sb("sbias", P, 2)
        biash = sb("biash", P, SB_H)
        pages = sb("pages", 1, DEC_B * PAGES, dt=I32)

        ones, ident = common[:, 0:P], common[:, P:2 * P]
        levelm = [pconst[:, l * P:(l + 1) * P] for l in range(LEVELS)]
        cumT, maskT, cum8, mask8, same8 = (pconst[:, (LEVELS + i) * P:(LEVELS + i + 1) * P] for i in range(5))
        suffix = pconst[:, 0:P]
        strict = pconst[:, P:P + SEQ]
        strict8 = pconst[:, P + SEQ:P + SEQ + DEC_B * NS]
        sq = membuf[:, 0:2 * NT].rearrange("p (a n) -> p a n", a=2)
        epsc, alog, dtb, ogain = small[:, 0:1], small[:, 1:7], small[:, 7:13], small[:, 13:14]
        nalog, vmax, vsum, vrec = small[:, 14:20], small[:, 20:24], small[:, 24:28], small[:, 28:32]
        onec = small[:, 32:33]

        rawp = kvr[:, 0:2 * (SEQ + 3)].rearrange("p (a n) -> p a n", a=2)
        o = 2 * (SEQ + 3)
        raws = kvr[:, o:o + 2 * DEC_B * 11].rearrange("p (a b n) -> p a b n", a=2, b=DEC_B)
        o += 2 * DEC_B * 11
        acc = kvr[:, o:o + 2 * NT].rearrange("p (a n) -> p a n", a=2)
        o += 2 * NT
        gate = kvr[:, o:o + NT]
        kvT = kvr[:, 0:SBC * NT].rearrange("p (c n) -> p c n", c=SBC)
        o = SBC * NT
        vtok = kvr[:, o:o + NCH * SBC * P].rearrange("p (t n) -> p t n", t=NCH)
        o += NCH * SBC * P
        vnew64 = kvr[:, o:o + SBC * P]

        w_full = [sem("w_full0"), sem("w_full1")]
        unit_done, evacuated = sem("unit_done"), sem("evacuated")
        mem_loaded, loaded, consts_b = sem("mem_loaded"), sem("loaded"), sem("consts_b")
        sq_ready, sq_summed, rstd_ready, normed = sem("sq_ready"), sem("sq_summed"), sem("rstd_ready"), sem("normed")
        dve_own, act_own, pool_own = sem("dve_own"), sem("act_own"), sem("pool_own")
        conv_done, tail_kept, gated = sem("conv_done"), sem("tail_kept"), sem("gated")
        y_ready, pads_ready, pads_zeroed = sem("y_ready"), sem("pads_ready"), sem("pads_zeroed")
        stored = sem("stored")
        state_in = sem("state_in")
        zeroed = sem("zeroed")
        tk_pe, tk_act, tk_dve = sem("tk_pe"), sem("tk_act"), sem("tk_dve")
        kv_stored, mkv_stored, queries = sem("kv_stored"), sem("mkv_stored"), sem("queries")
        mem_in = sem("mem_in")
        hid = sem("hid")
        n_stored = [0]

        def store(eng, out, src):
            eng.dma_start(out, src).then_inc(stored, 16)
            n_stored[0] += 16

        class Own:

            def __init__(self, s):
                self.sem, self.value = s, 0

            def inc(self):
                self.value += 1
                return 1

        dv, ac, po = Own(dve_own), Own(act_own), Own(pool_own)
        norm_no = [0]
        NORMS = ["mem", "mix_pre0", "mix_post0", "ffn_pre0", "ffn_post0", "kv", "mix_post1", "ffn_pre1", "ffn_post1"]
        APPLIES = ["mem0", "mem1", "mix_pre0", "mix_post0", "ffn_pre0", "ffn_post0", "kv", "mix_pre1",
                   "mix_post1", "ffn_pre1", "ffn_post1"]
        applied = {n: i + 1 for i, n in enumerate(APPLIES)}
        stat = {n: i + 1 for i, n in enumerate(NORMS)}

        xflat = xnT[:, :, :].rearrange("p c n -> p (c n)")
        HW = DN_H * P

        def tile6(i):
            if i < 6:
                a = xflat[:, i * HW:(i + 1) * HW]
            else:
                a = kvr[:, (i - 6) * HW:(i - 5) * HW]
            return a.rearrange("p (h n) -> p h n", h=DN_H)

        (qn, kn, eg, ktk, vb, wk, gamT, LT, Tm, TT, M1, BT, WTn, qdec, Sst) = (tile6(i) for i in range(15))
        sqq, sqk, rq, rk = Tm, TT, M1, BT
        ug, ib = vb, wk
        vst = WTn
        vnew, osq, ro = BT, M1, Tm
        bigv = big[:, :].rearrange("p (c n) -> p c n", n=NT)
        S8 = [membuf[:, i * 1024:(i + 1) * 1024].rearrange("p (b n) -> p b n", b=DEC_B) for i in range(2)]
        WTm = membuf[:, 2048:2048 + DEC_B * NS].rearrange("p (b n) -> p b n", b=DEC_B)
        WTd = membuf[:, 2048:2048 + DEC_B * (NS + DEC_T)].rearrange("p (b n) -> p b n", b=DEC_B)[:, :, 0:DEC_T]
        vmask = membuf[0:NS, 2624:2624 + 1024].rearrange("p (b n) -> p b n", b=DEC_B)
        G = range(2)

        def heads(a, g, rows=P, T=P):
            return a[0:rows, 3 * g:3 * g + 3, 0:T]

        def bank(b, rows=P, T=P):
            return PB[0:rows, b, 0:3 * P].rearrange("p (h n) -> p h n", h=3)[:, :, 0:T]

        def steps(prefix, table):
            return {e: Steps(sem(f"{prefix}_{e}"), names.split()) for e, names in table.items()}

        def dn_table(n, sample):
            pe = "ss0 ss1 gb0 gb1 bb0 bb1 kk0 kk1 kq0 kq1 kt0 kt1 vt0 vt1 t00 t01 "
            for l in range(1, n):
                pe += f"m{l}_0 m{l}_1 "
                if l < n - 1:
                    pe += f"x{l}_0 "
                pe += f"xt{l}_0 "
                if l < n - 1:
                    pe += f"x{l}_1 "
                pe += f"xt{l}_1 "
            pe += "wt0 wt1 "
            if sample:
                pe += " ".join(f"vn{h} o{h} sa{h} sb{h}" for h in range(DN_H)) + " "
            else:
                pe += "vn0 vn1 o0 o1 s0 s1 "
            pe += "os0 os1"
            act = "sq0 sk0 sq1 sk1 lq0 lk0 lq1 lk1 rq0 rk0 rq1 rk1 eg0 eg1 ga0 ga1 t00 t01 "
            act += " ".join(f"m{l}_{g}" for l in range(1, n) for g in G) + " "
            if sample:
                act += " ".join(f"wt{h} vn{h}" for h in range(DN_H)) + " "
            else:
                act += "wt0 wt1 vn0 vn1 "
            act += "os0 os1 ol0 ol1 or0 or1"
            dve = "qn0 kn0 qn1 kn1 ga00 ga01 ga02 ga10 ga11 ga12 lt0 at0 lb0 lt1 at1 lb1 tt00 tt01 kd0 wk0 vb0 kd1 wk1 vb1 "
            for l in range(1, n):
                for g in G:
                    if l < n - 1:
                        dve += f"x{l}_{g} "
                    dve += f"xt{l}_{g} "
            if sample:
                dve += " ".join(f"vm{h} sd{h} sn{h}" for h in range(DN_H)) + " "
            else:
                dve += "s0 s1 s2 s3 s4 s5 "
            dve += "on0 on1 oz0 oz1"
            pool = "ug ib vst " + " ".join(f"bt{l}" for l in range(n)) + " qd"
            return dict(pe=pe, act=act, dve=dve, pool=pool)

        dn_p = steps("dn", dn_table(LEVELS, False))
        dn_s = steps("dns", dn_table(LEVELS_S, True))
        s8_in, s8_out = [sem("s8_in0"), sem("s8_in1")], sem("s8_out")
        dnconv_out, ffconv_out = sem("dnconv_out"), sem("ffconv_out")
        MEM_LOADS, LOADS = 16 * 6, 16 * 9

        tB, tG, tGc, tGl, tNg, tEd, tBg, tA, tX = (tok[:, i, :, :] for i in range(9))

        block = ctx.enter_context(nc.Block())

        def pe_stats(pe, name, n=NT):
            j = stat[name] - 1
            if j:
                pe.wait_ge(rstd_ready, j)
            for k in range(KD):
                pe.wait_ge(sq_ready, j * KD + k + 1)
                for b, lo in enumerate(range(0, n, HALF)):
                    last = nc.tensor.matmul(PB[:, 4 + b, 0:min(n, HALF)], ones, sq[:, k % 2, lo:lo + min(n, HALF)],
                                            start=k == 0, stop=k == KD - 1)
                last.then_inc(sq_summed, 1)

        def act_stats(act, name, src, n=NT):
            j = stat[name] - 1
            for k in range(KD):
                if j * KD + k >= 2:
                    act.wait_ge(sq_summed, j * KD + k - 1)
                nc.scalar.activation(sq[:, k % 2, 0:n], src[:, k, 0:n], ACT.Square).then_inc(sq_ready, 1)
            act.wait_ge(sq_summed, (j + 1) * KD)
            before = {"mem": 0, "mix_pre0": applied["mem1"], "mix_post1": applied["mix_pre1"]}
            if name != "mem":
                act.wait_ge(normed, before.get(name, applied[name] - 1))
            for b, lo in enumerate(range(0, n, HALF)):
                last = nc.scalar.activation(rstd[:, lo:lo + min(n, HALF)], PB[:, 4 + b, 0:min(n, HALF)], ACT.Ln, bias=epsc,
                                            scale=1.0 / D_MODEL)
            last.then_inc(ac.sem, ac.inc())
            act.wait_ge(ac.sem, ac.value)
            nc.scalar.activation(rstd[:, 0:n], rstd[:, 0:n], ACT.Exp, scale=-0.5).then_inc(rstd_ready, 1)

        def dve_apply(dve, stat_name, name, src, dst, n=NT):
            dve.wait_ge(rstd_ready, stat[stat_name])
            g = GAINS.index(name)
            for k in range(KD):
                last = nc.vector.scalar_tensor_tensor(out=dst[:, k, 0:n], in0=src[:, k, 0:n],
                                                      scalar=gains[:, g, k:k + 1], in1=rstd[:, 0:n],
                                                      op0=ALU.mult, op1=ALU.mult)
            last.then_inc(normed, 1)

        HID = {n: i + 1 for i, n in enumerate(["mix_post0", "ffn_post0", "mix_post1", "ffn_post1"])}

        def dve_residual(dve, name):
            dve_apply(dve, name, name, xnT, xnT)
            dve.wait_ge(normed, applied[name])
            for k in range(KD):
                last = nc.vector.tensor_tensor(hT[:, k, :], hT[:, k, :], xnT[:, k, :], ALU.add)
            last.then_inc(hid, 1)

        def pe_units(pe, name, x, n=NT, swap=False, count=None, first=0):
            u0 = UNIT0[name] + first

            def unit(i, k):
                u = 2 * i + (u0 + k)
                if not (isinstance(i, int) and u < 2):
                    pe.wait_ge(evacuated, u - 1)
                pe.wait_ge(w_full[k], i * 16 + (u0 // 2 + 1) * 16)
                if not swap:
                    for c in range(KD):
                        for b, lo in enumerate(range(0, n, HALF)):
                            last = nc.tensor.matmul(PB[:, 2 * b + k, 0:min(n, HALF)], ring[:, k, c * P:(c + 1) * P],
                                                    x[:, c, lo:lo + min(n, HALF)], start=c == 0, stop=c == KD - 1)
                else:
                    for t in range(-(-n // P)):
                        m = min(P, n - t * P)
                        dst = PB[0:m, k, t * P:(t + 1) * P] if t < 4 else PB[0:m, 2 + k, 0:P]
                        for c in range(KD):
                            last = nc.tensor.matmul(dst, x[:, c, t * P:t * P + m], ring[:, k, c * P:(c + 1) * P],
                                                    start=c == 0, stop=c == KD - 1)
                last.then_inc(unit_done, 1)

            if u0 == 0:
                for k in range(2):
                    unit(0, k)
                u0, count = 2, count - 2
            if count == 2:
                for k in range(2):
                    unit(0, k)
            elif count:
                with pe.Fori(0, count // 2) as i:
                    for k in range(2):
                        unit(i, k)

        def pe_down(pe, name, x):
            u0 = UNIT0[name]
            with pe.Fori(0, KD // 2) as i:
                for m in range(2):
                    for half in range(2):
                        if half == 0:
                            pe.wait_ge(evacuated, 4 * i + (u0 + 2 * m - 2))
                        pe.wait_ge(w_full[half], i * 32 + (u0 // 2 + m + 1) * 16)
                        for c in range(FF // 2):
                            w = ring[:, half, c * P:(c + 1) * P]
                            st, sp_ = half == 0 and c == 0, half == 1 and c == FF // 2 - 1
                            for b in range(2):
                                last = nc.tensor.matmul(PB[:, 2 * b + m, 0:HALF], w,
                                                        x[:, half * (FF // 2) + c, b * HALF:(b + 1) * HALF],
                                                        start=st, stop=sp_)
                        last.then_inc(unit_done, 1)

        def act_evac(act, name, place, count, first=0, scale=1.0, func=ACT.Copy):
            u0 = UNIT0[name] + first

            def unit(i, k):
                act.wait_ge(unit_done, 2 * i + (u0 + k + 1))
                for dst, src in place(i, k):
                    last = nc.scalar.activation(dst, src, func, scale=scale)
                last.then_inc(evacuated, 1)
            if count == 2:
                for k in range(2):
                    unit(0, k)
            else:
                with act.Fori(0, count // 2) as i:
                    for k in range(2):
                        unit(i, k)

        def row(a, c, lo=0, hi=NT):
            if isinstance(c, int):
                return a[:, c, lo:hi]
            return a[:, bass.ds(c, 1), lo:hi].rearrange("p a n -> p (a n)")

        def chunked(a, first=0):
            return lambda i, k: [(row(a, 2 * i + (first + k), b * HALF, (b + 1) * HALF), PB[:, 2 * b + k, 0:HALF])
                                 for b in range(2)]

        def act_down(act, name):
            u0 = UNIT0[name]
            with act.Fori(0, KD // 2) as i:
                for m in range(2):
                    act.wait_ge(unit_done, 4 * i + (u0 + 2 * m + 2))
                    for b in range(2):
                        last = nc.scalar.activation(row(xnT, 2 * i + m, b * HALF, (b + 1) * HALF),
                                                    PB[:, 2 * b + m, 0:HALF], ACT.Copy)
                    last.then_inc(evacuated, 2)

        conv_base = {"in_a": 0, "up0": QKV, "up1": QKV + 2 * FF}

        def scalar_of(a, c, j):
            return a[:, bass.ds(c, 1), j:j + 1].rearrange("p a b -> p (a b)")

        def act_conv(act, name, taps, units):
            pad, u0, cb = taps - 1, UNIT0[name], conv_base[name]
            with act.Fori(0, units // 2) as i:
                for k in range(2):
                    act.wait_ge(unit_done, 2 * i + (u0 + k + 1))
                    act.wait_ge(conv_done, 2 * i + (cb + k + 1))
                    act.wait_ge(tail_kept, 2 * i + (cb + k + 1))
                    nc.scalar.activation(rawp[:, k, pad:pad + HALF], PB[:, k, 0:HALF], ACT.Copy)
                    nc.scalar.activation(rawp[:, k, pad + HALF:pad + SEQ], PB[:, 2 + k, 0:SEQ - HALF], ACT.Copy)
                    nc.scalar.activation(raws[:, k, :, pad:pad + DEC_T],
                                         PB[:, 2 + k, SEQ - HALF:HALF].rearrange("p (b t) -> p b t", b=DEC_B),
                                         ACT.Copy).then_inc(evacuated, 1)
                    if name == "in_a":
                        act.wait_ge(conv_done, 2 * i + (cb + k + 3))
                        nc.scalar.activation(row(bigv, 2 * i + k), acc[:, k, :], ACT.Silu).then_inc(gated, 1)
                    elif k == 0:
                        act.wait_ge(conv_done, 2 * i + (cb + k + 3))
                        act.wait_ge(y_ready, i + (cb // 2 + 1))
                        nc.scalar.activation(gate, acc[:, k, :], ACT.Gelu_apprx_tanh,
                                             bias=scalar_of(ffw[:, int(name[-1]), :, :], 2 * i, FF_TAPS)).then_inc(gated, 1)
                    else:
                        act.sem_inc(gated, 1)

        def dve_conv(dve, name, taps, units):
            cb, u0 = conv_base[name], UNIT0[name]
            wts = dnw if name == "in_a" else ffw[:, int(name[-1]), :, :]
            base = dv.value
            with dve.Fori(0, units // 2) as i:
                own = 0
                for k in range(2):
                    dve.wait_ge(evacuated, 2 * i + (u0 + k + 1))
                    dve.wait_ge(pads_ready, 2 * i + (cb + k + 1))
                    dve.wait_ge(gated, 2 * i + (cb + k + 1))
                    dve.wait_ge(y_ready, i + (cb // 2 + 1))
                    for tap in range(taps):
                        w = scalar_of(wts, 2 * i + k, tap)
                        xp, xs = rawp[:, k, tap:tap + SEQ], raws[:, k, :, tap:tap + DEC_T]
                        ap_, as_ = acc[:, k, 0:SEQ], acc[:, k, SEQ:NT].rearrange("p (b t) -> p b t", b=DEC_B)
                        if tap == 0:
                            nc.vector.tensor_scalar(ap_, xp, w, None, ALU.mult)
                            last = nc.vector.tensor_scalar(as_, xs, w, None, ALU.mult)
                        else:
                            dve.wait_ge(dv.sem, i * (2 * (taps - 1)) + (base + own))
                            nc.vector.scalar_tensor_tensor(out=ap_, in0=xp, scalar=w, in1=ap_, op0=ALU.mult, op1=ALU.add)
                            last = nc.vector.scalar_tensor_tensor(out=as_, in0=xs, scalar=w, in1=as_, op0=ALU.mult,
                                                                  op1=ALU.add)
                        if tap < taps - 1:
                            last.then_inc(dv.sem, 1)
                            own += 1
                    last.then_inc(conv_done, 1)
                if name != "in_a":
                    dve.wait_ge(gated, 2 * i + (cb + 3))
                    dve.wait_ge(conv_done, 2 * i + (cb + 4))
                    nc.vector.scalar_tensor_tensor(out=row(bigv, i), in0=acc[:, 1, :],
                                                   scalar=scalar_of(ffw[:, int(name[-1]), :, :], 2 * i + 1, FF_TAPS),
                                                   in1=gate, op0=ALU.add, op1=ALU.mult).then_inc(y_ready, 1)
                else:
                    dve.sem_inc(y_ready, 1)
            dv.value = base + (units // 2) * (2 * (taps - 1))

        def pool_conv(pool, name, taps, units):
            pad, cb, u0 = taps - 1, conv_base[name], UNIT0[name]
            st = cstate[:, 0:units * DEC_B * pad].rearrange("p (c b n) -> p c b n", c=units, b=DEC_B)
            ne = cnew[:, 0:units * (DEC_B + 1) * pad].rearrange("p (c b n) -> p c b n", c=units, b=DEC_B + 1)
            with pool.Fori(0, units // 2) as i:
                for k in range(2):
                    pool.wait_ge(conv_done, 2 * i + (cb + k + 1))
                    pool.wait_ge(tail_kept, 2 * i + (cb + k + 1))
                    nc.gpsimd.tensor_copy(raws[:, k, :, 0:pad],
                                          st[:, bass.ds(2 * i + k, 1), :, :].rearrange("p a b n -> p (a b) n")).then_inc(pads_ready, 1)
                for k in range(2):
                    pool.wait_ge(evacuated, 2 * i + (u0 + k + 1))
                    nc.gpsimd.tensor_copy(ne[:, bass.ds(2 * i + k, 1), 0:1, :].rearrange("p a b n -> p (a b n)"),
                                          rawp[:, k, SEQ:SEQ + pad])
                    nc.gpsimd.tensor_copy(ne[:, bass.ds(2 * i + k, 1), 1:, :].rearrange("p a b n -> p (a b) n"),
                                          raws[:, k, :, DEC_T:DEC_T + pad]).then_inc(tail_kept, 1)

        TILES = [(P, 0, NCH), (NS, NCH, NCH + 1)]
        baP = PB[:, 6, 0:(NCH + 1) * 2 * DN_H].rearrange("p (t x) -> p t x", x=2 * DN_H)

        def pe_tokens(pe):
            pe.wait_ge(normed, applied["mix_pre0"])
            for t in range(NCH + 1):
                m = min(P, NT - t * P)
                for c in range(KD):
                    last = nc.tensor.matmul(baP[0:m, t, :], xnT[:, c, t * P:t * P + m], wba[:, c, :],
                                            start=c == 0, stop=c == KD - 1)
            last.then_inc(tk_pe, 1)
            pe.wait_ge(tk_dve, 3)
            for i, (m, a, b) in enumerate(TILES):
                w = (b - a) * DN_H
                rhs = tG[0:m, a:b, :].rearrange("p t h -> p (t h)")
                nc.tensor.matmul(PB[0:m, 7, 32 * i:32 * i + w], (cumT, cum8)[i][0:m, 0:m], rhs, start=True, stop=True)
                last = nc.tensor.matmul(PB[0:m, 7, 64 + 32 * i:64 + 32 * i + w], (ones, same8)[i][0:m, 0:m], rhs,
                                        start=True, stop=True)
            last.then_inc(tk_pe, 1)

        def act_tokens(act):
            act.wait_ge(tk_pe, 1)
            for m, a, b in TILES:
                nc.scalar.activation(tB[0:m, a:b, :], baP[0:m, a:b, 0:DN_H], ACT.Exp, scale=-1.0)
            nc.scalar.activation(nalog, alog, ACT.Exp).then_inc(tk_act, 1)
            act.wait_ge(tk_dve, 2)
            for m, a, b in TILES:
                last = nc.scalar.activation(tX[0:m, a:b, :], tX[0:m, a:b, :], ACT.Exp)
            last.then_inc(tk_act, 1)
            act.wait_ge(tk_act, 2)
            for m, a, b in TILES:
                last = nc.scalar.activation(tX[0:m, a:b, :], tX[0:m, a:b, :], ACT.Ln, bias=onec[0:m, :])
            last.then_inc(tk_act, 1)
            act.wait_ge(tk_dve, 4)
            for m, a, b in TILES:
                nc.scalar.activation(tEd[0:m, a:b, :], tEd[0:m, a:b, :], ACT.Exp)
                last = nc.scalar.activation(tBg[0:m, a:b, :], tGc[0:m, a:b, :], ACT.Exp)
            last.then_inc(tk_act, 1)

        def dve_tokens(dve):
            def heads_of(x, m, n):
                return x[0:m, :].unsqueeze(1).to_broadcast([m, n, DN_H])
            dve.wait_ge(tk_act, 1)
            for m, a, b in TILES:
                nc.vector.tensor_scalar(tB[0:m, a:b, :], tB[0:m, a:b, :], 1.0, None, ALU.add)
                last = nc.vector.tensor_tensor(tA[0:m, a:b, :], baP[0:m, a:b, DN_H:], heads_of(dtb, m, b - a), ALU.add)
            last.then_inc(tk_dve, 1)
            dve.wait_ge(tk_dve, 1)
            for m, a, b in TILES:
                nc.vector.reciprocal(tB[0:m, a:b, :], tB[0:m, a:b, :])
                fl = lambda x: x[0:m, a:b, :].rearrange("p t h -> p (t h)")
                last = nc.vector.scalar_tensor_tensor(out=fl(tX), in0=fl(tA), scalar=-1.0, in1=fl(tA), op0=ALU.mult,
                                                      op1=ALU.min)
            last.then_inc(tk_dve, 1)
            dve.wait_ge(tk_act, 3)
            for m, a, b in TILES:
                fl = lambda x: x[0:m, a:b, :].rearrange("p t h -> p (t h)")
                last = nc.vector.scalar_tensor_tensor(out=fl(tX), in0=fl(tA), scalar=0.0, in1=fl(tX), op0=ALU.max,
                                                      op1=ALU.add)
            last.then_inc(dv.sem, dv.inc())
            dve.wait_ge(dv.sem, dv.value)
            for m, a, b in TILES:
                nc.vector.tensor_tensor(tG[0:m, a:b, :], tX[0:m, a:b, :], heads_of(nalog, m, b - a), ALU.mult)
                last = nc.vector.tensor_scalar(tX[0:m, a:b, :], tX[0:m, a:b, :], -1.0, None, ALU.mult)
            last.then_inc(dv.sem, dv.inc())
            dve.wait_ge(dv.sem, dv.value)
            for m, a, b in TILES:
                last = nc.vector.tensor_tensor(tG[0:m, a:b, :], tX[0:m, a:b, :], heads_of(nalog, m, b - a), ALU.mult)
            last.then_inc(tk_dve, 1)
            dve.wait_ge(tk_pe, 2)
            for i, (m, a, b) in enumerate(TILES):
                w = (b - a) * DN_H
                fl = lambda x: x[0:m, a:b, :].rearrange("p t h -> p (t h)")
                nc.vector.tensor_copy(fl(tGc), PB[0:m, 7, 32 * i:32 * i + w])
                last = nc.vector.tensor_scalar(fl(tNg), PB[0:m, 7, 32 * i:32 * i + w], -1.0, None, ALU.mult)
            last.then_inc(dv.sem, dv.inc())
            dve.wait_ge(dv.sem, dv.value)
            for i, (m, a, b) in enumerate(TILES):
                w = (b - a) * DN_H
                fl = lambda x: x[0:m, a:b, :].rearrange("p t h -> p (t h)")
                last = nc.vector.tensor_tensor(fl(tEd), PB[0:m, 7, 64 + 32 * i:64 + 32 * i + w], fl(tGc), ALU.subtract)
            last.then_inc(tk_dve, 1)
            dve.wait_ge(tk_act, 4)
            for m, a, b in TILES:
                last = nc.vector.tensor_tensor(tBg[0:m, a:b, :], tBg[0:m, a:b, :], tB[0:m, a:b, :], ALU.mult)
            last.then_inc(tk_dve, 1)

        def tile_of(i, rows_, c, h0, h1):
            if isinstance(c, int):
                return tok[0:rows_, i, c, h0:h1]
            return tok[0:rows_, i, bass.ds(c, 1), h0:h1].rearrange("p a h -> p (a h)")

        def dn_pe(pe, s, c, before, levels, T, sample):
            c = 0 if sample else c
            wait = lambda e, name: pe.wait_ge(s[e].sem, s[e].at(name, c))
            mark = s["pe"].mark
            S_ = s["pe"].sem
            bs, bt = before
            pe.wait_ge(bs["dve"].sem, bs["dve"].at("oz1", bt))
            pe.wait_ge(bs["act"].sem, bs["act"].at("or1", bt))
            for g in G:
                wait("act", f"sk{g}")
                nc.tensor.matmul(bank(g, P, T), ones, heads(sqq, g, P, T), start=True, stop=True)
                nc.tensor.matmul(bank(2 + g, P, T), ones, heads(sqk, g, P, T), start=True,
                                 stop=True).then_inc(S_, mark(f"ss{g}"))
            wait("pool", "ug")
            for g in G:
                nc.tensor.matmul(bank(4 + g, P, T), ones[0:T, :], heads(ug, g, T, T), start=True,
                                 stop=True).then_inc(S_, mark(f"gb{g}"))
            wait("pool", "ib")
            for g in G:
                nc.tensor.matmul(bank(6 + g, T, T), ones[0:T, 0:T], heads(ib, g, T, T), start=True,
                                 stop=True).then_inc(S_, mark(f"bb{g}"))
            for g in G:
                wait("dve", f"kn{g}")
                for h in range(3):
                    kh = kn[:, 3 * g + h, 0:T]
                    last = nc.tensor.matmul(bank(g, T, T)[:, h, :], kh, kh, start=True, stop=True)
                last.then_inc(S_, mark(f"kk{g}"))
            for g in G:
                for h in range(3):
                    last = nc.tensor.matmul(bank(2 + g, T, T)[:, h, :], kn[:, 3 * g + h, 0:T], qn[:, 3 * g + h, 0:T],
                                            start=True, stop=True)
                last.then_inc(S_, mark(f"kq{g}"))
            for g in G:
                wait("act", f"eg{g}")
                wait("dve", f"ga{g}2")
                for h in range(3):
                    last = nc.tensor.transpose(bank(4 + g, T, P)[:, h, :], kn[:, 3 * g + h, 0:T], ident)
                last.then_inc(S_, mark(f"kt{g}"))
            wait("pool", "vst")
            for g in G:
                wait("dve", f"lb{g}")
                for h in range(3):
                    last = nc.tensor.transpose(bank(6 + g, T, P)[:, h, :], vst[:, 3 * g + h, 0:T], ident)
                last.then_inc(S_, mark(f"vt{g}"))
            for g in G:
                wait("dve", f"tt0{g}")
                for h in range(3):
                    last = nc.tensor.transpose(bank(g, T, T)[:, h, :], TT[0:T, 3 * g + h, 0:T], ident[0:T, 0:T])
                last.then_inc(S_, mark(f"t0{g}"))
            for l in range(1, levels):
                wait("pool", f"bt{l}")
                for g in G:
                    if l == 1:
                        wait("act", f"t0{g}")
                    else:
                        wait("dve", f"x{l - 1}_{g}")
                    for h in range(3 * g, 3 * g + 3):
                        last = nc.tensor.matmul(bank(g, T, T)[:, h - 3 * g, :], BT[0:T, h, 0:T], Tm[0:T, h, 0:T],
                                                start=True, stop=True)
                    last.then_inc(S_, mark(f"m{l}_{g}"))
                for g in G:
                    wait("act", f"m{l}_{g}")
                    wait("dve", f"wk{g}" if l == 1 else f"xt{l - 1}_{g}")
                    if l < levels - 1:
                        for h in range(3 * g, 3 * g + 3):
                            last = nc.tensor.matmul(bank(2 + g, T, T)[:, h - 3 * g, :], TT[0:T, h, 0:T], M1[0:T, h, 0:T],
                                                    start=True, stop=True)
                        last.then_inc(S_, mark(f"x{l}_{g}"))
                    for h in range(3 * g, 3 * g + 3):
                        last = nc.tensor.matmul(bank(4 + g, T, T)[:, h - 3 * g, :], M1[0:T, h, 0:T], TT[0:T, h, 0:T],
                                                start=True, stop=True)
                    last.then_inc(S_, mark(f"xt{l}_{g}"))
            for g in G:
                wait("dve", f"xt{levels - 1}_{g}")
                for h in range(3):
                    last = nc.tensor.matmul(bank(g, P, T)[:, h, :], wk[0:T, 3 * g + h, :], TT[0:T, 3 * g + h, 0:T],
                                            start=True, stop=True)
                last.then_inc(S_, mark(f"wt{g}"))
            if not sample:
                for g in G:
                    wait("act", f"wt{g}")
                    for h in range(3 * g, 3 * g + 3):
                        dst = bank(2 + g)[:, h - 3 * g, :]
                        nc.tensor.matmul(dst, TT[:, h, :], vb[:, h, :], start=True, stop=False)
                        last = nc.tensor.matmul(dst, WTn[:, h, :], Sst[:, h, :], start=False, stop=True)
                    last.then_inc(S_, mark(f"vn{g}"))
                wait("pool", "qd")
                for g in G:
                    wait("act", f"vn{g}")
                    for h in range(3 * g, 3 * g + 3):
                        dst = bank(4 + g)[:, h - 3 * g, :]
                        nc.tensor.matmul(dst, Sst[:, h, :], qdec[:, h, :], start=True, stop=False)
                        last = nc.tensor.matmul(dst, vnew[:, h, :], gamT[:, h, :], start=False, stop=True)
                    last.then_inc(S_, mark(f"o{g}"))
                for g in G:
                    wait("dve", f"vb{g}")
                    for h in range(3 * g, 3 * g + 3):
                        last = nc.tensor.matmul(bank(6 + g)[:, h - 3 * g, :], ktk[:, h, :], vnew[:, h, :],
                                                start=True, stop=True)
                    last.then_inc(S_, mark(f"s{g}"))
            else:
                wait("pool", "qd")
                wait("dve", "vb1")
                for h in range(DN_H):
                    S8h = S8[h % 2]
                    wait("act", f"wt{h}")
                    pe.wait_ge(s8_in[h % 2], 16 * (h // 2 + 1))
                    if h >= 2:
                        wait("act", f"vn{h - 2}")
                    dst = PB[0:T, 2 + h % 2, 0:P]
                    nc.tensor.matmul(dst, TT[0:T, h, 0:T], vb[0:T, h, :], start=True, stop=False)
                    for b in range(DEC_B):
                        last = nc.tensor.matmul(dst, WTm[:, b, :], S8h[:, b, :], start=False, stop=b == DEC_B - 1)
                    last.then_inc(S_, mark(f"vn{h}"))
                    wait("act", f"vn{h}")
                    dst = bank(4 + h // 3, P, T)[:, h % 3, :]
                    nc.tensor.matmul(dst, vnew[0:T, h, :], gamT[0:T, h, 0:T], start=True, stop=False)
                    for b in range(DEC_B):
                        last = nc.tensor.matmul(dst[:, 8 * b:8 * b + 8], S8h[:, b, :], qdec[:, h, 8 * b:8 * b + 8],
                                                start=False, stop=b == DEC_B - 1)
                    last.then_inc(S_, mark(f"o{h}"))
                    wait("dve", f"vm{h}")
                    if h:
                        wait("dve", f"sn{h - 1}")
                    for half in range(2):
                        nc.tensor.matmul(PB[:, 6 + half, :], ktk[0:T, h, :],
                                         vmask[:, 4 * half:4 * half + 4, :].rearrange("p b n -> p (b n)"),
                                         start=True, stop=True).then_inc(S_, mark(f"s{'ab'[half]}{h}"))
            for g in G:
                wait("act", f"os{g}")
                nc.tensor.matmul(bank(g, P, T), ones, heads(osq, g, P, T), start=True, stop=True).then_inc(S_, mark(f"os{g}"))

        def dn_act(act, s, c, before, levels, T, sample, cols):
            c = 0 if sample else c
            wait = lambda e, name: act.wait_ge(s[e].sem, s[e].at(name, c))
            mark, S_ = s["act"].mark, s["act"].sem
            bs, bt = before
            act.wait_ge(bs["pe"].sem, bs["pe"].at("os1", bt))
            act.wait_ge(bs["dve"].sem, bs["dve"].at("on1", bt))
            for g in G:
                nc.scalar.activation(heads(sqq, g, P, T), cols(0, g), ACT.Square).then_inc(S_, mark(f"sq{g}"))
                nc.scalar.activation(heads(sqk, g, P, T), cols(1, g), ACT.Square).then_inc(S_, mark(f"sk{g}"))
            for g in G:
                wait("pe", f"ss{g}")
                nc.scalar.activation(heads(rq, g, P, T), bank(g, P, T), ACT.Ln, bias=epsc).then_inc(S_, mark(f"lq{g}"))
                nc.scalar.activation(heads(rk, g, P, T), bank(2 + g, P, T), ACT.Ln, bias=epsc).then_inc(S_, mark(f"lk{g}"))
            for g in G:
                wait("act", f"lk{g}")
                nc.scalar.activation(heads(rq, g, P, T), heads(rq, g, P, T), ACT.Exp, scale=-0.5).then_inc(S_, mark(f"rq{g}"))
                nc.scalar.activation(heads(rk, g, P, T), heads(rk, g, P, T), ACT.Exp, scale=-0.5).then_inc(S_, mark(f"rk{g}"))
            for g in G:
                wait("pe", f"gb{g}")
                nc.scalar.activation(heads(eg, g, P, T), bank(4 + g, P, T), ACT.Exp).then_inc(S_, mark(f"eg{g}"))
            for g in G:
                wait("dve", f"ga{g}2")
                nc.scalar.activation(heads(gamT, g, T, T), heads(gamT, g, T, T), ACT.Exp).then_inc(S_, mark(f"ga{g}"))
            for g in G:
                wait("pe", f"t0{g}")
                nc.scalar.activation(heads(Tm, g, T, T), bank(g, T, T), ACT.Copy).then_inc(S_, mark(f"t0{g}"))
            for l in range(1, levels):
                for g in G:
                    wait("pe", f"m{l}_{g}")
                    nc.scalar.activation(heads(M1, g, T, T), bank(g, T, T), ACT.Copy).then_inc(S_, mark(f"m{l}_{g}"))
            if not sample:
                for g in G:
                    wait("pe", f"wt{g}")
                    nc.scalar.activation(heads(WTn, g, P, T), bank(g, P, T), ACT.Copy, scale=-1.0).then_inc(S_, mark(f"wt{g}"))
                for g in G:
                    wait("pe", f"vn{g}")
                    nc.scalar.activation(heads(vnew, g, T, P), bank(2 + g, T, P), ACT.Copy).then_inc(S_, mark(f"vn{g}"))
            else:
                for h in range(DN_H):
                    wait("pe", "wt1" if h == 0 else f"vn{h - 1}")
                    nc.scalar.activation(WTd, bank(h // 3, P, T)[:, h % 3, :].rearrange("p (b t) -> p b t", b=DEC_B),
                                         ACT.Copy, scale=-1.0).then_inc(S_, mark(f"wt{h}"))
                    wait("pe", f"vn{h}")
                    nc.scalar.activation(vnew[0:T, h, :], PB[0:T, 2 + h % 2, 0:P], ACT.Copy).then_inc(S_, mark(f"vn{h}"))
            for g in G:
                wait("pe", f"o{3 * g + 2}" if sample else f"o{g}")
                nc.scalar.activation(heads(osq, g, P, T), bank(4 + g, P, T), ACT.Square).then_inc(S_, mark(f"os{g}"))
            for g in G:
                wait("pe", f"os{g}")
                nc.scalar.activation(heads(ro, g, P, T), bank(g, P, T), ACT.Ln, bias=epsc, scale=1.0 / P).then_inc(S_, mark(f"ol{g}"))
            for g in G:
                wait("act", f"ol{g}")
                nc.scalar.activation(heads(ro, g, P, T), heads(ro, g, P, T), ACT.Exp, scale=-0.5).then_inc(S_, mark(f"or{g}"))

        def dn_dve(dve, s, c, before, levels, T, sample, cols, out):
            ct, c = c, 0 if sample else c
            wait = lambda e, name: dve.wait_ge(s[e].sem, s[e].at(name, c))
            mark, S_ = s["dve"].mark, s["dve"].sem
            bs, bt = before
            dve.wait_ge(bs["pe"].sem, bs["pe"].at("os1", bt))
            mask = (mask8 if sample else maskT)[0:T, 0:T]
            for g in G:
                wait("act", f"rk{g}")
                nc.vector.scalar_tensor_tensor(out=heads(qn, g, P, T), in0=cols(0, g), scalar=float(P) ** -0.5,
                                               in1=heads(rq, g, P, T), op0=ALU.mult, op1=ALU.mult).then_inc(S_, mark(f"qn{g}"))
                nc.vector.tensor_tensor(heads(kn, g, P, T), cols(1, g), heads(rk, g, P, T), ALU.mult).then_inc(S_, mark(f"kn{g}"))
            for g in G:
                wait("act", f"eg{g}")
                for h in range(3):
                    nc.vector.scalar_tensor_tensor(out=gamT[0:T, 3 * g + h, 0:T], in0=bank(4 + g, T, T)[:, h, :],
                                                   scalar=tile_of(4, T, ct, 3 * g + h, 3 * g + h + 1),
                                                   in1=mask, op0=ALU.add, op1=ALU.add).then_inc(S_, mark(f"ga{g}{h}"))
            for g in G:
                wait("pe", f"kk{g}")
                wait("act", f"ga{g}")
                nc.vector.tensor_tensor(heads(LT, g, T, T), bank(g, T, T), heads(gamT, g, T, T), ALU.mult).then_inc(S_, mark(f"lt{g}"))
                wait("pe", f"kq{g}")
                wait("dve", f"lt{g}")
                nc.vector.tensor_tensor(heads(gamT, g, T, T), bank(2 + g, T, T), heads(gamT, g, T, T), ALU.mult).then_inc(S_, mark(f"at{g}"))
                wait("pe", f"bb{g}")
                nc.vector.tensor_tensor(heads(LT, g, T, T), heads(LT, g, T, T), bank(6 + g, T, T), ALU.mult).then_inc(S_, mark(f"lb{g}"))
            wait("pool", "bt0")
            for g in G:
                nc.vector.tensor_tensor(heads(TT, g, T, T), ident[0:T, 0:T].unsqueeze(1).to_broadcast([T, 3, T]),
                                        heads(BT, g, T, T), ALU.subtract).then_inc(S_, mark(f"tt0{g}"))

            def bc(i, g):
                return tile_of(i, T, ct, 3 * g, 3 * g + 3).unsqueeze(2).to_broadcast([T, 3, P])
            for g in G:
                wait("pe", f"kt{g}")
                nc.vector.tensor_tensor(heads(ktk, g, T, P), bank(4 + g, T, P), bc(5, g), ALU.mult).then_inc(S_, mark(f"kd{g}"))
                nc.vector.tensor_tensor(heads(wk, g, T, P), bank(4 + g, T, P), bc(6, g), ALU.mult).then_inc(S_, mark(f"wk{g}"))
                wait("pe", f"vt{g}")
                nc.vector.tensor_tensor(heads(vb, g, T, P), bank(6 + g, T, P), bc(0, g), ALU.mult).then_inc(S_, mark(f"vb{g}"))
            for l in range(1, levels):
                for g in G:
                    if l < levels - 1:
                        wait("pe", f"x{l}_{g}")
                        if l > 1:
                            wait("dve", f"x{l - 1}_{g}")
                        nc.vector.tensor_tensor(heads(Tm, g, T, T), heads(Tm, g, T, T), bank(2 + g, T, T),
                                                ALU.subtract).then_inc(S_, mark(f"x{l}_{g}"))
                    wait("pe", f"xt{l}_{g}")
                    wait("dve", f"tt0{g}" if l == 1 else f"xt{l - 1}_{g}")
                    nc.vector.tensor_tensor(heads(TT, g, T, T), heads(TT, g, T, T), bank(4 + g, T, T),
                                            ALU.subtract).then_inc(S_, mark(f"xt{l}_{g}"))
            if not sample:
                for h in range(DN_H):
                    g = h // 3
                    wait("pe", f"s{g}")
                    nc.vector.scalar_tensor_tensor(out=Sst[:, h, :], in0=Sst[:, h, :], scalar=eg[:, h, T - 1:T],
                                                   in1=bank(6 + g)[:, h % 3, :], op0=ALU.mult, op1=ALU.add).then_inc(S_, mark(f"s{h}"))
            else:
                for h in range(DN_H):
                    wait("act", f"vn{h}")
                    if h:
                        wait("pe", f"sb{h - 1}")
                    nc.vector.tensor_tensor(vmask, vnew[0:T, h, :].unsqueeze(1).to_broadcast([T, DEC_B, P]),
                                            same8[0:T, 0:T:DEC_T].unsqueeze(2).to_broadcast([T, DEC_B, P]),
                                            ALU.mult).then_inc(S_, mark(f"vm{h}"))
                    wait("pe", f"o{h}")
                    nc.vector.tensor_tensor(S8[h % 2], S8[h % 2],
                                            eg[:, h, DEC_T - 1:T:DEC_T].unsqueeze(2).to_broadcast([P, DEC_B, P]),
                                            ALU.mult).then_inc(S_, mark(f"sd{h}"))
                    wait("pe", f"sb{h}")
                    wait("dve", f"sd{h}")
                    nc.vector.tensor_tensor(S8[h % 2].rearrange("p b n -> p (b n)"), S8[h % 2].rearrange("p b n -> p (b n)"),
                                            PB[:, 6:8, :].rearrange("p a n -> p (a n)"), ALU.add).then_inc(S_, mark(f"sn{h}"))
            for g in G:
                wait("act", f"or{g}")
                nc.vector.scalar_tensor_tensor(out=heads(qn, g, P, T), in0=bank(4 + g, P, T), scalar=ogain,
                                               in1=heads(ro, g, P, T), op0=ALU.mult, op1=ALU.mult).then_inc(S_, mark(f"on{g}"))
            for g in G:
                wait("dve", f"on{g}")
                nc.vector.tensor_tensor(out(g), heads(qn, g, P, T), cols(3, g), ALU.mult).then_inc(S_, mark(f"oz{g}"))

        def dn_pool(pool, s, c, before, levels, T, sample, vcols):
            ct, c = c, 0 if sample else c
            wait = lambda e, name: pool.wait_ge(s[e].sem, s[e].at(name, c))
            mark, S_ = s["pool"].mark, s["pool"].sem
            bs, bt = before
            pool.wait_ge(bs["pe"].sem, bs["pe"].at("os1", bt))
            cum = (cum8 if sample else cumT)[0:T, 0:T]

            def six(m, i):
                return (m.unsqueeze(1).to_broadcast([T, DN_H, T]), tile_of(i, T, ct, 0, DN_H).unsqueeze(2).to_broadcast([T, DN_H, T]))
            a, b = six(cum, 1)
            nc.gpsimd.tensor_tensor(ug[0:T, :, 0:T], a, b, ALU.mult).then_inc(S_, mark("ug"))
            a, b = six(ident[0:T, 0:T], 0)
            nc.gpsimd.tensor_tensor(ib[0:T, :, 0:T], a, b, ALU.mult).then_inc(S_, mark("ib"))
            nc.gpsimd.tensor_copy(vst[:, :, 0:T], vcols).then_inc(S_, mark("vst"))
            for l in range(levels):
                if l == 0:
                    wait("dve", "lb1")
                elif l == 1:
                    wait("dve", "tt01")
                else:
                    wait("pe", f"m{l - 1}_1")
                nc.gpsimd.tensor_tensor(BT[0:T, :, 0:T], LT[0:T, :, 0:T],
                                        levelm[l][0:T, 0:T].unsqueeze(1).to_broadcast([T, DN_H, T]),
                                        ALU.mult).then_inc(S_, mark(f"bt{l}"))
            wait("act", "eg1")
            wait("dve", "qn1")
            nc.gpsimd.tensor_tensor(qdec[:, :, 0:T], qn[:, :, 0:T], eg[:, :, 0:T], ALU.mult).then_inc(S_, mark("qd"))

        def dn_cols(c):
            def f(part, g):
                r = bigv[:, DN_H * part + 3 * g:DN_H * part + 3 * g + 3, :]
                return r[:, :, SEQ:NT] if isinstance(c, int) else r[:, :, bass.ds(c * P, P)]
            return f

        def dn_run(eng, e, fn, extra):
            eng.sem_inc(dn_p[e].sem, dn_p[e].n)
            eng.sem_inc(dn_s[e].sem, dn_s[e].n)
            with eng.Fori(0, NCH) as c:
                fn(eng, dn_p, c, (dn_p, c - 1), LEVELS, P, False, *extra(c))
            fn(eng, dn_s, NCH, (dn_p, NCH - 1), LEVELS_S, NS, True, *extra(NCH))

        ma = {}
        for layer in range(2):
            ma[layer] = (steps(f"map{layer}", dict(
                pe="sc tr av", act="e0 e1 e2 e3 tc o", dve="mx rc pn", pool="st")),
                steps(f"mas{layer}", dict(pe="sc tr av", act="e0 tc o0 o1", dve="mx rc pn", pool="qz")))
        xs_ = xflat
        prob = xs_[:, 0:1024].rearrange("p (h m) -> p h m", h=4)
        probT = xs_[:, 1024:2048].rearrange("p (x t) -> p x t", x=8)
        mqst = xs_[:, 2048:2048 + MEMC * P].rearrange("p (c t) -> p c t", c=MEMC)
        km = membuf[:, 0:2048].rearrange("p (b c m) -> p b c m", b=4, c=MEMC)
        vm = membuf[:, 2048:4096].rearrange("p (b c f) -> p b c f", b=4, c=2)

        def pe_mem(pe, layer):
            sp_, ss_ = ma[layer]
            mk, mv = mkv[:, layer, 0, :, :], mkv[:, layer, 1, :, :]
            s = sp_
            pe.sem_inc(s["pe"].sem, s["pe"].n)
            with pe.Fori(0, NCH) as t:
                pe.wait_ge(s["pool"].sem, s["pool"].at("st", t))
                pe.wait_ge(s["act"].sem, s["act"].at("e3", t - 1))
                pe.wait_ge(s["dve"].sem, s["dve"].at("mx", t - 1))
                for x in range(4):
                    e, f = x // 2, x % 2
                    last = nc.tensor.matmul(PB[:, e, f * N_MEM:(f + 1) * N_MEM], mqst[64 * e:64 * e + 64, f, :],
                                            mk[64 * e:64 * e + 64, f, :], start=True, stop=True)
                last.then_inc(s["pe"].sem, s["pe"].mark("sc"))
                pe.wait_ge(s["dve"].sem, s["dve"].at("pn", t))
                pe.wait_ge(s["act"].sem, s["act"].at("tc", t - 1))
                for x in range(8):
                    last = nc.tensor.transpose(PB[:, 2 + x // 4, (x % 4) * P:(x % 4 + 1) * P],
                                               prob[:, x // 2, (x % 2) * P:(x % 2 + 1) * P], ident)
                last.then_inc(s["pe"].sem, s["pe"].mark("tr"))
                pe.wait_ge(s["act"].sem, s["act"].at("tc", t))
                pe.wait_ge(s["act"].sem, s["act"].at("o", t - 1))
                for x in range(4):
                    e, f = x // 2, x % 2
                    h = 2 * f + e
                    for mc in range(2):
                        last = nc.tensor.matmul(PB[64 * e:64 * e + 64, 6, f * P:(f + 1) * P],
                                                mv[:, mc, h * DH:(h + 1) * DH], probT[:, 2 * x + mc, :],
                                                start=mc == 0, stop=mc == 1)
                last.then_inc(s["pe"].sem, s["pe"].mark("av"))
            s = ss_
            pe.sem_inc(s["pe"].sem, s["pe"].n)
            pe.wait_ge(s["pool"].sem, s["pool"].at("qz"))
            for g in G:
                pe.wait_ge(sp_["act"].sem, sp_["act"].at("o", NCH - 1))
                pe.wait_ge(mem_in, 16 * 2 * (2 * layer + g + 1))
                if g:
                    pe.wait_ge(s["act"].sem, s["act"].at("o1", 0))
                for b in range(4):
                    for f in range(MEMC):
                        last = nc.tensor.matmul(PB[32 * b:32 * b + 32, 0, 0:N_MEM], qmblk[:, f, 4 * g + b, :],
                                                km[:, b, f, :], start=f == 0, stop=f == MEMC - 1)
                last.then_inc(s["pe"].sem, s["pe"].mark("sc"))
                pe.wait_ge(s["dve"].sem, s["dve"].at("pn", g))
                for x in range(2):
                    last = nc.tensor.transpose(PB[:, 2, x * P:(x + 1) * P], prob[:, 0, x * P:(x + 1) * P], ident)
                last.then_inc(s["pe"].sem, s["pe"].mark("tr"))
                pe.wait_ge(s["act"].sem, s["act"].at("tc", g))
                for b in range(4):
                    for f in range(MEMC):
                        for mc in range(2):
                            last = nc.tensor.matmul(PB[:, 6, (f * 4 + b) * QC:(f * 4 + b + 1) * QC],
                                                    vm[:, b, mc, f * P:(f + 1) * P],
                                                    probT[:, mc, 32 * b + QC * f:32 * b + QC * f + QC],
                                                    start=mc == 0, stop=mc == 1)
                last.then_inc(s["pe"].sem, s["pe"].mark("av"))

        def act_mem(act, layer):
            s, ss_ = ma[layer]
            act.sem_inc(s["act"].sem, s["act"].n)
            with act.Fori(0, NCH) as t:
                act.wait_ge(s["dve"].sem, s["dve"].at("mx", t))
                act.wait_ge(s["pe"].sem, s["pe"].at("tr", t - 1))
                for h in range(4):
                    nc.scalar.activation(prob[:, h, :], PB[:, h // 2, (h % 2) * N_MEM:(h % 2 + 1) * N_MEM], ACT.Exp,
                                         bias=vmax[:, h:h + 1], accum_out=vsum[:, h:h + 1]).then_inc(
                                             s["act"].sem, s["act"].mark(f"e{h}"))
                act.wait_ge(s["pe"].sem, s["pe"].at("tr", t))
                act.wait_ge(s["pe"].sem, s["pe"].at("av", t - 1))
                nc.scalar.activation(probT[:, :, :], PB[:, 2:4, :].rearrange("p a (x t) -> p (a x) t", t=P),
                                     ACT.Copy).then_inc(s["act"].sem, s["act"].mark("tc"))
                act.wait_ge(s["pe"].sem, s["pe"].at("av", t))
                nc.scalar.activation(mixT[:, 6:8, bass.ds(t * P, P)], PB[:, 6, 0:2 * P].rearrange("p (f t) -> p f t", f=2),
                                     ACT.Copy).then_inc(s["act"].sem, s["act"].mark("o"))
            s = ss_
            act.sem_inc(s["act"].sem, s["act"].n)
            for g in G:
                act.wait_ge(s["dve"].sem, s["dve"].at("mx", g))
                if g:
                    act.wait_ge(s["pe"].sem, s["pe"].at("av", g - 1))
                nc.scalar.activation(prob[:, 0, :], PB[:, 0, 0:N_MEM], ACT.Exp, bias=vmax[:, 0:1],
                                     accum_out=vsum[:, 0:1]).then_inc(s["act"].sem, s["act"].mark("e0"))
                act.wait_ge(s["pe"].sem, s["pe"].at("tr", g))
                nc.scalar.activation(probT[:, 0:2, :], PB[:, 2, 0:2 * P].rearrange("p (x t) -> p x t", x=2),
                                     ACT.Copy).then_inc(s["act"].sem, s["act"].mark("tc"))
                act.wait_ge(s["pe"].sem, s["pe"].at("av", g))
                for e in range(2):
                    for f in range(MEMC):
                        last = nc.scalar.activation(
                            mixT[64 * e:64 * e + 64, 6 + f, SEQ + 32 * g:SEQ + 32 * g + 32].rearrange("p (b t) -> p b t", b=4),
                            PB[64 * e:64 * e + 64, 6, f * 64:(f + 1) * 64].rearrange("p (b x) -> p b x", b=4)[:, :, 8 * e:8 * e + 8],
                            ACT.Copy)
                    last.then_inc(s["act"].sem, s["act"].mark(f"o{e}"))

        def dve_mem(dve, layer):
            s, ss_ = ma[layer]
            dve.sem_inc(s["dve"].sem, s["dve"].n)
            with dve.Fori(0, NCH) as t:
                dve.wait_ge(s["pe"].sem, s["pe"].at("sc", t))
                dve.wait_ge(s["act"].sem, s["act"].at("e3", t - 1))
                nc.vector.tensor_reduce(vmax, PB[:, 0:2, :].rearrange("p a (e m) -> p (a e) m", e=2), AX_X, ALU.max,
                                        negate=True).then_inc(s["dve"].sem, s["dve"].mark("mx"))
                dve.wait_ge(s["act"].sem, s["act"].at("e3", t))
                nc.vector.reciprocal(vrec, vsum).then_inc(s["dve"].sem, s["dve"].mark("rc"))
                dve.wait_ge(s["dve"].sem, s["dve"].at("rc", t))
                nc.vector.tensor_tensor(prob, prob, vrec.unsqueeze(2).to_broadcast([P, 4, N_MEM]),
                                        ALU.mult).then_inc(s["dve"].sem, s["dve"].mark("pn"))
            s = ss_
            dve.sem_inc(s["dve"].sem, s["dve"].n)
            for g in G:
                dve.wait_ge(s["pe"].sem, s["pe"].at("sc", g))
                nc.vector.tensor_reduce(vmax[:, 0:1], PB[:, 0, 0:N_MEM], AX_X, ALU.max, negate=True).then_inc(
                    s["dve"].sem, s["dve"].mark("mx"))
                dve.wait_ge(s["act"].sem, s["act"].at("e0", g))
                nc.vector.reciprocal(vrec[:, 0:1], vsum[:, 0:1]).then_inc(s["dve"].sem, s["dve"].mark("rc"))
                dve.wait_ge(s["dve"].sem, s["dve"].at("rc", g))
                nc.vector.tensor_scalar(prob[:, 0, :], prob[:, 0, :], vrec[:, 0:1], None, ALU.mult).then_inc(
                    s["dve"].sem, s["dve"].mark("pn"))

        def pool_mem(pool, layer):
            s, ss_ = ma[layer]
            pool.sem_inc(ss_["pool"].sem, ss_["pool"].n)
            for h in range(4):
                e = h % 2
                last = nc.gpsimd.tensor_copy(qmblk[64 * e:64 * e + 64, h // 2, :, 8 * h:8 * h + 8],
                                             mq[64 * e:64 * e + 64, h // 2, SEQ:NT].rearrange("p (b t) -> p b t", b=DEC_B))
            last.then_inc(ss_["pool"].sem, ss_["pool"].mark("qz"))
            pool.wait_ge(ss_["pool"].sem, ss_["pool"].at("qz"))
            pool.sem_inc(s["pool"].sem, s["pool"].n)
            with pool.Fori(0, NCH) as t:
                pool.wait_ge(s["pe"].sem, s["pe"].at("sc", t - 1))
                nc.gpsimd.tensor_copy(mqst, mq[:, :, bass.ds(t * P, P)]).then_inc(s["pool"].sem, s["pool"].mark("st"))

        spr = steps("sbp", dict(
            pe="z0 z1 c0 c1 v0 v1", act="e0 l0 e1 l1 w0 w1 o",
            dve="z0 m0 z1 m1 s0 s1 d0 d1", pool="st"))
        zoff = [0, 512, 896, 1152]
        sbs = xs_[:, 0:4608]
        zP = [sbs[:, 0:1280], sbs[:, 1280:2560]]
        sP = [sbs[:, 2560:3840], membuf[:, 0:1280]]
        qst, kst = membuf[:, 1280:1792], membuf[:, 1792:2304]
        vstP = membuf[:, 2304:2816].rearrange("p (j n) -> p j n", j=NCH)
        zb = [(0, 0), (1, 0), (2, 0), (2, 256)]

        def region(base, j):
            b, c = zb[j]
            return PB[:, base + b, c:c + SEQ - j * P]

        def zreg(a, j, lo=0):
            return a[:, zoff[j] + lo:zoff[j] + SEQ - j * P]

        def pe_sbp(pe):
            s = spr
            pe.sem_inc(s["pe"].sem, s["pe"].n)
            with pe.Fori(0, SBC) as i:
                pe.wait_ge(s["pool"].sem, s["pool"].at("st", i))
                for e in range(2):
                    pe.wait_ge(s["dve"].sem, s["dve"].at("z1", i - 1) if e == 0 else s["dve"].at("z0", i))
                    for j in range(NCH):
                        last = nc.tensor.matmul(region(0, j), kst[64 * e:64 * e + 64, j * P:(j + 1) * P],
                                                qst[64 * e:64 * e + 64, j * P:SEQ], start=True, stop=True)
                    last.then_inc(s["pe"].sem, s["pe"].mark(f"z{e}"))
                for e in range(2):
                    pe.wait_ge(s["dve"].sem, s["dve"].at(f"s{e}", i))
                    pe.wait_ge(s["dve"].sem, s["dve"].at("d1", i - 1) if e == 0 else s["dve"].at("d0", i))
                    for j in range(NCH):
                        r = region(3, j)
                        nc_after = list(range(j + 1, NCH))
                        last = nc.tensor.matmul(r, suffix, zreg(sP[e], j), start=True, stop=not nc_after)
                        for jj in nc_after:
                            last = nc.tensor.matmul(r[:, (jj - j) * P:], ones, zreg(sP[e], jj), start=False,
                                                    stop=jj == NCH - 1)
                    last.then_inc(s["pe"].sem, s["pe"].mark(f"c{e}"))
                for e in range(2):
                    pe.wait_ge(s["act"].sem, s["act"].at(f"w{e}", i))
                    pe.wait_ge(s["act"].sem, s["act"].at("o", i - 1))
                    for j in range(NCH):
                        last = nc.tensor.matmul(PB[64 * e:64 * e + 64, 6, j * P:SEQ], vstP[:, j, 64 * e:64 * e + 64],
                                                zreg(zP[e], j), start=j == 0, stop=j == NCH - 1)
                    last.then_inc(s["pe"].sem, s["pe"].mark(f"v{e}"))

        def act_sbp(act):
            s = spr
            act.sem_inc(s["act"].sem, s["act"].n)
            with act.Fori(0, SBC) as i:
                for e in range(2):
                    act.wait_ge(s["dve"].sem, s["dve"].at(f"m{e}", i))
                    nc.scalar.activation(sP[e], sP[e], ACT.Exp).then_inc(s["act"].sem, s["act"].mark(f"e{e}"))
                    act.wait_ge(s["act"].sem, s["act"].at(f"e{e}", i))
                    nc.scalar.activation(sP[e], sP[e], ACT.Ln, bias=onec).then_inc(s["act"].sem, s["act"].mark(f"l{e}"))
                for e in range(2):
                    act.wait_ge(s["dve"].sem, s["dve"].at(f"d{e}", i))
                    nc.scalar.activation(zP[e], zP[e], ACT.Exp).then_inc(s["act"].sem, s["act"].mark(f"w{e}"))
                act.wait_ge(s["pe"].sem, s["pe"].at("v1", i))
                nc.scalar.activation(mixT[:, bass.ds(i, 1), 0:SEQ].rearrange("p a n -> p (a n)"), PB[:, 6, :],
                                     ACT.Copy).then_inc(s["act"].sem, s["act"].mark("o"))

        def dve_sbp(dve):
            s = spr
            dve.sem_inc(s["dve"].sem, s["dve"].n)
            with dve.Fori(0, SBC) as i:
                for e in range(2):
                    dve.wait_ge(s["pe"].sem, s["pe"].at(f"z{e}", i))
                    dve.wait_ge(s["pe"].sem, s["pe"].at(f"v{e}", i - 1))
                    bias = biash[:, bass.ds(2 * i + e, 1)]
                    for j in range(NCH):
                        last = nc.vector.scalar_tensor_tensor(out=zreg(zP[e], j), in0=region(0, j), scalar=bias,
                                                              in1=strict[:, 0:SEQ - j * P], op0=ALU.add, op1=ALU.add)
                    last.then_inc(s["dve"].sem, s["dve"].mark(f"z{e}"))
                    dve.wait_ge(s["dve"].sem, s["dve"].at(f"z{e}", i))
                    nc.vector.tensor_scalar(sP[e], zP[e], 40.0, None, ALU.min).then_inc(s["dve"].sem, s["dve"].mark(f"m{e}"))
                for e in range(2):
                    dve.wait_ge(s["act"].sem, s["act"].at(f"l{e}", i))
                    nc.vector.tensor_tensor(sP[e], sP[e], zP[e], ALU.max).then_inc(s["dve"].sem, s["dve"].mark(f"s{e}"))
                for e in range(2):
                    dve.wait_ge(s["pe"].sem, s["pe"].at(f"c{e}", i))
                    for j in range(NCH):
                        last = nc.vector.tensor_tensor(zreg(zP[e], j), zreg(zP[e], j), region(3, j), ALU.subtract)
                    last.then_inc(s["dve"].sem, s["dve"].mark(f"d{e}"))

        def pool_sbp(pool):
            s = spr
            pool.sem_inc(s["pool"].sem, s["pool"].n)
            with pool.Fori(0, SBC) as i:
                pool.wait_ge(s["pe"].sem, s["pe"].at("v1", i - 1))
                nc.gpsimd.tensor_copy(qst, mixT[:, bass.ds(i, 1), 0:SEQ].rearrange("p a n -> p (a n)"))
                nc.gpsimd.tensor_copy(kst, kvT[:, bass.ds(i, 1), 0:SEQ].rearrange("p a n -> p (a n)"))
                nc.gpsimd.tensor_copy(vstP, vtok[:, :, bass.ds(i * P, P)]).then_inc(s["pool"].sem, s["pool"].mark("st"))

        ssm = steps("sbs", dict(pe="z " + " ".join(f"t{u}" for u in range(5)) + " v r",
                                act="z0 z1 e0 l0 e1 l1 w0 w1 t0 t2 t4 o m",
                                dve="k0 k1 m0 m1 s0 c0 s1 c1 d0 d1 t1 t3", pool="q"))
        kpage = big[:, 0:PAGES * SBC * P].rearrange("p (c n) -> p c n", c=PAGES)
        vpage = big[:, PAGES * SBC * P:2 * PAGES * SBC * P].rearrange("p (c n) -> p c n", c=PAGES)
        k_in, v_in = sem("k_in"), sem("v_in")
        SROWS = [P, P // 2]
        PAST = PAGES * P
        zS = [xflat[0:SROWS[w], w * ZW:(w + 1) * ZW] for w in range(2)]
        sS = [membuf[0:SROWS[w], w * ZW:(w + 1) * ZW] for w in range(2)]
        TW = P + P // 2
        wT = membuf[:, 0:NC * TW].rearrange("p (c r) -> p c r", c=NC)
        oS = big[:, 12288:12288 + 2 * P]
        qs = big[:, 12288 + 2 * P:12288 + 2 * P + SBC * 32].rearrange("p (f x) -> p f x", f=SBC)
        SETS = [(0, 4), (4, SBC)]
        units_of = [(0, 2), (2, 4), (4, 6), (6, PAGES - 1), (PAGES - 1, NC)]

        def pe_sbs(pe):
            s = ssm
            pe.sem_inc(s["pe"].sem, s["pe"].n)
            with pe.Fori(0, DEC_B) as b:
                pe.wait_ge(k_in, b * (16 * PAGES) + 16 * PAGES)
                pe.wait_ge(s["pool"].sem, s["pool"].at("q", b))
                pe.wait_ge(s["act"].sem, s["act"].at("z1", b - 1))
                for w, (f0, f1) in enumerate(SETS):
                    for span in range(3):
                        for f in range(f0, f1):
                            g = f - f0
                            if span < 2:
                                rhs = kpage[:, 4 * span:4 * span + 4, f * P:(f + 1) * P]
                                dst = PB[32 * g:32 * g + 32, 2 * w + span, :].rearrange("p (c n) -> p c n", c=4)
                            else:
                                rhs, dst = kvT[:, f, SEQ:NT], PB[32 * g:32 * g + 32, 4, w * NS:(w + 1) * NS]
                            last = nc.tensor.matmul(dst, qs[:, f, :], rhs, start=True, stop=True)
                last.then_inc(s["pe"].sem, s["pe"].mark("z"))
                for u, (c0, c1) in enumerate(units_of):
                    if u >= 2:
                        e = "act" if u % 2 == 0 else "dve"
                        pe.wait_ge(s[e].sem, s[e].at(f"t{u - 2}", b))
                    elif u == 0:
                        pe.wait_ge(s["act"].sem, s["act"].at("w1", b))
                    for c in range(c0, c1):
                        n = P if c < PAGES else NS
                        for w in range(2):
                            o = (c - c0) * TW + w * P
                            last = nc.tensor.transpose(PB[0:n, 5 + u % 2, o:o + SROWS[w]], zS[w][:, c * P:c * P + n],
                                                       ident[0:SROWS[w], 0:SROWS[w]])
                    last.then_inc(s["pe"].sem, s["pe"].mark(f"t{u}"))
                pe.wait_ge(s["act"].sem, s["act"].at("t4", b))
                pe.wait_ge(s["dve"].sem, s["dve"].at("t3", b))
                pe.wait_ge(v_in, b * (16 * PAGES) + 16 * PAGES)
                for w, (f0, f1) in enumerate(SETS):
                    for c in range(NC):
                        for f in range(f0, f1):
                            g, n = f - f0, P if c < PAGES else NS
                            v = vpage[:, c, f * P:(f + 1) * P] if c < PAGES else vnew64[0:NS, f * P:(f + 1) * P]
                            last = nc.tensor.matmul(PB[32 * g:32 * g + 32, 7, w * P:(w + 1) * P],
                                                    wT[0:n, c, w * P + 32 * g:w * P + 32 * g + 32], v,
                                                    start=c == 0, stop=c == NC - 1)
                last.then_inc(s["pe"].sem, s["pe"].mark("v"))
                pe.wait_ge(s["act"].sem, s["act"].at("o", b))
                for w in range(2):
                    last = nc.tensor.transpose(PB[:, 5, w * P:w * P + SROWS[w]], oS[0:SROWS[w], w * P:(w + 1) * P],
                                               ident[0:SROWS[w], 0:SROWS[w]])
                last.then_inc(s["pe"].sem, s["pe"].mark("r"))

        def sbs_t_evac(u):
            c0, c1 = units_of[u]
            parts = [(c0, c1, P)] if c1 < NC else [(c0, PAGES, P), (PAGES, NC, NS)]
            return [(wT[0:n, a:b, :], PB[0:n, 5 + u % 2, (a - c0) * TW:(b - c0) * TW].rearrange("p (c r) -> p c r", c=b - a))
                    for a, b, n in parts]

        def act_sbs(act):
            s = ssm
            S_, mark = s["act"].sem, s["act"].mark
            act.sem_inc(S_, s["act"].n)
            with act.Fori(0, DEC_B) as b:
                wait = lambda e, name, it=b: act.wait_ge(s[e].sem, s[e].at(name, it))
                wait("pe", "z")
                for w in range(2):
                    r = SROWS[w]
                    nc.scalar.activation(zS[w][:, 0:PAST], PB[0:r, 2 * w:2 * w + 2, :].rearrange("p a n -> p (a n)"),
                                         ACT.Identity, bias=sbias[0:r, w:w + 1])
                    nc.scalar.activation(zS[w][:, PAST:ZW], PB[0:r, 4, w * NS:(w + 1) * NS], ACT.Identity,
                                         bias=sbias[0:r, w:w + 1]).then_inc(S_, mark(f"z{w}"))
                for w in range(2):
                    wait("dve", f"m{w}")
                    nc.scalar.activation(sS[w], sS[w], ACT.Exp).then_inc(S_, mark(f"e{w}"))
                    wait("act", f"e{w}")
                    nc.scalar.activation(sS[w], sS[w], ACT.Ln, bias=onec[0:SROWS[w], :]).then_inc(S_, mark(f"l{w}"))
                for w in range(2):
                    wait("dve", f"d{w}")
                    nc.scalar.activation(zS[w], zS[w], ACT.Exp).then_inc(S_, mark(f"w{w}"))
                for u in range(0, len(units_of), 2):
                    wait("pe", f"t{u}")
                    wait("dve", "d1")
                    for dst, src in sbs_t_evac(u):
                        last = nc.scalar.activation(dst, src, ACT.Copy)
                    last.then_inc(S_, mark(f"t{u}"))
                wait("pe", "v")
                nc.scalar.activation(oS[:, 0:P], PB[:, 7, 0:P], ACT.Copy)
                nc.scalar.activation(oS[0:P // 2, P:2 * P], PB[0:P // 2, 7, P:2 * P], ACT.Copy).then_inc(S_, mark("o"))
                wait("pe", "r")
                for e in range(2):
                    for w, (f0, f1) in enumerate(SETS):
                        src = PB[64 * e:64 * e + 64, 5, w * P:w * P + SROWS[w]].rearrange("p (g x) -> p g x", x=32)
                        last = nc.scalar.activation(mixT[64 * e:64 * e + 64, f0:f1, bass.ds(b * DEC_T + SEQ, DEC_T)],
                                                    src[:, :, 8 * e:8 * e + 8], ACT.Copy)
                last.then_inc(S_, mark("m"))

        def dve_sbs(dve):
            s = ssm
            S_, mark = s["dve"].sem, s["dve"].mark
            dve.sem_inc(S_, s["dve"].n)
            with dve.Fori(0, DEC_B) as b:
                wait = lambda e, name, it=b: dve.wait_ge(s[e].sem, s[e].at(name, it))
                for w in range(2):
                    wait("act", f"z{w}")
                    nc.vector.tensor_tensor(zS[w][:, PAST:ZW], zS[w][:, PAST:ZW],
                                            strict8[0:SROWS[w], bass.ds(b * NS, NS)], ALU.add).then_inc(S_, mark(f"k{w}"))
                wait("pe", "v", b - 1)
                for w in range(2):
                    wait("dve", f"k{w}")
                    nc.vector.tensor_scalar(sS[w], zS[w], 40.0, None, ALU.min).then_inc(S_, mark(f"m{w}"))
                for w in range(2):
                    wait("act", f"l{w}")
                    nc.vector.tensor_tensor(sS[w], sS[w], zS[w], ALU.max).then_inc(S_, mark(f"s{w}"))
                    wait("dve", f"s{w}")
                    back = sS[w][:, ::-1]
                    nc.vector.tensor_tensor_scan(back, back, back, 0.0, ALU.add, ALU.max).then_inc(S_, mark(f"c{w}"))
                for w in range(2):
                    wait("dve", f"c{w}")
                    nc.vector.tensor_tensor(zS[w], zS[w], sS[w], ALU.subtract).then_inc(S_, mark(f"d{w}"))
                for u in (1, 3):
                    wait("pe", f"t{u}")
                    for dst, src in sbs_t_evac(u):
                        last = nc.vector.tensor_copy(dst, src)
                    last.then_inc(S_, mark(f"t{u}"))

        def pool_sbs(pool):
            s = ssm
            pool.sem_inc(s["pool"].sem, s["pool"].n)
            with pool.Fori(0, DEC_B) as b:
                pool.wait_ge(s["pe"].sem, s["pe"].at("z", b - 1))
                nc.gpsimd.tensor_copy(qs[:, :, 0:QC], qblk[:, :, bass.ds(b, 1), :].rearrange("p f a x -> p f (a x)")).then_inc(
                    s["pool"].sem, s["pool"].mark("q"))

        def mem_place(layer, which):
            if which == 0:
                return lambda i, k: [(mkv[:, layer, 0, k, :], PB[:, k, 0:N_MEM])]
            return lambda i, k: [(mkv[:, layer, 1, :, k * P:(k + 1) * P], PB[:, k, 0:N_MEM].rearrange("p (t n) -> p t n", t=2))]

        def v_place(i, k):
            col = bass.ds((2 * i + k) * P, P)
            return [(vtok[:, :, col], PB[:, k, :].rearrange("p (t n) -> p t n", t=NCH)),
                    (vnew64[0:NS, col], PB[0:NS, 2 + k, 0:P])]

        @block.tensor
        def _(pe):
            mn = [bigv[:, 0:KD, :], bigv[:, KD:2 * KD, :]]
            pe.wait_ge(mem_loaded, MEM_LOADS)
            pe_stats(pe, "mem", N_MEM)
            pe_stats(pe, "mix_pre0")
            for layer in range(2):
                pe.wait_ge(normed, applied[f"mem{layer}"])
                pe_units(pe, f"mem{layer}", mn[layer], N_MEM, count=2)
                pe_units(pe, f"mem{layer}", mn[layer], N_MEM, swap=True, count=2, first=2)
            pe.wait_ge(loaded, LOADS)
            pe_tokens(pe)
            pe_units(pe, "in_a", xnT, count=UNITS["in_a"])
            dn_run(pe, "pe", dn_pe, lambda c: ())
            pe_mem(pe, 0)
            pe.wait_ge(ma[0][1]["act"].sem, ma[0][1]["act"].at("o1", 1))
            pe.wait_ge(dn_s["dve"].sem, dn_s["dve"].at("oz1"))
            pe_units(pe, "out_a", mixT, count=KD)
            pe_stats(pe, "mix_post0")
            for layer in range(2):
                if layer:
                    pe_stats(pe, "kv")
                    pe.wait_ge(normed, applied["kv"])
                    pe_units(pe, "kv", xnT, count=SBC)
                    pe_units(pe, "kv", xnT, swap=True, count=SBC, first=SBC)
                    pe.wait_ge(normed, applied["mix_pre1"])
                    pe_units(pe, "in_b", xnT, count=UNITS["in_b"])
                    pe_mem(pe, 1)
                    pe.wait_ge(consts_b, 16)
                    pe_sbp(pe)
                    pe_sbs(pe)
                    pe.wait_ge(ssm["act"].sem, ssm["act"].at("m", DEC_B - 1))
                    pe_units(pe, "out_b", mixT, count=KD)
                    pe_stats(pe, "mix_post1")
                pe_stats(pe, f"ffn_pre{layer}")
                pe.wait_ge(normed, applied[f"ffn_pre{layer}"])
                pe_units(pe, f"up{layer}", xnT, count=2 * FF)
                pe.wait_ge(y_ready, 1 + (conv_base[f"up{layer}"] + 2 * FF) // 2)
                pe_down(pe, f"down{layer}", bigv)
                pe_stats(pe, f"ffn_post{layer}")

        @block.scalar
        def _(act):
            act.sem_inc(gated, 2)
            nc.scalar.preload_act_table_set(EXP_LN)
            act.wait_ge(zeroed, 1)
            act.wait_ge(mem_loaded, MEM_LOADS)
            act_stats(act, "mem", mixT, N_MEM)
            act.wait_ge(loaded, LOADS)
            act_stats(act, "mix_pre0", hT)
            for layer in range(2):
                act_evac(act, f"mem{layer}", mem_place(layer, 0), 2)
                act_evac(act, f"mem{layer}", mem_place(layer, 1), 2, first=2)
            act_tokens(act)
            act_conv(act, "in_a", DN_TAPS, QKV)
            act_evac(act, "in_a", chunked(bigv, QKV), DN_H, first=QKV, func=ACT.Silu)
            act_evac(act, "in_a", chunked(mq), 2, first=QKV + DN_H, scale=DH ** -0.5)
            act.wait_ge(conv_done, 2 + QKV)
            act.wait_ge(tail_kept, 2 + QKV)
            nc.scalar.preload_act_table_set(EXP_LN)
            dn_run(act, "act", dn_act, lambda c: (dn_cols(c),))
            act_mem(act, 0)
            act_evac(act, "out_a", chunked(xnT), KD)
            act_stats(act, "mix_post0", xnT)
            for layer in range(2):
                if layer:
                    act_stats(act, "kv", hT)
                    act.wait_ge(tail_kept, 2 + QKV + 2 * FF)
                    act_evac(act, "kv", chunked(kvT), SBC)
                    act_evac(act, "kv", v_place, SBC, first=SBC)
                    act_evac(act, "in_b", chunked(mixT), SBC, scale=DH ** -0.5)
                    act_evac(act, "in_b", chunked(mq), 2, first=SBC, scale=DH ** -0.5)
                    act_mem(act, 1)
                    act_sbp(act)
                    act_sbs(act)
                    act_evac(act, "out_b", chunked(xnT), KD)
                    act_stats(act, "mix_post1", xnT)
                    act.wait_ge(kv_stored, 16 * 3)
                act.wait_ge(hid, HID[f"mix_post{layer}"])
                act_stats(act, f"ffn_pre{layer}", hT)
                act.wait_ge(pads_zeroed, layer + 2)
                act_conv(act, f"up{layer}", FF_TAPS, 2 * FF)
                act_down(act, f"down{layer}")
                nc.scalar.preload_act_table_set(EXP_LN)
                act_stats(act, f"ffn_post{layer}", xnT)
                act.wait_ge(hid, HID[f"ffn_post{layer}"])

        @block.vector
        def _(dve):
            dve.sem_inc(conv_done, 2)
            dve.sem_inc(y_ready, 1)
            mn = [bigv[:, 0:KD, :], bigv[:, KD:2 * KD, :]]
            dve.wait_ge(mem_loaded, MEM_LOADS)
            for layer in range(2):
                dve_apply(dve, "mem", f"mem{layer}", mixT, mn[layer], N_MEM)
            dve.wait_ge(loaded, LOADS)
            dve_apply(dve, "mix_pre0", "mix_pre0", hT, xnT)
            dve_tokens(dve)
            dve.wait_ge(pads_zeroed, 1)
            dve_conv(dve, "in_a", DN_TAPS, QKV)
            dve.wait_ge(evacuated, UNIT0["in_a"] + UNITS["in_a"])
            dve.wait_ge(gated, 2 + QKV)
            dn_run(dve, "dve", dn_dve, lambda c: (dn_cols(c), (lambda g: mixT[:, 3 * g:3 * g + 3, SEQ:NT]) if isinstance(c, int)
                                                 else (lambda g: mixT[:, 3 * g:3 * g + 3, bass.ds(c * P, P)])))
            dve_mem(dve, 0)
            dve_residual(dve, "mix_post0")
            for layer in range(2):
                if layer:
                    dve_apply(dve, "kv", "kv", hT, xnT)
                    dve.wait_ge(unit_done, UNIT0["kv"] + UNITS["kv"])
                    dve_apply(dve, "kv", "mix_pre1", hT, xnT)
                    dve_mem(dve, 1)
                    dve.wait_ge(consts_b, 16)
                    dve_sbp(dve)
                    dve_sbs(dve)
                    dve_residual(dve, "mix_post1")
                dve_apply(dve, f"ffn_pre{layer}", f"ffn_pre{layer}", hT, xnT)
                dve_conv(dve, f"up{layer}", FF_TAPS, 2 * FF)
                dve_residual(dve, f"ffn_post{layer}")

        @block.gpsimd
        def _(pool):
            nc.gpsimd.memset(qmblk[:, :, :, :], 0.0)
            nc.gpsimd.memset(qblk[:, :, :, :], 0.0)
            nc.gpsimd.memset(epsc, EPS)
            nc.gpsimd.memset(onec, 1.0).then_inc(zeroed, 1)
            nc.gpsimd.memset(rawp[:, :, 0:DN_TAPS - 1], 0.0).then_inc(pads_zeroed, 1)
            pool.sem_inc(tail_kept, 2)
            pool.wait_ge(loaded, LOADS)
            pool.wait_ge(zeroed, 1)
            pool_conv(pool, "in_a", DN_TAPS, QKV)
            pool.wait_ge(tail_kept, 2 + QKV)
            pool.dma_start(d["o_dnconv"], cnew[:, 0:QKV * (DEC_B + 1) * (DN_TAPS - 1)]).then_inc(dnconv_out, 16)
            pool.wait_ge(pads_ready, QKV)
            pool.dma_start(cstate[:, :], d["ff_state"][0]).then_inc(state_in, 16)
            pool.wait_ge(rstd_ready, stat["mix_pre0"])
            pool.wait_ge(unit_done, UNIT0["out_a"])
            pool.wait_ge(gated, 2 + QKV)
            pool.wait_ge(conv_done, 2 + QKV)
            nc.gpsimd.memset(Sst[:, :, :], 0.0)
            nc.gpsimd.memset(WTm[:, :, :], 0.0).then_inc(po.sem, po.inc())
            pool.wait_ge(po.sem, po.value)
            dn_run(pool, "pool", dn_pool, lambda c: ((bigv[:, 2 * DN_H:3 * DN_H, SEQ:NT] if isinstance(c, int)
                                                      else bigv[:, 2 * DN_H:3 * DN_H, bass.ds(c * P, P)]),))
            pool.wait_ge(dn_s["dve"].sem, dn_s["dve"].at("oz1"))
            pool_mem(pool, 0)
            for layer in range(2):
                if layer:
                    pool.dma_start(pconst[:, 0:P + SEQ + DEC_B * NS], d["c_sb"]).then_inc(consts_b, 16)
                    pool.wait_ge(evacuated, UNIT0["in_b"] + UNITS["in_b"])
                    for e in range(2):
                        last = nc.gpsimd.tensor_copy(
                            qblk[64 * e:64 * e + 64, :, :, 8 * e:8 * e + 8],
                            mixT[64 * e:64 * e + 64, 0:SBC, SEQ:NT].rearrange("p c (b t) -> p c b t", b=DEC_B))
                    last.then_inc(po.sem, po.inc())
                    pool.wait_ge(po.sem, po.value)
                    pool_mem(pool, 1)
                    pool.wait_ge(ma[1][1]["pe"].sem, ma[1][1]["pe"].at("av", 1))
                    nc.gpsimd.memset(qs[:, :, QC:32], 0.0)
                    pool_sbp(pool)
                    pool_sbs(pool)
                pool.wait_ge(hid, HID[f"mix_post{layer}"])
                if layer:
                    pool.wait_ge(kv_stored, 16 * 3)
                nc.gpsimd.memset(rawp[:, :, 0:FF_TAPS - 1], 0.0).then_inc(pads_zeroed, 1)
                pool.wait_ge(state_in, 16 * (layer + 1))
                pool.wait_ge(dnconv_out if layer == 0 else ffconv_out, 16)
                pool_conv(pool, f"up{layer}", FF_TAPS, 2 * FF)
                pool.wait_ge(tail_kept, 2 + QKV + 2 * FF * (layer + 1))
                pool.dma_start(d["o_ffconv"][layer], cnew[:, :]).then_inc(ffconv_out, 16)
                if not layer:
                    pool.wait_ge(pads_ready, QKV + 2 * FF)
                    pool.dma_start(cstate[:, :], d["ff_state"][1]).then_inc(state_in, 16)
            pool.wait_ge(ffconv_out, 32)

        @block.sync
        def _(sp):
            def load(s, dst, src):
                sp.dma_start(dst, src).then_inc(s, 16)
            load(mem_loaded, mixT[:, :, 0:N_MEM], d["memT"].rearrange("c p n -> p c n"))
            load(mem_loaded, common[:, :], d["c_common"])
            load(mem_loaded, gains[:, :, :], d["gains"])
            load(mem_loaded, alog, d["a_log"].to_broadcast([P, DN_H]))
            load(mem_loaded, dtb, d["dt_bias"].to_broadcast([P, DN_H]))
            load(mem_loaded, ogain, d["o_gain"])

            def feed(name, first=0, count=None):
                n = UNITS[name] if count is None else count
                u0 = UNIT0[name] + first

                def unit(i, k):
                    if not (isinstance(i, int) and u0 + k < 2):
                        sp.wait_ge(unit_done, 2 * i + (u0 + k - 1))
                    if name.startswith("down"):
                        r = 2 * i + (first + k)
                        src, dst = d["w_down"][int(name[-1])], ring[:, k, :]
                    else:
                        r = 2 * i + (W8_ROW[name] + first + k)
                        src, dst = d["w8"], ring[:, k, 0:KD * P]
                    src = src[r] if isinstance(r, int) else src[bass.ds(r, 1), :, :].rearrange("a p n -> p (a n)")
                    sp.dma_start(dst, src).then_inc(w_full[k], 16)
                if n == 2:
                    for k in range(2):
                        unit(0, k)
                else:
                    with sp.Fori(0, n // 2) as i:
                        for k in range(2):
                            unit(i, k)

            feed("mem0", count=2)
            load(loaded, hT[:, :, :], d["xT"].rearrange("c p n -> p c n"))
            load(loaded, pconst[:, :], d["c_dn"])
            load(loaded, dnw[:, :, :], d["dn_w"])
            load(loaded, cstate[:, 0:QKV * DEC_B * (DN_TAPS - 1)], d["dn_state"])
            load(loaded, wba[:, :, :], d["w_ba"])
            load(loaded, biash[:, :], d["sb_bias"].to_broadcast([P, SB_H]))
            load(loaded, ffw[:, :, :, :], d["ff_w"])
            load(loaded, pages[:, :], d["page_table"])
            load(loaded, sbias[:, :], d["sb_bias_rows"])
            feed("mem0", first=2, count=2)
            feed("mem1")
            feed("in_a")
            sp.wait_ge(evacuated, UNIT0["in_a"])
            store(sp, d["o_mkv"], mkv[:, :, :, :, :].rearrange("p l w c n -> p (l w c n)"))
            feed("out_a", count=2)
            sp.wait_ge(rstd_ready, stat["mix_pre0"])
            for h in range(2):
                sp.dma_start(S8[h], d["state_dn"][h]).then_inc(s8_in[h], 16)
            sp.wait_ge(dn_p["dve"].sem, dn_p["dve"].at("s5", NCH - 1))
            store(sp, d["o_dns_p"], Sst[:, :, :])
            for h in range(DN_H):
                sp.wait_ge(dn_s["dve"].sem, dn_s["dve"].at(f"sn{h}"))
                sp.dma_start(d["o_dns_s"][h], S8[h % 2]).then_inc(s8_out, 16)
                if h + 2 < DN_H:
                    sp.wait_ge(s8_out, 16 * (h + 1))
                    sp.dma_start(S8[h % 2], d["state_dn"][h + 2]).then_inc(s8_in[h % 2], 16)
            sp.wait_ge(s8_out, 16 * DN_H)

            def mem_load(layer, g):
                sp.dma_start(km[:, :, :, :].rearrange("p b c m -> p b (c m)"),
                             d["cache_mk"][layer, 4 * g:4 * g + 4].rearrange("b p n -> p b n")).then_inc(mem_in, 16)
                sp.dma_start(vm[:, :, :, :].rearrange("p b c m -> p b (c m)"),
                             d["cache_mv"][layer, 4 * g:4 * g + 4].rearrange("b p n -> p b n")).then_inc(mem_in, 16)
            mem_load(0, 0)
            sp.wait_ge(ma[0][1]["pe"].sem, ma[0][1]["pe"].at("av", 0))
            mem_load(0, 1)
            feed("out_a", first=2, count=KD - 2)
            feed("up0")
            feed("down0")
            feed("kv")

            def page_loads(b):
                at = [sp.value_load(pages[0:1, b * PAGES + j:b * PAGES + j + 1] if isinstance(b, int)
                                    else pages[0:1, bass.ds(b * PAGES + j, 1)],
                                    min_val=0, max_val=d["kpages"].shape[0] - 1) for j in range(PAGES)]
                for cache, dst, s, used in (("kpages", kpage, k_in, "z"), ("vpages", vpage, v_in, "v")):
                    if not isinstance(b, int):
                        sp.wait_ge(ssm["pe"].sem, ssm["pe"].at(used, b - 1))
                    for j in range(PAGES):
                        sp.dma_start(dst[:, j, :], d[cache][bass.ds(at[j], 1), :, :].rearrange("a p n -> p (a n)")).then_inc(s, 16)
            sp.wait_ge(unit_done, UNIT0["kv"])
            page_loads(0)
            feed("in_b")
            sp.wait_ge(evacuated, UNIT0["in_b"])
            sp.dma_start(d["o_k"], kvT[:, :, :]).then_inc(kv_stored, 16)
            sp.dma_start(d["o_v"], vtok[:, :, :]).then_inc(kv_stored, 16)
            sp.dma_start(d["o_vs"], vnew64[0:NS, :]).then_inc(kv_stored, 16)
            sp.wait_ge(rstd_ready, stat["kv"])
            mem_load(1, 0)
            feed("out_b", count=2)
            sp.wait_ge(ma[1][1]["pe"].sem, ma[1][1]["pe"].at("av", 0))
            mem_load(1, 1)
            with sp.Fori(1, DEC_B) as b:
                page_loads(b)
            feed("out_b", first=2, count=KD - 2)
            feed("up1")
            feed("down1")
            sp.wait_ge(hid, HID["ffn_post1"])
            store(sp, d["o_y"].rearrange("c p n -> p c n"), hT[:, :, :])
            sp.wait_ge(kv_stored, 16 * 3)
            sp.wait_ge(stored, n_stored[0])


def kernel(**inputs):
    from concourse.bacc import Bacc
    from concourse.bass_utils import run_bass_kernel_spmd

    x = {n: np.asarray(a) for n, a in inputs.items()}
    A = np.ascontiguousarray
    nu = D_MODEL // P

    def units(w):
        return w.reshape(nu, P, -1, P).transpose(2, 1, 0, 3).reshape(-1, P, nu * P)

    def halves(a):
        return a.reshape(a.shape[:-1] + (2, FF, P)).swapaxes(-3, -2).reshape(a.shape)

    def chunks(a):
        r = a.reshape(a.shape[:-1] + (-1, P))
        return np.moveaxis(r, (-1, -2), (0, 1))

    def bias_rows(b):
        r = np.zeros((2, 4, 4, DEC_T), b.dtype)
        r[:, :, 0:2] = np.concatenate([b, np.zeros(4, b.dtype)]).reshape(2, 4, 2)[..., None]
        return A(r.reshape(2, P).T)

    zcols = (QKV + DN_H) * P
    wa, wb = x["w_in_a"][0], x["w_in_b"][0]
    parts = {"mem0": x["w_mem_kv"][0], "mem1": x["w_mem_kv"][1],
             "in_a": np.concatenate([wa[:, :zcols], wa[:, zcols + 2 * DN_H:]], 1), "out_a": x["w_out_a"][0],
             "up0": halves(x["ffn_w_up"][0]), "kv": x["w_kv"], "in_b": wb, "out_b": x["w_out_b"][0],
             "up1": halves(x["ffn_w_up"][1])}
    c_common, c_dn, c_sb = constants()
    n_phys = x["cache_k"].shape[0]
    gains_ = np.concatenate([x["mem_norm"], x["norm_mix_pre"], x["norm_mix_post"], x["norm_ffn_pre"], x["norm_ffn_post"],
                             x["kv_norm"][None]], 0)
    order = [0, 1, 2, 4, 6, 8, 10, 3, 5, 7, 9]
    arrays = {
        "xT": A(np.concatenate([x["x_prompt"].reshape(SEQ, -1), x["x_sample"].reshape(NS, -1)]).T.reshape(nu, P, NT)),
        "memT": A(x["mem_prompt"][0].T.reshape(nu, P, N_MEM)),
        "w8": np.concatenate([units(parts[n]) for n in W8]),
        "w_down": A(x["ffn_w_down"].reshape(2, 2, FF // 2, P, nu, P).transpose(0, 4, 1, 3, 2, 5).reshape(2, 2 * nu, P, SLOT)),
        "w_ba": A(wa[:, zcols:zcols + 2 * DN_H].reshape(nu, P, 2 * DN_H).transpose(1, 0, 2)),
        "gains": A(chunks(gains_[order]).transpose(0, 2, 1)),
        "a_log": A(x["dn_a_log"].reshape(1, DN_H)), "dt_bias": A(x["dn_dt_bias"].reshape(1, DN_H)),
        "o_gain": A(x["dn_o_gain"].reshape(P, 1)), "sb_bias": A(x["sb_bias"].reshape(1, SB_H)),
        "sb_bias_rows": bias_rows(x["sb_bias"].reshape(SB_H)),
        "dn_w": A(chunks(x["dn_conv_w"][0])),
        "ff_w": A(chunks(halves(np.concatenate([x["ffn_conv_w"], x["ffn_conv_b"][:, None]], 1))).transpose(0, 2, 1, 3)),
        "dn_state": A(chunks(x["state_dn_conv"][0]).reshape(P, -1)),
        "ff_state": A(np.stack([chunks(halves(x["state_ffn_conv"][l])).reshape(P, -1) for l in range(2)])),
        "state_dn": A(x["state_dn"][0].transpose(1, 2, 0, 3)),
        "cache_mk": A(x["cache_mem_k"].reshape(2, DEC_B, N_MEM, MEMC, P).transpose(0, 1, 4, 3, 2).reshape(2, DEC_B, P, -1)),
        "cache_mv": A(x["cache_mem_v"].reshape(2, DEC_B, 2, P, MEMC * P).transpose(0, 1, 3, 2, 4).reshape(2, DEC_B, P, -1)),
        "kpages": A(x["cache_k"].reshape(n_phys, P, SBC, P).transpose(0, 3, 2, 1).reshape(n_phys, P, SBC * P)),
        "vpages": A(x["cache_v"].reshape(n_phys, P, SBC * P)),
        "page_table": A(x["page_table"].reshape(1, -1)),
        "c_common": c_common, "c_dn": c_dn, "c_sb": c_sb,
    }
    outs = {"o_y": (nu, P, NT), "o_dns_p": (P, DN_H, P), "o_dns_s": (DN_H, P, DEC_B, P),
            "o_dnconv": (P, QKV * (DEC_B + 1) * (DN_TAPS - 1)), "o_ffconv": (2, P, 2 * FF * (DEC_B + 1) * (FF_TAPS - 1)),
            "o_k": (P, SBC, NT), "o_v": (P, NCH, SBC * P), "o_vs": (NS, SBC * P), "o_mkv": (P, 2 * 2 * 2 * N_MEM)}
    nc = Bacc("TRN2", target_bir_lowering=False, num_devices=1)
    d = {n: nc.dram_tensor(f"in_{n}", a.shape, mybir.dt.from_np(a.dtype), kind="ExternalInput").ap() for n, a in arrays.items()}
    d.update({n: nc.dram_tensor(n, s, F32, kind="ExternalOutput").ap() for n, s in outs.items()})
    build(nc, d)
    r = run_bass_kernel_spmd(nc, [{f"in_{n}": a for n, a in arrays.items()}], core_ids=[0]).results[0]

    y = r["o_y"].transpose(2, 0, 1).reshape(NT, D_MODEL)

    def unchunk(a, n, taps):
        a = a.reshape(P, n, DEC_B + 1, taps).transpose(2, 3, 1, 0)
        return a.reshape(DEC_B + 1, taps, n * P)

    def unhalve(a):
        return a.reshape(a.shape[:-1] + (FF, 2, P)).swapaxes(-3, -2).reshape(a.shape)

    dc = unchunk(r["o_dnconv"], QKV, DN_TAPS - 1)
    fc = np.stack([unhalve(unchunk(r["o_ffconv"][l], 2 * FF, FF_TAPS - 1)) for l in range(2)])
    k = r["o_k"].transpose(2, 1, 0).reshape(NT, SB_H, DH)
    vp = r["o_v"].transpose(1, 0, 2).reshape(1, SEQ, SB_H, DH)
    mkv = r["o_mkv"].reshape(P, 2, 2, 2, N_MEM)
    mk = mkv[:, :, 0].transpose(1, 3, 2, 0).reshape(2, 1, N_MEM, 4, DH)
    mv = mkv[:, :, 1].transpose(1, 2, 0, 3).reshape(2, 1, N_MEM, 4, DH)
    return (A(y[:SEQ]).reshape(1, SEQ, D_MODEL), A(y[SEQ:]).reshape(DEC_B, DEC_T, D_MODEL),
            A(r["o_dns_p"].transpose(1, 0, 2))[None, None], A(dc[0:1])[None], A(fc[:, 0:1]),
            A(k[:SEQ])[None], A(vp), A(mk), A(mv),
            A(r["o_dns_s"].transpose(2, 0, 1, 3))[None], A(dc[1:])[None], A(fc[:, 1:]),
            A(k[SEQ:]).reshape(DEC_B, DEC_T, SB_H, DH), A(r["o_vs"]).reshape(DEC_B, DEC_T, SB_H, DH))
```

```python
from contextlib import ExitStack

import numpy as np
import concourse.bass as bass
from concourse import mybir
from concourse.alu_op_type import AluOpType as ALU

ACT = mybir.ActivationFunctionType
F32 = mybir.dt.float32
F32R = mybir.dt.float32r
I32 = mybir.dt.int32
AX_X = mybir.AxisListType.X

P = 128
D_MODEL = 1024
KD = D_MODEL // P
SEQ = 512
DEC_B, DEC_T = 8, 8
NS = DEC_B * DEC_T
NT = SEQ + NS
HALF = NT // 2
DN_H = 6
QKV = 3 * DN_H
DN_TAPS, FF_TAPS = 4, 3
FF = 2816 // P
SB_H, DH = 12, 64
SBC = SB_H * DH // P
MEMC = 2
N_MEM = 256
PAGES = 8
NC = PAGES + 1
QC = 2 * DEC_T
ZW = PAGES * P + NS
SLOT = KD * P
THIRDS = [KD, KD, FF - 2 * KD]
NEG = -1.0e30
EPS = 1e-6
EXP_LN = "natural_log_exp_and_others"
NCH = SEQ // P
KVR = SBC * NT + NCH * SBC * P + SBC * P
ARENA = (QKV + DN_H + 2 * KD) * NT + KVR
CH = ARENA // NT
LEVELS = 7
LEVELS_S = 3


class Steps:

    def __init__(self, sem, names):
        self.sem, self.names, self.n, self.next = sem, names, len(names), 0

    def mark(self, name):
        assert self.names[self.next % self.n] == name, (name, self.names[self.next % self.n])
        self.next += 1
        return 1

    def at(self, name, turn=0):
        return (turn + 1) * self.n + self.names.index(name) + 1


def constants():
    s, t = np.arange(P)[:, None], np.arange(P)[None, :]
    same8 = s // 8 == t // 8
    f = lambda m: m.astype(np.float32)
    neg = lambda m: np.where(m, 0.0, NEG).astype(np.float32)
    levels = [f((s >> (l + 1) == t >> (l + 1)) & (((t >> l) & 1) == 1) & (((s >> l) & 1) == 0))
              for l in range(LEVELS)]
    common = np.concatenate([np.ones((P, P), np.float32), f(s == t)], 1)
    dn = np.concatenate(levels + [f(s <= t), neg(s <= t), f(same8 & (s <= t)), neg(same8 & (s <= t)), f(same8)], 1)
    b, col = np.arange(DEC_B)[None, :, None], np.arange(NS)[None, None, :]
    new = neg((col // DEC_T == b) & (col % DEC_T < s[:, :, None] % DEC_T)).reshape(P, -1)
    sb = np.concatenate([f(s >= t), neg(s < t), np.zeros((P, SEQ - P), np.float32), new], 1)
    return common, dn, sb


UNIT_PLAN = [("mem0", 4), ("mem1", 4), ("in_a", QKV + DN_H + MEMC), ("out_a", KD), ("up0", 2 * FF), ("down0", 3 * KD),
             ("v", SBC), ("k", SBC), ("in_b", SBC + MEMC), ("out_b", KD), ("up1", 2 * FF), ("down1", 3 * KD)]
UNITS = dict(UNIT_PLAN)
PLAIN = ("mem0", "mem1", "v")
XSPLIT = [("in_a", KD), ("out_a", KD), ("up0", KD), ("down0", FF), ("k", KD), ("in_b", KD), ("out_b", KD), ("up1", KD),
          ("down1", FF)]
UNIT0, SPLIT0, X0 = {}, {}, {}
_u = _s = 0
for _name, _n in UNIT_PLAN:
    UNIT0[_name], SPLIT0[_name] = _u, _s
    _u += _n
    _s += 0 if _name in PLAIN else _n
_x = 0
for _name, _n in XSPLIT:
    X0[_name] = _x
    _x += _n
AFTER = {b: a for (a, _), (b, _) in zip(UNIT_PLAN, UNIT_PLAN[1:])}
GAINS = ["mem0", "mem1", "mix_pre0", "mix_post0", "ffn_pre0", "ffn_post0", "kv", "mix_pre1", "mix_post1",
         "ffn_pre1", "ffn_post1"]


def build(nc, d):
    with ExitStack() as ctx:
        def sb(name, *shape, dt=F32):
            return ctx.enter_context(nc.sbuf_tensor(name, list(shape), dt))

        def sem(name):
            return ctx.enter_context(nc.semaphore(name))

        PB = ctx.enter_context(nc.psum_tensor("PB", [P, 8, 512], F32))
        hT = sb("hT", P, KD, NT)
        at = nc.sbuf_base
        arena = sb("arena", P, ARENA)
        BIG, MIX, XN = (QKV + DN_H), (QKV + DN_H) + KD, (QKV + DN_H) + 2 * KD
        big = arena[:, 0:BIG * NT]
        allv = arena[:, 0:CH * NT].rearrange("p (c n) -> p c n", n=NT)
        mixT, xnT = allv[:, BIG:MIX, :], allv[:, MIX:XN, :]
        ring = sb("ring", P, 2, SLOT)
        kvr = arena[:, XN * NT:ARENA]
        mb_at = nc.sbuf_base
        membuf = sb("membuf", P, 4 * SLOT)
        wparts = nc.alloc_sbuf_tensor_at("wparts", [P, 2, 2, SLOT], F32R, offset=mb_at)
        mkv = sb("mkv", P, 2, 2, 2, N_MEM)
        mq = sb("mq", P, MEMC, NT)
        qmblk = sb("qmblk", P, MEMC, DEC_B, 4 * DEC_T)
        qblk = sb("qblk", P, SBC, DEC_B, QC)
        common = sb("common", P, 2 * P)
        pconst = sb("pconst", P, 12 * P)
        gains = sb("gains", P, len(GAINS), KD)
        dnw = sb("dnw", P, QKV, DN_TAPS)
        ffw = sb("ffw", P, 2, 2 * FF, FF_TAPS + 1)
        cstate = sb("cstate", P, 2 * FF * DEC_B * 2)
        cnew = sb("cnew", P, 2 * FF * (DEC_B + 1) * 2)
        rstd = sb("rstd", P, NT)
        wba = sb("wba", P, KD, 2 * DN_H)
        tok = sb("tok", P, 9, NCH + 1, DN_H)
        small = sb("small", P, 48)
        sbias = sb("sbias", P, 2)
        biash = sb("biash", P, SB_H)
        pages = sb("pages", 1, DEC_B * PAGES, dt=I32)

        ones, ident = common[:, 0:P], common[:, P:2 * P]
        levelm = [pconst[:, l * P:(l + 1) * P] for l in range(LEVELS)]
        cumT, maskT, cum8, mask8, same8 = (pconst[:, (LEVELS + i) * P:(LEVELS + i + 1) * P] for i in range(5))
        suffix = pconst[:, 0:P]
        strict = pconst[:, P:P + SEQ]
        strict8 = pconst[:, P + SEQ:P + SEQ + DEC_B * NS]
        sq = allv[:, BIG - 2:BIG, :]
        A, R = slice(0, KD), slice(MIX, XN)
        M, U, Z = slice(BIG, MIX), slice(KD, 2 * KD), slice(2 * KD, BIG)
        PLACE = {"in_a": (Z, R, M), "out_a": (M, R, M), "k": (U, R, M), "in_b": (A, Z, A), "out_b": (M, R, M)}
        for layer in range(2):
            PLACE[f"up{layer}"] = (M, R, M)
            PLACE[f"down{layer}"] = (slice(0, FF), slice(FF, 2 * FF), slice(0, FF))
        parts = {(p.start, p.stop): nc.alloc_sbuf_tensor_at(f"parts{p.start}_{p.stop}", [P, p.stop - p.start, NT], F32R,
                                                            offset=at + 4 * NT * p.start)
                 for p in (A, R, M, Z, slice(0, FF), slice(FF, 2 * FF))}
        PLACE = {n: (allv[:, x, :], parts[h.start, h.stop], parts[lo.start, lo.stop]) for n, (x, h, lo) in PLACE.items()}
        outv = allv[:, A, :]
        downv = allv[:, 2 * FF:2 * FF + KD, :]
        epsc, alog, dtb, ogain = small[:, 0:1], small[:, 1:7], small[:, 7:13], small[:, 13:14]
        nalog, vmax, vsum, vrec = small[:, 14:20], small[:, 20:24], small[:, 24:28], small[:, 28:32]
        onec = small[:, 32:33]

        rawp = kvr[:, 0:2 * (SEQ + 3)].rearrange("p (a n) -> p a n", a=2)
        o = 2 * (SEQ + 3)
        raws = kvr[:, o:o + 2 * DEC_B * 11].rearrange("p (a b n) -> p a b n", a=2, b=DEC_B)
        o += 2 * DEC_B * 11
        acc = kvr[:, o:o + 2 * NT].rearrange("p (a n) -> p a n", a=2)
        o += 2 * NT
        gate = kvr[:, o:o + NT]
        kvT = kvr[:, 0:SBC * NT].rearrange("p (c n) -> p c n", c=SBC)
        o = SBC * NT
        vtok = kvr[:, o:o + NCH * SBC * P].rearrange("p (t n) -> p t n", t=NCH)
        o += NCH * SBC * P
        vnew64 = kvr[:, o:o + SBC * P]

        w_full = [sem("w_full0"), sem("w_full1")]
        hi_ready, lo_ready, xhi, xlo = sem("hi_ready"), sem("lo_ready"), sem("xhi"), sem("xlo")
        unit_done, evacuated = sem("unit_done"), sem("evacuated")
        mem_loaded, loaded, consts_b = sem("mem_loaded"), sem("loaded"), sem("consts_b")
        sq_ready, sq_summed, rstd_ready, normed = sem("sq_ready"), sem("sq_summed"), sem("rstd_ready"), sem("normed")
        dve_own, act_own, pool_own = sem("dve_own"), sem("act_own"), sem("pool_own")
        conv_done, tail_kept, gated = sem("conv_done"), sem("tail_kept"), sem("gated")
        y_ready, pads_ready, pads_zeroed = sem("y_ready"), sem("pads_ready"), sem("pads_zeroed")
        stored = sem("stored")
        state_in = sem("state_in")
        zeroed = sem("zeroed")
        tk_pe, tk_act, tk_dve = sem("tk_pe"), sem("tk_act"), sem("tk_dve")
        kv_stored, mkv_stored, queries = sem("kv_stored"), sem("mkv_stored"), sem("queries")
        mem_in = sem("mem_in")
        hid = sem("hid")
        n_stored = [0]

        def store(eng, out, src):
            eng.dma_start(out, src).then_inc(stored, 16)
            n_stored[0] += 16

        class Own:

            def __init__(self, s):
                self.sem, self.value = s, 0

            def inc(self):
                self.value += 1
                return 1

        dv, ac, po = Own(dve_own), Own(act_own), Own(pool_own)
        norm_no = [0]
        NORMS = ["mem", "mix_pre0", "mix_post0", "ffn_pre0", "ffn_post0", "kv", "mix_post1", "ffn_pre1", "ffn_post1"]
        APPLIES = ["mem0", "mem1", "mix_pre0", "mix_post0", "ffn_pre0", "ffn_post0", "kv", "mix_pre1",
                   "mix_post1", "ffn_pre1", "ffn_post1"]
        applied = {n: (i + 1) * KD for i, n in enumerate(APPLIES)}
        stat = {n: i + 1 for i, n in enumerate(NORMS)}

        xflat = xnT[:, :, :].rearrange("p c n -> p (c n)")
        HW = DN_H * P

        def tile6(i):
            if i < 6:
                a = xflat[:, i * HW:(i + 1) * HW]
            else:
                a = kvr[:, (i - 6) * HW:(i - 5) * HW]
            return a.rearrange("p (h n) -> p h n", h=DN_H)

        (qn, kn, eg, ktk, vb, wk, gamT, LT, Tm, TT, M1, BT, WTn, qdec, Sst) = (tile6(i) for i in range(15))
        sqq, sqk, rq, rk = Tm, TT, M1, BT
        ug, ib = vb, wk
        vst = WTn
        vnew, osq, ro = BT, M1, Tm
        bigv = big[:, :].rearrange("p (c n) -> p c n", n=NT)
        S8 = [membuf[:, i * 1024:(i + 1) * 1024].rearrange("p (b n) -> p b n", b=DEC_B) for i in range(2)]
        WTm = membuf[:, 2048:2048 + DEC_B * NS].rearrange("p (b n) -> p b n", b=DEC_B)
        WTd = membuf[:, 2048:2048 + DEC_B * (NS + DEC_T)].rearrange("p (b n) -> p b n", b=DEC_B)[:, :, 0:DEC_T]
        vmask = membuf[0:NS, 2624:2624 + 1024].rearrange("p (b n) -> p b n", b=DEC_B)
        G = range(2)

        def heads(a, g, rows=P, T=P):
            return a[0:rows, 3 * g:3 * g + 3, 0:T]

        def bank(b, rows=P, T=P):
            return PB[0:rows, b, 0:3 * P].rearrange("p (h n) -> p h n", h=3)[:, :, 0:T]

        def steps(prefix, table):
            return {e: Steps(sem(f"{prefix}_{e}"), names.split()) for e, names in table.items()}

        def dn_table(n, sample):
            pe = "ss0 ss1 gb0 gb1 bb0 bb1 kk0 kk1 kq0 kq1 kt0 kt1 vt0 vt1 t00 t01 "
            for l in range(1, n):
                pe += f"m{l}_0 m{l}_1 "
                if l < n - 1:
                    pe += f"x{l}_0 "
                pe += f"xt{l}_0 "
                if l < n - 1:
                    pe += f"x{l}_1 "
                pe += f"xt{l}_1 "
            pe += "wt0 wt1 "
            if sample:
                pe += " ".join(f"vn{h} o{h} sa{h} sb{h}" for h in range(DN_H)) + " "
            else:
                pe += "vn0 vn1 o0 o1 s0 s1 "
            pe += "os0 os1"
            act = "sq0 sk0 sq1 sk1 lq0 lk0 lq1 lk1 rq0 rk0 rq1 rk1 eg0 eg1 ga0 ga1 t00 t01 "
            act += " ".join(f"m{l}_{g}" for l in range(1, n) for g in G) + " "
            if sample:
                act += " ".join(f"wt{h} vn{h}" for h in range(DN_H)) + " "
            else:
                act += "wt0 wt1 vn0 vn1 "
            act += "os0 os1 ol0 ol1 or0 or1"
            dve = "qn0 kn0 qn1 kn1 ga00 ga01 ga02 ga10 ga11 ga12 lt0 at0 lb0 lt1 at1 lb1 tt00 tt01 kd0 wk0 vb0 kd1 wk1 vb1 "
            for l in range(1, n):
                for g in G:
                    if l < n - 1:
                        dve += f"x{l}_{g} "
                    dve += f"xt{l}_{g} "
            if sample:
                dve += " ".join(f"vm{h} sd{h} sn{h}" for h in range(DN_H)) + " "
            else:
                dve += "s0 s1 s2 s3 s4 s5 "
            dve += "on0 on1 oz0 oz1"
            pool = "ug ib vst " + " ".join(f"bt{l}" for l in range(n)) + " qd"
            return dict(pe=pe, act=act, dve=dve, pool=pool)

        dn_p = steps("dn", dn_table(LEVELS, False))
        dn_s = steps("dns", dn_table(LEVELS_S, True))
        s8_in, s8_out = [sem("s8_in0"), sem("s8_in1")], sem("s8_out")
        dnconv_out, ffconv_out = sem("dnconv_out"), sem("ffconv_out")
        MEM_LOADS, LOADS = 16 * 6, 16 * 9

        tB, tG, tGc, tGl, tNg, tEd, tBg, tA, tX = (tok[:, i, :, :] for i in range(9))

        block = ctx.enter_context(nc.Block())

        def pe_stats(pe, name, n=NT):
            j = stat[name] - 1
            if j:
                pe.wait_ge(rstd_ready, j)
            for k in range(KD):
                pe.wait_ge(sq_ready, j * KD + k + 1)
                for b, lo in enumerate(range(0, n, HALF)):
                    last = nc.tensor.matmul(PB[:, 4 + b, 0:min(n, HALF)], ones, sq[:, k % 2, lo:lo + min(n, HALF)],
                                            start=k == 0, stop=k == KD - 1)
                last.then_inc(sq_summed, 1)

        def act_stats(act, name, src, n=NT, after=None):
            j = stat[name] - 1
            for k in range(KD):
                if j * KD + k >= 2:
                    act.wait_ge(sq_summed, j * KD + k - 1)
                if after:
                    act.wait_ge(hid, HID[after] - KD + k + 1)
                nc.scalar.activation(sq[:, k % 2, 0:n], src[:, k, 0:n], ACT.Square).then_inc(sq_ready, 1)
            act.wait_ge(sq_summed, (j + 1) * KD)
            before = {"mem": 0, "mix_pre0": applied["mem1"], "mix_post1": applied["mix_pre1"]}
            if name != "mem":
                act.wait_ge(normed, before.get(name, applied[name] - KD))
            for b, lo in enumerate(range(0, n, HALF)):
                last = nc.scalar.activation(rstd[:, lo:lo + min(n, HALF)], PB[:, 4 + b, 0:min(n, HALF)], ACT.Ln, bias=epsc,
                                            scale=1.0 / D_MODEL)
            last.then_inc(ac.sem, ac.inc())
            act.wait_ge(ac.sem, ac.value)
            nc.scalar.activation(rstd[:, 0:n], rstd[:, 0:n], ACT.Exp, scale=-0.5).then_inc(rstd_ready, 1)

        def dve_apply(dve, stat_name, name, src, dst, n=NT):
            dve.wait_ge(rstd_ready, stat[stat_name])
            g = GAINS.index(name)
            for k in range(KD):
                last = nc.vector.scalar_tensor_tensor(out=dst[:, k, 0:n], in0=src[:, k, 0:n],
                                                      scalar=gains[:, g, k:k + 1], in1=rstd[:, 0:n],
                                                      op0=ALU.mult, op1=ALU.mult)
                last.then_inc(normed, 1)

        HID = {n: (i + 1) * KD for i, n in enumerate(["mix_post0", "ffn_post0", "mix_post1", "ffn_post1"])}

        def dve_residual(dve, name):
            src = downv if name.startswith("ffn") else outv
            dve.wait_ge(rstd_ready, stat[name])
            for k in range(KD + 1):
                if k < KD:
                    nc.vector.scalar_tensor_tensor(out=src[:, k, :], in0=src[:, k, :],
                                                   scalar=gains[:, GAINS.index(name), k:k + 1], in1=rstd[:, :],
                                                   op0=ALU.mult, op1=ALU.mult).then_inc(normed, 1)
                if k:
                    dve.wait_ge(normed, applied[name] - KD + k)
                    nc.vector.tensor_tensor(hT[:, k - 1, :], hT[:, k - 1, :], src[:, k - 1, :], ALU.add).then_inc(hid, 1)

        def act_hi(act, name, i, k, first=0):
            u = UNIT0[name] + first + k
            act.wait_ge(w_full[k], 16 * i + (u // 2 + 1) * 16)
            act.wait_ge(unit_done, 2 * i + (u - 1))
            nc.scalar.activation(wparts[:, 0, k, :], ring[:, k, :], ACT.Copy).then_inc(hi_ready, 1)

        def pool_lo(pool, name, i, k, first=0):
            pool.wait_ge(hi_ready, 2 * i + (SPLIT0[name] + first + k + 1))
            nc.gpsimd.tensor_tensor(wparts[:, 1, k, :], ring[:, k, :], wparts[:, 0, k, :].bitcast(F32), ALU.subtract).then_inc(lo_ready, 1)

        def pool_los(pool, name, first, count):
            with pool.Fori(0, count // 2) as i:
                for k in range(2):
                    pool_lo(pool, name, i, k, first)

        def act_xhi(act, name, ready):
            x, h, _ = PLACE[name]
            for c in range(dict(XSPLIT)[name]):
                ready(c)
                nc.scalar.activation(h[:, c, :], x[:, c, :], ACT.Copy).then_inc(xhi, 1)

        def normed_chunk(act, name):
            return lambda c: act.wait_ge(normed, applied[name] - KD + c + 1)

        def x_lo(eng, ops, name):
            x, h, lo = PLACE[name]
            for c in range(dict(XSPLIT)[name]):
                eng.wait_ge(xhi, X0[name] + c + 1)
                ops.tensor_tensor(lo[:, c, :], x[:, c, :], h[:, c, :].bitcast(F32), ALU.subtract).then_inc(xlo, 1)

        def products(pe, name, dst, k, c, block, start, stop):
            _, h, lo = PLACE[name]
            pe.wait_ge(xlo, X0[name] + c + 1)
            for part, x in ((0, h), (0, lo), (1, h)):
                for b in range(2):
                    last = nc.tensor.matmul(dst(b), wparts[:, part, k, block * P:(block + 1) * P],
                                            x[:, c, b * HALF:(b + 1) * HALF], start=start and part == 0 and x is h,
                                            stop=stop and part == 1)
            return last

        def pe_split(pe, name):
            u0, s0 = UNIT0[name], SPLIT0[name]
            with pe.Fori(0, UNITS[name] // 2) as i:
                for k in range(2):
                    pe.wait_ge(evacuated, 2 * i + (u0 + k - 1))
                    pe.wait_ge(lo_ready, 2 * i + (s0 + k + 1))
                    for c in range(KD):
                        last = products(pe, name, lambda b: PB[:, 2 * b + k, 0:HALF], k, c, c, c == 0, c == KD - 1)
                    last.then_inc(unit_done, 1)

        def pe_down(pe, name):
            u0, s0 = UNIT0[name], SPLIT0[name]
            pe.wait_ge(evacuated, u0)
            with pe.Fori(0, KD // 2) as i:
                for m in range(2):
                    for third, blocks in enumerate(THIRDS):
                        w = 3 * m + third
                        if third == 0:
                            pe.wait_ge(evacuated, 6 * i + (u0 + 3 * m - 3))
                        pe.wait_ge(lo_ready, 6 * i + (s0 + w + 1))
                        for j in range(blocks):
                            c = KD * third + j
                            last = products(pe, name, lambda b: PB[:, 2 * b + m, 0:HALF], w % 2, c, j, c == 0, c == FF - 1)
                        last.then_inc(unit_done, 1)

        def pe_plain(pe, name, x, n=NT, swap=False, count=2, first=0):
            u0 = UNIT0[name] + first

            def unit(i, k):
                if not (isinstance(i, int) and u0 + k < 2):
                    pe.wait_ge(evacuated, 2 * i + (u0 + k - 1))
                pe.wait_ge(w_full[k], i * 16 + (u0 // 2 + 1) * 16)
                if not swap:
                    for c in range(KD):
                        last = nc.tensor.matmul(PB[:, k, 0:n], ring[:, k, c * P:(c + 1) * P], x[:, c, 0:n],
                                                start=c == 0, stop=c == KD - 1)
                else:
                    for t in range(-(-n // P)):
                        m = min(P, n - t * P)
                        dst = PB[0:m, k, t * P:(t + 1) * P] if t < 4 else PB[0:m, 2 + k, 0:P]
                        for c in range(KD):
                            last = nc.tensor.matmul(dst, x[:, c, t * P:t * P + m], ring[:, k, c * P:(c + 1) * P],
                                                    start=c == 0, stop=c == KD - 1)
                last.then_inc(unit_done, 1)

            if count == 2:
                for k in range(2):
                    unit(0, k)
            else:
                with pe.Fori(0, count // 2) as i:
                    for k in range(2):
                        unit(i, k)

        def act_evac(act, name, place, count, first=0, scale=1.0, func=ACT.Copy, split=True, split_end=True):
            u0 = UNIT0[name] + first

            def turn(i, ahead):
                for k in range(2):
                    act.wait_ge(unit_done, 2 * i + (u0 + k + 1))
                    for dst, src in place(i, k):
                        last = nc.scalar.activation(dst, src, func, scale=scale)
                    last.then_inc(evacuated, 1)
                    if ahead:
                        act_hi(act, name, i, k, first + 2)
            whole = count // 2 if split == split_end else count // 2 - 1
            if whole > 1:
                with act.Fori(0, whole) as i:
                    turn(i, split)
            elif whole:
                turn(0, split)
            if whole < count // 2:
                turn(whole, split_end)

        def row(a, c, lo=0, hi=NT):
            if isinstance(c, int):
                return a[:, c, lo:hi]
            return a[:, bass.ds(c, 1), lo:hi].rearrange("p a n -> p (a n)")

        def chunked(a, first=0):
            return lambda i, k: [(row(a, 2 * i + (first + k), b * HALF, (b + 1) * HALF), PB[:, 2 * b + k, 0:HALF])
                                 for b in range(2)]

        def act_down(act, name):
            u0 = UNIT0[name]

            def turn(i, end):
                for m in range(2):
                    for third in range(3):
                        w = 3 * m + third
                        act.wait_ge(unit_done, 6 * i + (u0 + w + 1))
                        if third == 2:
                            for b in range(2):
                                last = nc.scalar.activation(row(downv, 2 * i + m, b * HALF, (b + 1) * HALF),
                                                            PB[:, 2 * b + m, 0:HALF], ACT.Copy)
                            last.then_inc(evacuated, 3)
                        if not (end and w >= 4):
                            act_hi(act, name, 3 * i, w % 2, w // 2 * 2 + 2)
            with act.Fori(0, KD // 2 - 1) as i:
                turn(i, False)
            turn(KD // 2 - 1, True)

        conv_base = {"in_a": 0, "up0": QKV, "up1": QKV + 2 * FF}

        def scalar_of(a, c, j):
            return a[:, bass.ds(c, 1), j:j + 1].rearrange("p a b -> p (a b)")

        def act_conv(act, name, taps, units):
            pad, u0, cb = taps - 1, UNIT0[name], conv_base[name]
            with act.Fori(0, units // 2) as i:
                for k in range(2):
                    act.wait_ge(unit_done, 2 * i + (u0 + k + 1))
                    act.wait_ge(conv_done, 2 * i + (cb + k + 1))
                    act.wait_ge(tail_kept, 2 * i + (cb + k + 1))
                    nc.scalar.activation(rawp[:, k, pad:pad + HALF], PB[:, k, 0:HALF], ACT.Copy)
                    nc.scalar.activation(rawp[:, k, pad + HALF:pad + SEQ], PB[:, 2 + k, 0:SEQ - HALF], ACT.Copy)
                    nc.scalar.activation(raws[:, k, :, pad:pad + DEC_T],
                                         PB[:, 2 + k, SEQ - HALF:HALF].rearrange("p (b t) -> p b t", b=DEC_B),
                                         ACT.Copy).then_inc(evacuated, 1)
                    act_hi(act, name, i, k, 2)
                    if name == "in_a":
                        act.wait_ge(conv_done, 2 * i + (cb + k + 3))
                        nc.scalar.activation(row(bigv, 2 * i + k), acc[:, k, :], ACT.Silu).then_inc(gated, 1)
                    elif k == 0:
                        act.wait_ge(conv_done, 2 * i + (cb + k + 3))
                        act.wait_ge(y_ready, i + (cb // 2 + 1))
                        nc.scalar.activation(gate, acc[:, k, :], ACT.Gelu_apprx_tanh,
                                             bias=scalar_of(ffw[:, int(name[-1]), :, :], 2 * i, FF_TAPS)).then_inc(gated, 1)
                    else:
                        act.sem_inc(gated, 1)

        def dve_conv(dve, name, taps, units):
            cb, u0 = conv_base[name], UNIT0[name]
            wts = dnw if name == "in_a" else ffw[:, int(name[-1]), :, :]
            base = dv.value
            with dve.Fori(0, units // 2) as i:
                own = 0
                for k in range(2):
                    dve.wait_ge(evacuated, 2 * i + (u0 + k + 1))
                    dve.wait_ge(pads_ready, 2 * i + (cb + k + 1))
                    dve.wait_ge(gated, 2 * i + (cb + k + 1))
                    dve.wait_ge(y_ready, i + (cb // 2 + 1))
                    for tap in range(taps):
                        w = scalar_of(wts, 2 * i + k, tap)
                        xp, xs = rawp[:, k, tap:tap + SEQ], raws[:, k, :, tap:tap + DEC_T]
                        ap_, as_ = acc[:, k, 0:SEQ], acc[:, k, SEQ:NT].rearrange("p (b t) -> p b t", b=DEC_B)
                        if tap == 0:
                            nc.vector.tensor_scalar(ap_, xp, w, None, ALU.mult)
                            last = nc.vector.tensor_scalar(as_, xs, w, None, ALU.mult)
                        else:
                            dve.wait_ge(dv.sem, i * (2 * (taps - 1)) + (base + own))
                            nc.vector.scalar_tensor_tensor(out=ap_, in0=xp, scalar=w, in1=ap_, op0=ALU.mult, op1=ALU.add)
                            last = nc.vector.scalar_tensor_tensor(out=as_, in0=xs, scalar=w, in1=as_, op0=ALU.mult,
                                                                  op1=ALU.add)
                        if tap < taps - 1:
                            last.then_inc(dv.sem, 1)
                            own += 1
                    last.then_inc(conv_done, 1)
                if name != "in_a":
                    dve.wait_ge(gated, 2 * i + (cb + 3))
                    dve.wait_ge(conv_done, 2 * i + (cb + 4))
                    nc.vector.scalar_tensor_tensor(out=row(bigv, i), in0=acc[:, 1, :],
                                                   scalar=scalar_of(ffw[:, int(name[-1]), :, :], 2 * i + 1, FF_TAPS),
                                                   in1=gate, op0=ALU.add, op1=ALU.mult).then_inc(y_ready, 1)
                else:
                    dve.sem_inc(y_ready, 1)
            dv.value = base + (units // 2) * (2 * (taps - 1))

        def pool_conv(pool, name, taps, units):
            pad, cb, u0 = taps - 1, conv_base[name], UNIT0[name]
            st = cstate[:, 0:units * DEC_B * pad].rearrange("p (c b n) -> p c b n", c=units, b=DEC_B)
            ne = cnew[:, 0:units * (DEC_B + 1) * pad].rearrange("p (c b n) -> p c b n", c=units, b=DEC_B + 1)
            with pool.Fori(0, units // 2) as i:
                for k in range(2):
                    pool.wait_ge(conv_done, 2 * i + (cb + k + 1))
                    pool.wait_ge(tail_kept, 2 * i + (cb + k + 1))
                    nc.gpsimd.tensor_copy(raws[:, k, :, 0:pad],
                                          st[:, bass.ds(2 * i + k, 1), :, :].rearrange("p a b n -> p (a b) n")).then_inc(pads_ready, 1)
                for k in range(2):
                    pool_lo(pool, name, i, k, 2)
                    pool.wait_ge(evacuated, 2 * i + (u0 + k + 1))
                    nc.gpsimd.tensor_copy(ne[:, bass.ds(2 * i + k, 1), 0:1, :].rearrange("p a b n -> p (a b n)"),
                                          rawp[:, k, SEQ:SEQ + pad])
                    nc.gpsimd.tensor_copy(ne[:, bass.ds(2 * i + k, 1), 1:, :].rearrange("p a b n -> p (a b) n"),
                                          raws[:, k, :, DEC_T:DEC_T + pad]).then_inc(tail_kept, 1)

        TILES = [(P, 0, NCH), (NS, NCH, NCH + 1)]
        baP = PB[:, 6, 0:(NCH + 1) * 2 * DN_H].rearrange("p (t x) -> p t x", x=2 * DN_H)

        def pe_tokens(pe):
            pe.wait_ge(normed, applied["mix_pre0"])
            for t in range(NCH + 1):
                m = min(P, NT - t * P)
                for c in range(KD):
                    last = nc.tensor.matmul(baP[0:m, t, :], PLACE["in_a"][0][:, c, t * P:t * P + m], wba[:, c, :],
                                            start=c == 0, stop=c == KD - 1)
            last.then_inc(tk_pe, 1)
            pe.wait_ge(tk_dve, 3)
            for i, (m, a, b) in enumerate(TILES):
                w = (b - a) * DN_H
                rhs = tG[0:m, a:b, :].rearrange("p t h -> p (t h)")
                nc.tensor.matmul(PB[0:m, 7, 32 * i:32 * i + w], (cumT, cum8)[i][0:m, 0:m], rhs, start=True, stop=True)
                last = nc.tensor.matmul(PB[0:m, 7, 64 + 32 * i:64 + 32 * i + w], (ones, same8)[i][0:m, 0:m], rhs,
                                        start=True, stop=True)
            last.then_inc(tk_pe, 1)

        def act_tokens(act):
            act.wait_ge(tk_pe, 1)
            for m, a, b in TILES:
                nc.scalar.activation(tB[0:m, a:b, :], baP[0:m, a:b, 0:DN_H], ACT.Exp, scale=-1.0)
            nc.scalar.activation(nalog, alog, ACT.Exp).then_inc(tk_act, 1)
            act.wait_ge(tk_dve, 2)
            for m, a, b in TILES:
                last = nc.scalar.activation(tX[0:m, a:b, :], tX[0:m, a:b, :], ACT.Exp)
            last.then_inc(tk_act, 1)
            act.wait_ge(tk_act, 2)
            for m, a, b in TILES:
                last = nc.scalar.activation(tX[0:m, a:b, :], tX[0:m, a:b, :], ACT.Ln, bias=onec[0:m, :])
            last.then_inc(tk_act, 1)
            act.wait_ge(tk_dve, 4)
            for m, a, b in TILES:
                nc.scalar.activation(tEd[0:m, a:b, :], tEd[0:m, a:b, :], ACT.Exp)
                last = nc.scalar.activation(tBg[0:m, a:b, :], tGc[0:m, a:b, :], ACT.Exp)
            last.then_inc(tk_act, 1)

        def dve_tokens(dve):
            def heads_of(x, m, n):
                return x[0:m, :].unsqueeze(1).to_broadcast([m, n, DN_H])
            dve.wait_ge(tk_act, 1)
            for m, a, b in TILES:
                nc.vector.tensor_scalar(tB[0:m, a:b, :], tB[0:m, a:b, :], 1.0, None, ALU.add)
                last = nc.vector.tensor_tensor(tA[0:m, a:b, :], baP[0:m, a:b, DN_H:], heads_of(dtb, m, b - a), ALU.add)
            last.then_inc(tk_dve, 1)
            dve.wait_ge(tk_dve, 1)
            for m, a, b in TILES:
                nc.vector.reciprocal(tB[0:m, a:b, :], tB[0:m, a:b, :])
                fl = lambda x: x[0:m, a:b, :].rearrange("p t h -> p (t h)")
                last = nc.vector.scalar_tensor_tensor(out=fl(tX), in0=fl(tA), scalar=-1.0, in1=fl(tA), op0=ALU.mult,
                                                      op1=ALU.min)
            last.then_inc(tk_dve, 1)
            dve.wait_ge(tk_act, 3)
            for m, a, b in TILES:
                fl = lambda x: x[0:m, a:b, :].rearrange("p t h -> p (t h)")
                last = nc.vector.scalar_tensor_tensor(out=fl(tX), in0=fl(tA), scalar=0.0, in1=fl(tX), op0=ALU.max,
                                                      op1=ALU.add)
            last.then_inc(dv.sem, dv.inc())
            dve.wait_ge(dv.sem, dv.value)
            for m, a, b in TILES:
                nc.vector.tensor_tensor(tG[0:m, a:b, :], tX[0:m, a:b, :], heads_of(nalog, m, b - a), ALU.mult)
                last = nc.vector.tensor_scalar(tX[0:m, a:b, :], tX[0:m, a:b, :], -1.0, None, ALU.mult)
            last.then_inc(dv.sem, dv.inc())
            dve.wait_ge(dv.sem, dv.value)
            for m, a, b in TILES:
                last = nc.vector.tensor_tensor(tG[0:m, a:b, :], tX[0:m, a:b, :], heads_of(nalog, m, b - a), ALU.mult)
            last.then_inc(tk_dve, 1)
            dve.wait_ge(tk_pe, 2)
            for i, (m, a, b) in enumerate(TILES):
                w = (b - a) * DN_H
                fl = lambda x: x[0:m, a:b, :].rearrange("p t h -> p (t h)")
                nc.vector.tensor_copy(fl(tGc), PB[0:m, 7, 32 * i:32 * i + w])
                last = nc.vector.tensor_scalar(fl(tNg), PB[0:m, 7, 32 * i:32 * i + w], -1.0, None, ALU.mult)
            last.then_inc(dv.sem, dv.inc())
            dve.wait_ge(dv.sem, dv.value)
            for i, (m, a, b) in enumerate(TILES):
                w = (b - a) * DN_H
                fl = lambda x: x[0:m, a:b, :].rearrange("p t h -> p (t h)")
                last = nc.vector.tensor_tensor(fl(tEd), PB[0:m, 7, 64 + 32 * i:64 + 32 * i + w], fl(tGc), ALU.subtract)
            last.then_inc(tk_dve, 1)
            dve.wait_ge(tk_act, 4)
            for m, a, b in TILES:
                last = nc.vector.tensor_tensor(tBg[0:m, a:b, :], tBg[0:m, a:b, :], tB[0:m, a:b, :], ALU.mult)
            last.then_inc(tk_dve, 1)

        def tile_of(i, rows_, c, h0, h1):
            if isinstance(c, int):
                return tok[0:rows_, i, c, h0:h1]
            return tok[0:rows_, i, bass.ds(c, 1), h0:h1].rearrange("p a h -> p (a h)")

        def dn_pe(pe, s, c, before, levels, T, sample):
            c = 0 if sample else c
            wait = lambda e, name: pe.wait_ge(s[e].sem, s[e].at(name, c))
            mark = s["pe"].mark
            S_ = s["pe"].sem
            bs, bt = before
            pe.wait_ge(bs["dve"].sem, bs["dve"].at("oz1", bt))
            pe.wait_ge(bs["act"].sem, bs["act"].at("or1", bt))
            for g in G:
                wait("act", f"sk{g}")
                nc.tensor.matmul(bank(g, P, T), ones, heads(sqq, g, P, T), start=True, stop=True)
                nc.tensor.matmul(bank(2 + g, P, T), ones, heads(sqk, g, P, T), start=True,
                                 stop=True).then_inc(S_, mark(f"ss{g}"))
            wait("pool", "ug")
            for g in G:
                nc.tensor.matmul(bank(4 + g, P, T), ones[0:T, :], heads(ug, g, T, T), start=True,
                                 stop=True).then_inc(S_, mark(f"gb{g}"))
            wait("pool", "ib")
            for g in G:
                nc.tensor.matmul(bank(6 + g, T, T), ones[0:T, 0:T], heads(ib, g, T, T), start=True,
                                 stop=True).then_inc(S_, mark(f"bb{g}"))
            for g in G:
                wait("dve", f"kn{g}")
                for h in range(3):
                    kh = kn[:, 3 * g + h, 0:T]
                    last = nc.tensor.matmul(bank(g, T, T)[:, h, :], kh, kh, start=True, stop=True)
                last.then_inc(S_, mark(f"kk{g}"))
            for g in G:
                for h in range(3):
                    last = nc.tensor.matmul(bank(2 + g, T, T)[:, h, :], kn[:, 3 * g + h, 0:T], qn[:, 3 * g + h, 0:T],
                                            start=True, stop=True)
                last.then_inc(S_, mark(f"kq{g}"))
            for g in G:
                wait("act", f"eg{g}")
                wait("dve", f"ga{g}2")
                for h in range(3):
                    last = nc.tensor.transpose(bank(4 + g, T, P)[:, h, :], kn[:, 3 * g + h, 0:T], ident)
                last.then_inc(S_, mark(f"kt{g}"))
            wait("pool", "vst")
            for g in G:
                wait("dve", f"lb{g}")
                for h in range(3):
                    last = nc.tensor.transpose(bank(6 + g, T, P)[:, h, :], vst[:, 3 * g + h, 0:T], ident)
                last.then_inc(S_, mark(f"vt{g}"))
            for g in G:
                wait("dve", f"tt0{g}")
                for h in range(3):
                    last = nc.tensor.transpose(bank(g, T, T)[:, h, :], TT[0:T, 3 * g + h, 0:T], ident[0:T, 0:T])
                last.then_inc(S_, mark(f"t0{g}"))
            for l in range(1, levels):
                wait("pool", f"bt{l}")
                for g in G:
                    if l == 1:
                        wait("act", f"t0{g}")
                    else:
                        wait("dve", f"x{l - 1}_{g}")
                    for h in range(3 * g, 3 * g + 3):
                        last = nc.tensor.matmul(bank(g, T, T)[:, h - 3 * g, :], BT[0:T, h, 0:T], Tm[0:T, h, 0:T],
                                                start=True, stop=True)
                    last.then_inc(S_, mark(f"m{l}_{g}"))
                for g in G:
                    wait("act", f"m{l}_{g}")
                    wait("dve", f"wk{g}" if l == 1 else f"xt{l - 1}_{g}")
                    if l < levels - 1:
                        for h in range(3 * g, 3 * g + 3):
                            last = nc.tensor.matmul(bank(2 + g, T, T)[:, h - 3 * g, :], TT[0:T, h, 0:T], M1[0:T, h, 0:T],
                                                    start=True, stop=True)
                        last.then_inc(S_, mark(f"x{l}_{g}"))
                    for h in range(3 * g, 3 * g + 3):
                        last = nc.tensor.matmul(bank(4 + g, T, T)[:, h - 3 * g, :], M1[0:T, h, 0:T], TT[0:T, h, 0:T],
                                                start=True, stop=True)
                    last.then_inc(S_, mark(f"xt{l}_{g}"))
            for g in G:
                wait("dve", f"xt{levels - 1}_{g}")
                for h in range(3):
                    last = nc.tensor.matmul(bank(g, P, T)[:, h, :], wk[0:T, 3 * g + h, :], TT[0:T, 3 * g + h, 0:T],
                                            start=True, stop=True)
                last.then_inc(S_, mark(f"wt{g}"))
            if not sample:
                for g in G:
                    wait("act", f"wt{g}")
                    for h in range(3 * g, 3 * g + 3):
                        dst = bank(2 + g)[:, h - 3 * g, :]
                        nc.tensor.matmul(dst, TT[:, h, :], vb[:, h, :], start=True, stop=False)
                        last = nc.tensor.matmul(dst, WTn[:, h, :], Sst[:, h, :], start=False, stop=True)
                    last.then_inc(S_, mark(f"vn{g}"))
                wait("pool", "qd")
                for g in G:
                    wait("act", f"vn{g}")
                    for h in range(3 * g, 3 * g + 3):
                        dst = bank(4 + g)[:, h - 3 * g, :]
                        nc.tensor.matmul(dst, Sst[:, h, :], qdec[:, h, :], start=True, stop=False)
                        last = nc.tensor.matmul(dst, vnew[:, h, :], gamT[:, h, :], start=False, stop=True)
                    last.then_inc(S_, mark(f"o{g}"))
                for g in G:
                    wait("dve", f"vb{g}")
                    for h in range(3 * g, 3 * g + 3):
                        last = nc.tensor.matmul(bank(6 + g)[:, h - 3 * g, :], ktk[:, h, :], vnew[:, h, :],
                                                start=True, stop=True)
                    last.then_inc(S_, mark(f"s{g}"))
            else:
                wait("pool", "qd")
                wait("dve", "vb1")
                for h in range(DN_H):
                    S8h = S8[h % 2]
                    wait("act", f"wt{h}")
                    pe.wait_ge(s8_in[h % 2], 16 * (h // 2 + 1))
                    if h >= 2:
                        wait("act", f"vn{h - 2}")
                    dst = PB[0:T, 2 + h % 2, 0:P]
                    nc.tensor.matmul(dst, TT[0:T, h, 0:T], vb[0:T, h, :], start=True, stop=False)
                    for b in range(DEC_B):
                        last = nc.tensor.matmul(dst, WTm[:, b, :], S8h[:, b, :], start=False, stop=b == DEC_B - 1)
                    last.then_inc(S_, mark(f"vn{h}"))
                    wait("act", f"vn{h}")
                    dst = bank(4 + h // 3, P, T)[:, h % 3, :]
                    nc.tensor.matmul(dst, vnew[0:T, h, :], gamT[0:T, h, 0:T], start=True, stop=False)
                    for b in range(DEC_B):
                        last = nc.tensor.matmul(dst[:, 8 * b:8 * b + 8], S8h[:, b, :], qdec[:, h, 8 * b:8 * b + 8],
                                                start=False, stop=b == DEC_B - 1)
                    last.then_inc(S_, mark(f"o{h}"))
                    wait("dve", f"vm{h}")
                    if h:
                        wait("dve", f"sn{h - 1}")
                    for half in range(2):
                        nc.tensor.matmul(PB[:, 6 + half, :], ktk[0:T, h, :],
                                         vmask[:, 4 * half:4 * half + 4, :].rearrange("p b n -> p (b n)"),
                                         start=True, stop=True).then_inc(S_, mark(f"s{'ab'[half]}{h}"))
            for g in G:
                wait("act", f"os{g}")
                nc.tensor.matmul(bank(g, P, T), ones, heads(osq, g, P, T), start=True, stop=True).then_inc(S_, mark(f"os{g}"))

        def dn_act(act, s, c, before, levels, T, sample, cols):
            c = 0 if sample else c
            wait = lambda e, name: act.wait_ge(s[e].sem, s[e].at(name, c))
            mark, S_ = s["act"].mark, s["act"].sem
            bs, bt = before
            act.wait_ge(bs["pe"].sem, bs["pe"].at("os1", bt))
            act.wait_ge(bs["dve"].sem, bs["dve"].at("on1", bt))
            for g in G:
                nc.scalar.activation(heads(sqq, g, P, T), cols(0, g), ACT.Square).then_inc(S_, mark(f"sq{g}"))
                nc.scalar.activation(heads(sqk, g, P, T), cols(1, g), ACT.Square).then_inc(S_, mark(f"sk{g}"))
            for g in G:
                wait("pe", f"ss{g}")
                nc.scalar.activation(heads(rq, g, P, T), bank(g, P, T), ACT.Ln, bias=epsc).then_inc(S_, mark(f"lq{g}"))
                nc.scalar.activation(heads(rk, g, P, T), bank(2 + g, P, T), ACT.Ln, bias=epsc).then_inc(S_, mark(f"lk{g}"))
            for g in G:
                wait("act", f"lk{g}")
                nc.scalar.activation(heads(rq, g, P, T), heads(rq, g, P, T), ACT.Exp, scale=-0.5).then_inc(S_, mark(f"rq{g}"))
                nc.scalar.activation(heads(rk, g, P, T), heads(rk, g, P, T), ACT.Exp, scale=-0.5).then_inc(S_, mark(f"rk{g}"))
            for g in G:
                wait("pe", f"gb{g}")
                nc.scalar.activation(heads(eg, g, P, T), bank(4 + g, P, T), ACT.Exp).then_inc(S_, mark(f"eg{g}"))
            for g in G:
                wait("dve", f"ga{g}2")
                nc.scalar.activation(heads(gamT, g, T, T), heads(gamT, g, T, T), ACT.Exp).then_inc(S_, mark(f"ga{g}"))
            for g in G:
                wait("pe", f"t0{g}")
                nc.scalar.activation(heads(Tm, g, T, T), bank(g, T, T), ACT.Copy).then_inc(S_, mark(f"t0{g}"))
            for l in range(1, levels):
                for g in G:
                    wait("pe", f"m{l}_{g}")
                    nc.scalar.activation(heads(M1, g, T, T), bank(g, T, T), ACT.Copy).then_inc(S_, mark(f"m{l}_{g}"))
            if not sample:
                for g in G:
                    wait("pe", f"wt{g}")
                    nc.scalar.activation(heads(WTn, g, P, T), bank(g, P, T), ACT.Copy, scale=-1.0).then_inc(S_, mark(f"wt{g}"))
                for g in G:
                    wait("pe", f"vn{g}")
                    nc.scalar.activation(heads(vnew, g, T, P), bank(2 + g, T, P), ACT.Copy).then_inc(S_, mark(f"vn{g}"))
            else:
                for h in range(DN_H):
                    wait("pe", "wt1" if h == 0 else f"vn{h - 1}")
                    nc.scalar.activation(WTd, bank(h // 3, P, T)[:, h % 3, :].rearrange("p (b t) -> p b t", b=DEC_B),
                                         ACT.Copy, scale=-1.0).then_inc(S_, mark(f"wt{h}"))
                    wait("pe", f"vn{h}")
                    nc.scalar.activation(vnew[0:T, h, :], PB[0:T, 2 + h % 2, 0:P], ACT.Copy).then_inc(S_, mark(f"vn{h}"))
            for g in G:
                wait("pe", f"o{3 * g + 2}" if sample else f"o{g}")
                nc.scalar.activation(heads(osq, g, P, T), bank(4 + g, P, T), ACT.Square).then_inc(S_, mark(f"os{g}"))
            for g in G:
                wait("pe", f"os{g}")
                nc.scalar.activation(heads(ro, g, P, T), bank(g, P, T), ACT.Ln, bias=epsc, scale=1.0 / P).then_inc(S_, mark(f"ol{g}"))
            for g in G:
                wait("act", f"ol{g}")
                nc.scalar.activation(heads(ro, g, P, T), heads(ro, g, P, T), ACT.Exp, scale=-0.5).then_inc(S_, mark(f"or{g}"))

        def dn_dve(dve, s, c, before, levels, T, sample, cols, out):
            ct, c = c, 0 if sample else c
            wait = lambda e, name: dve.wait_ge(s[e].sem, s[e].at(name, c))
            mark, S_ = s["dve"].mark, s["dve"].sem
            bs, bt = before
            dve.wait_ge(bs["pe"].sem, bs["pe"].at("os1", bt))
            mask = (mask8 if sample else maskT)[0:T, 0:T]
            for g in G:
                wait("act", f"rk{g}")
                nc.vector.scalar_tensor_tensor(out=heads(qn, g, P, T), in0=cols(0, g), scalar=float(P) ** -0.5,
                                               in1=heads(rq, g, P, T), op0=ALU.mult, op1=ALU.mult).then_inc(S_, mark(f"qn{g}"))
                nc.vector.tensor_tensor(heads(kn, g, P, T), cols(1, g), heads(rk, g, P, T), ALU.mult).then_inc(S_, mark(f"kn{g}"))
            for g in G:
                wait("act", f"eg{g}")
                for h in range(3):
                    nc.vector.scalar_tensor_tensor(out=gamT[0:T, 3 * g + h, 0:T], in0=bank(4 + g, T, T)[:, h, :],
                                                   scalar=tile_of(4, T, ct, 3 * g + h, 3 * g + h + 1),
                                                   in1=mask, op0=ALU.add, op1=ALU.add).then_inc(S_, mark(f"ga{g}{h}"))
            for g in G:
                wait("pe", f"kk{g}")
                wait("act", f"ga{g}")
                nc.vector.tensor_tensor(heads(LT, g, T, T), bank(g, T, T), heads(gamT, g, T, T), ALU.mult).then_inc(S_, mark(f"lt{g}"))
                wait("pe", f"kq{g}")
                wait("dve", f"lt{g}")
                nc.vector.tensor_tensor(heads(gamT, g, T, T), bank(2 + g, T, T), heads(gamT, g, T, T), ALU.mult).then_inc(S_, mark(f"at{g}"))
                wait("pe", f"bb{g}")
                nc.vector.tensor_tensor(heads(LT, g, T, T), heads(LT, g, T, T), bank(6 + g, T, T), ALU.mult).then_inc(S_, mark(f"lb{g}"))
            wait("pool", "bt0")
            for g in G:
                nc.vector.tensor_tensor(heads(TT, g, T, T), ident[0:T, 0:T].unsqueeze(1).to_broadcast([T, 3, T]),
                                        heads(BT, g, T, T), ALU.subtract).then_inc(S_, mark(f"tt0{g}"))

            def bc(i, g):
                return tile_of(i, T, ct, 3 * g, 3 * g + 3).unsqueeze(2).to_broadcast([T, 3, P])
            for g in G:
                wait("pe", f"kt{g}")
                nc.vector.tensor_tensor(heads(ktk, g, T, P), bank(4 + g, T, P), bc(5, g), ALU.mult).then_inc(S_, mark(f"kd{g}"))
                nc.vector.tensor_tensor(heads(wk, g, T, P), bank(4 + g, T, P), bc(6, g), ALU.mult).then_inc(S_, mark(f"wk{g}"))
                wait("pe", f"vt{g}")
                nc.vector.tensor_tensor(heads(vb, g, T, P), bank(6 + g, T, P), bc(0, g), ALU.mult).then_inc(S_, mark(f"vb{g}"))
            for l in range(1, levels):
                for g in G:
                    if l < levels - 1:
                        wait("pe", f"x{l}_{g}")
                        if l > 1:
                            wait("dve", f"x{l - 1}_{g}")
                        nc.vector.tensor_tensor(heads(Tm, g, T, T), heads(Tm, g, T, T), bank(2 + g, T, T),
                                                ALU.subtract).then_inc(S_, mark(f"x{l}_{g}"))
                    wait("pe", f"xt{l}_{g}")
                    wait("dve", f"tt0{g}" if l == 1 else f"xt{l - 1}_{g}")
                    nc.vector.tensor_tensor(heads(TT, g, T, T), heads(TT, g, T, T), bank(4 + g, T, T),
                                            ALU.subtract).then_inc(S_, mark(f"xt{l}_{g}"))
            if not sample:
                for h in range(DN_H):
                    g = h // 3
                    wait("pe", f"s{g}")
                    nc.vector.scalar_tensor_tensor(out=Sst[:, h, :], in0=Sst[:, h, :], scalar=eg[:, h, T - 1:T],
                                                   in1=bank(6 + g)[:, h % 3, :], op0=ALU.mult, op1=ALU.add).then_inc(S_, mark(f"s{h}"))
            else:
                for h in range(DN_H):
                    wait("act", f"vn{h}")
                    if h:
                        wait("pe", f"sb{h - 1}")
                    nc.vector.tensor_tensor(vmask, vnew[0:T, h, :].unsqueeze(1).to_broadcast([T, DEC_B, P]),
                                            same8[0:T, 0:T:DEC_T].unsqueeze(2).to_broadcast([T, DEC_B, P]),
                                            ALU.mult).then_inc(S_, mark(f"vm{h}"))
                    wait("pe", f"o{h}")
                    nc.vector.tensor_tensor(S8[h % 2], S8[h % 2],
                                            eg[:, h, DEC_T - 1:T:DEC_T].unsqueeze(2).to_broadcast([P, DEC_B, P]),
                                            ALU.mult).then_inc(S_, mark(f"sd{h}"))
                    wait("pe", f"sb{h}")
                    wait("dve", f"sd{h}")
                    nc.vector.tensor_tensor(S8[h % 2].rearrange("p b n -> p (b n)"), S8[h % 2].rearrange("p b n -> p (b n)"),
                                            PB[:, 6:8, :].rearrange("p a n -> p (a n)"), ALU.add).then_inc(S_, mark(f"sn{h}"))
            for g in G:
                wait("act", f"or{g}")
                nc.vector.scalar_tensor_tensor(out=heads(qn, g, P, T), in0=bank(4 + g, P, T), scalar=ogain,
                                               in1=heads(ro, g, P, T), op0=ALU.mult, op1=ALU.mult).then_inc(S_, mark(f"on{g}"))
            for g in G:
                wait("dve", f"on{g}")
                nc.vector.tensor_tensor(out(g), heads(qn, g, P, T), cols(3, g), ALU.mult).then_inc(S_, mark(f"oz{g}"))

        def dn_pool(pool, s, c, before, levels, T, sample, vcols):
            ct, c = c, 0 if sample else c
            wait = lambda e, name: pool.wait_ge(s[e].sem, s[e].at(name, c))
            mark, S_ = s["pool"].mark, s["pool"].sem
            bs, bt = before
            pool.wait_ge(bs["pe"].sem, bs["pe"].at("os1", bt))
            cum = (cum8 if sample else cumT)[0:T, 0:T]

            def six(m, i):
                return (m.unsqueeze(1).to_broadcast([T, DN_H, T]), tile_of(i, T, ct, 0, DN_H).unsqueeze(2).to_broadcast([T, DN_H, T]))
            a, b = six(cum, 1)
            nc.gpsimd.tensor_tensor(ug[0:T, :, 0:T], a, b, ALU.mult).then_inc(S_, mark("ug"))
            a, b = six(ident[0:T, 0:T], 0)
            nc.gpsimd.tensor_tensor(ib[0:T, :, 0:T], a, b, ALU.mult).then_inc(S_, mark("ib"))
            nc.gpsimd.tensor_copy(vst[:, :, 0:T], vcols).then_inc(S_, mark("vst"))
            for l in range(levels):
                if l == 0:
                    wait("dve", "lb1")
                elif l == 1:
                    wait("dve", "tt01")
                else:
                    wait("pe", f"m{l - 1}_1")
                nc.gpsimd.tensor_tensor(BT[0:T, :, 0:T], LT[0:T, :, 0:T],
                                        levelm[l][0:T, 0:T].unsqueeze(1).to_broadcast([T, DN_H, T]),
                                        ALU.mult).then_inc(S_, mark(f"bt{l}"))
            wait("act", "eg1")
            wait("dve", "qn1")
            nc.gpsimd.tensor_tensor(qdec[:, :, 0:T], qn[:, :, 0:T], eg[:, :, 0:T], ALU.mult).then_inc(S_, mark("qd"))

        def dn_cols(c):
            def f(part, g):
                r = bigv[:, DN_H * part + 3 * g:DN_H * part + 3 * g + 3, :]
                return r[:, :, SEQ:NT] if isinstance(c, int) else r[:, :, bass.ds(c * P, P)]
            return f

        def dn_run(eng, e, fn, extra):
            eng.sem_inc(dn_p[e].sem, dn_p[e].n)
            eng.sem_inc(dn_s[e].sem, dn_s[e].n)
            with eng.Fori(0, NCH) as c:
                fn(eng, dn_p, c, (dn_p, c - 1), LEVELS, P, False, *extra(c))
            fn(eng, dn_s, NCH, (dn_p, NCH - 1), LEVELS_S, NS, True, *extra(NCH))

        ma = {}
        for layer in range(2):
            ma[layer] = (steps(f"map{layer}", dict(
                pe="sc tr av", act="e0 e1 e2 e3 tc o", dve="mx rc pn", pool="st")),
                steps(f"mas{layer}", dict(pe="sc tr av", act="e0 tc o0 o1", dve="mx rc pn", pool="qz")))
        xs_ = xflat
        prob = xs_[:, 0:1024].rearrange("p (h m) -> p h m", h=4)
        probT = xs_[:, 1024:2048].rearrange("p (x t) -> p x t", x=8)
        mqst = xs_[:, 2048:2048 + MEMC * P].rearrange("p (c t) -> p c t", c=MEMC)
        km = membuf[:, 0:2048].rearrange("p (b c m) -> p b c m", b=4, c=MEMC)
        vm = membuf[:, 2048:4096].rearrange("p (b c f) -> p b c f", b=4, c=2)

        def pe_mem(pe, layer):
            sp_, ss_ = ma[layer]
            mk, mv = mkv[:, layer, 0, :, :], mkv[:, layer, 1, :, :]
            s = sp_
            pe.sem_inc(s["pe"].sem, s["pe"].n)
            with pe.Fori(0, NCH) as t:
                pe.wait_ge(s["pool"].sem, s["pool"].at("st", t))
                pe.wait_ge(s["act"].sem, s["act"].at("e3", t - 1))
                pe.wait_ge(s["dve"].sem, s["dve"].at("mx", t - 1))
                for x in range(4):
                    e, f = x // 2, x % 2
                    last = nc.tensor.matmul(PB[:, e, f * N_MEM:(f + 1) * N_MEM], mqst[64 * e:64 * e + 64, f, :],
                                            mk[64 * e:64 * e + 64, f, :], start=True, stop=True)
                last.then_inc(s["pe"].sem, s["pe"].mark("sc"))
                pe.wait_ge(s["dve"].sem, s["dve"].at("pn", t))
                pe.wait_ge(s["act"].sem, s["act"].at("tc", t - 1))
                for x in range(8):
                    last = nc.tensor.transpose(PB[:, 2 + x // 4, (x % 4) * P:(x % 4 + 1) * P],
                                               prob[:, x // 2, (x % 2) * P:(x % 2 + 1) * P], ident)
                last.then_inc(s["pe"].sem, s["pe"].mark("tr"))
                pe.wait_ge(s["act"].sem, s["act"].at("tc", t))
                pe.wait_ge(s["act"].sem, s["act"].at("o", t - 1))
                for x in range(4):
                    e, f = x // 2, x % 2
                    h = 2 * f + e
                    for mc in range(2):
                        last = nc.tensor.matmul(PB[64 * e:64 * e + 64, 6, f * P:(f + 1) * P],
                                                mv[:, mc, h * DH:(h + 1) * DH], probT[:, 2 * x + mc, :],
                                                start=mc == 0, stop=mc == 1)
                last.then_inc(s["pe"].sem, s["pe"].mark("av"))
            s = ss_
            pe.sem_inc(s["pe"].sem, s["pe"].n)
            pe.wait_ge(s["pool"].sem, s["pool"].at("qz"))
            for g in G:
                pe.wait_ge(sp_["act"].sem, sp_["act"].at("o", NCH - 1))
                pe.wait_ge(mem_in, 16 * 2 * (2 * layer + g + 1))
                if g:
                    pe.wait_ge(s["act"].sem, s["act"].at("o1", 0))
                for b in range(4):
                    for f in range(MEMC):
                        last = nc.tensor.matmul(PB[32 * b:32 * b + 32, 0, 0:N_MEM], qmblk[:, f, 4 * g + b, :],
                                                km[:, b, f, :], start=f == 0, stop=f == MEMC - 1)
                last.then_inc(s["pe"].sem, s["pe"].mark("sc"))
                pe.wait_ge(s["dve"].sem, s["dve"].at("pn", g))
                for x in range(2):
                    last = nc.tensor.transpose(PB[:, 2, x * P:(x + 1) * P], prob[:, 0, x * P:(x + 1) * P], ident)
                last.then_inc(s["pe"].sem, s["pe"].mark("tr"))
                pe.wait_ge(s["act"].sem, s["act"].at("tc", g))
                for b in range(4):
                    for f in range(MEMC):
                        for mc in range(2):
                            last = nc.tensor.matmul(PB[:, 6, (f * 4 + b) * QC:(f * 4 + b + 1) * QC],
                                                    vm[:, b, mc, f * P:(f + 1) * P],
                                                    probT[:, mc, 32 * b + QC * f:32 * b + QC * f + QC],
                                                    start=mc == 0, stop=mc == 1)
                last.then_inc(s["pe"].sem, s["pe"].mark("av"))

        def act_mem(act, layer):
            s, ss_ = ma[layer]
            act.sem_inc(s["act"].sem, s["act"].n)
            with act.Fori(0, NCH) as t:
                act.wait_ge(s["dve"].sem, s["dve"].at("mx", t))
                act.wait_ge(s["pe"].sem, s["pe"].at("tr", t - 1))
                for h in range(4):
                    nc.scalar.activation(prob[:, h, :], PB[:, h // 2, (h % 2) * N_MEM:(h % 2 + 1) * N_MEM], ACT.Exp,
                                         bias=vmax[:, h:h + 1], accum_out=vsum[:, h:h + 1]).then_inc(
                                             s["act"].sem, s["act"].mark(f"e{h}"))
                act.wait_ge(s["pe"].sem, s["pe"].at("tr", t))
                act.wait_ge(s["pe"].sem, s["pe"].at("av", t - 1))
                nc.scalar.activation(probT[:, :, :], PB[:, 2:4, :].rearrange("p a (x t) -> p (a x) t", t=P),
                                     ACT.Copy).then_inc(s["act"].sem, s["act"].mark("tc"))
                act.wait_ge(s["pe"].sem, s["pe"].at("av", t))
                nc.scalar.activation(mixT[:, 6:8, bass.ds(t * P, P)], PB[:, 6, 0:2 * P].rearrange("p (f t) -> p f t", f=2),
                                     ACT.Copy).then_inc(s["act"].sem, s["act"].mark("o"))
            s = ss_
            act.sem_inc(s["act"].sem, s["act"].n)
            for g in G:
                act.wait_ge(s["dve"].sem, s["dve"].at("mx", g))
                if g:
                    act.wait_ge(s["pe"].sem, s["pe"].at("av", g - 1))
                nc.scalar.activation(prob[:, 0, :], PB[:, 0, 0:N_MEM], ACT.Exp, bias=vmax[:, 0:1],
                                     accum_out=vsum[:, 0:1]).then_inc(s["act"].sem, s["act"].mark("e0"))
                act.wait_ge(s["pe"].sem, s["pe"].at("tr", g))
                nc.scalar.activation(probT[:, 0:2, :], PB[:, 2, 0:2 * P].rearrange("p (x t) -> p x t", x=2),
                                     ACT.Copy).then_inc(s["act"].sem, s["act"].mark("tc"))
                act.wait_ge(s["pe"].sem, s["pe"].at("av", g))
                for e in range(2):
                    for f in range(MEMC):
                        last = nc.scalar.activation(
                            mixT[64 * e:64 * e + 64, 6 + f, SEQ + 32 * g:SEQ + 32 * g + 32].rearrange("p (b t) -> p b t", b=4),
                            PB[64 * e:64 * e + 64, 6, f * 64:(f + 1) * 64].rearrange("p (b x) -> p b x", b=4)[:, :, 8 * e:8 * e + 8],
                            ACT.Copy)
                    last.then_inc(s["act"].sem, s["act"].mark(f"o{e}"))

        def dve_mem(dve, layer):
            s, ss_ = ma[layer]
            dve.sem_inc(s["dve"].sem, s["dve"].n)
            with dve.Fori(0, NCH) as t:
                dve.wait_ge(s["pe"].sem, s["pe"].at("sc", t))
                dve.wait_ge(s["act"].sem, s["act"].at("e3", t - 1))
                nc.vector.tensor_reduce(vmax, PB[:, 0:2, :].rearrange("p a (e m) -> p (a e) m", e=2), AX_X, ALU.max,
                                        negate=True).then_inc(s["dve"].sem, s["dve"].mark("mx"))
                dve.wait_ge(s["act"].sem, s["act"].at("e3", t))
                nc.vector.reciprocal(vrec, vsum).then_inc(s["dve"].sem, s["dve"].mark("rc"))
                dve.wait_ge(s["dve"].sem, s["dve"].at("rc", t))
                nc.vector.tensor_tensor(prob, prob, vrec.unsqueeze(2).to_broadcast([P, 4, N_MEM]),
                                        ALU.mult).then_inc(s["dve"].sem, s["dve"].mark("pn"))
            s = ss_
            dve.sem_inc(s["dve"].sem, s["dve"].n)
            for g in G:
                dve.wait_ge(s["pe"].sem, s["pe"].at("sc", g))
                nc.vector.tensor_reduce(vmax[:, 0:1], PB[:, 0, 0:N_MEM], AX_X, ALU.max, negate=True).then_inc(
                    s["dve"].sem, s["dve"].mark("mx"))
                dve.wait_ge(s["act"].sem, s["act"].at("e0", g))
                nc.vector.reciprocal(vrec[:, 0:1], vsum[:, 0:1]).then_inc(s["dve"].sem, s["dve"].mark("rc"))
                dve.wait_ge(s["dve"].sem, s["dve"].at("rc", g))
                nc.vector.tensor_scalar(prob[:, 0, :], prob[:, 0, :], vrec[:, 0:1], None, ALU.mult).then_inc(
                    s["dve"].sem, s["dve"].mark("pn"))

        def pool_mem(pool, layer):
            s, ss_ = ma[layer]
            pool.sem_inc(ss_["pool"].sem, ss_["pool"].n)
            for h in range(4):
                e = h % 2
                last = nc.gpsimd.tensor_copy(qmblk[64 * e:64 * e + 64, h // 2, :, 8 * h:8 * h + 8],
                                             mq[64 * e:64 * e + 64, h // 2, SEQ:NT].rearrange("p (b t) -> p b t", b=DEC_B))
            last.then_inc(ss_["pool"].sem, ss_["pool"].mark("qz"))
            pool.wait_ge(ss_["pool"].sem, ss_["pool"].at("qz"))
            pool.sem_inc(s["pool"].sem, s["pool"].n)
            with pool.Fori(0, NCH) as t:
                pool.wait_ge(s["pe"].sem, s["pe"].at("sc", t - 1))
                nc.gpsimd.tensor_copy(mqst, mq[:, :, bass.ds(t * P, P)]).then_inc(s["pool"].sem, s["pool"].mark("st"))

        spr = steps("sbp", dict(
            pe="z0 z1 c0 c1 v0 v1", act="e0 l0 e1 l1 w0 w1 o",
            dve="z0 m0 z1 m1 s0 s1 d0 d1", pool="st"))
        zoff = [0, 512, 896, 1152]
        sbs = xs_[:, 0:4608]
        zP = [sbs[:, 0:1280], sbs[:, 1280:2560]]
        sP = [sbs[:, 2560:3840], membuf[:, 0:1280]]
        qst, kst = membuf[:, 1280:1792], membuf[:, 1792:2304]
        vstP = membuf[:, 2304:2816].rearrange("p (j n) -> p j n", j=NCH)
        zb = [(0, 0), (1, 0), (2, 0), (2, 256)]

        def region(base, j):
            b, c = zb[j]
            return PB[:, base + b, c:c + SEQ - j * P]

        def zreg(a, j, lo=0):
            return a[:, zoff[j] + lo:zoff[j] + SEQ - j * P]

        def pe_sbp(pe):
            s = spr
            pe.sem_inc(s["pe"].sem, s["pe"].n)
            with pe.Fori(0, SBC) as i:
                pe.wait_ge(s["pool"].sem, s["pool"].at("st", i))
                for e in range(2):
                    pe.wait_ge(s["dve"].sem, s["dve"].at("z1", i - 1) if e == 0 else s["dve"].at("z0", i))
                    for j in range(NCH):
                        last = nc.tensor.matmul(region(0, j), kst[64 * e:64 * e + 64, j * P:(j + 1) * P],
                                                qst[64 * e:64 * e + 64, j * P:SEQ], start=True, stop=True)
                    last.then_inc(s["pe"].sem, s["pe"].mark(f"z{e}"))
                for e in range(2):
                    pe.wait_ge(s["dve"].sem, s["dve"].at(f"s{e}", i))
                    pe.wait_ge(s["dve"].sem, s["dve"].at("d1", i - 1) if e == 0 else s["dve"].at("d0", i))
                    for j in range(NCH):
                        r = region(3, j)
                        nc_after = list(range(j + 1, NCH))
                        last = nc.tensor.matmul(r, suffix, zreg(sP[e], j), start=True, stop=not nc_after)
                        for jj in nc_after:
                            last = nc.tensor.matmul(r[:, (jj - j) * P:], ones, zreg(sP[e], jj), start=False,
                                                    stop=jj == NCH - 1)
                    last.then_inc(s["pe"].sem, s["pe"].mark(f"c{e}"))
                for e in range(2):
                    pe.wait_ge(s["act"].sem, s["act"].at(f"w{e}", i))
                    pe.wait_ge(s["act"].sem, s["act"].at("o", i - 1))
                    for j in range(NCH):
                        last = nc.tensor.matmul(PB[64 * e:64 * e + 64, 6, j * P:SEQ], vstP[:, j, 64 * e:64 * e + 64],
                                                zreg(zP[e], j), start=j == 0, stop=j == NCH - 1)
                    last.then_inc(s["pe"].sem, s["pe"].mark(f"v{e}"))

        def act_sbp(act):
            s = spr
            act.sem_inc(s["act"].sem, s["act"].n)
            with act.Fori(0, SBC) as i:
                for e in range(2):
                    act.wait_ge(s["dve"].sem, s["dve"].at(f"m{e}", i))
                    nc.scalar.activation(sP[e], sP[e], ACT.Exp).then_inc(s["act"].sem, s["act"].mark(f"e{e}"))
                    act.wait_ge(s["act"].sem, s["act"].at(f"e{e}", i))
                    nc.scalar.activation(sP[e], sP[e], ACT.Ln, bias=onec).then_inc(s["act"].sem, s["act"].mark(f"l{e}"))
                for e in range(2):
                    act.wait_ge(s["dve"].sem, s["dve"].at(f"d{e}", i))
                    nc.scalar.activation(zP[e], zP[e], ACT.Exp).then_inc(s["act"].sem, s["act"].mark(f"w{e}"))
                act.wait_ge(s["pe"].sem, s["pe"].at("v1", i))
                nc.scalar.activation(mixT[:, bass.ds(i, 1), 0:SEQ].rearrange("p a n -> p (a n)"), PB[:, 6, :],
                                     ACT.Copy).then_inc(s["act"].sem, s["act"].mark("o"))

        def dve_sbp(dve):
            s = spr
            dve.sem_inc(s["dve"].sem, s["dve"].n)
            with dve.Fori(0, SBC) as i:
                for e in range(2):
                    dve.wait_ge(s["pe"].sem, s["pe"].at(f"z{e}", i))
                    dve.wait_ge(s["pe"].sem, s["pe"].at(f"v{e}", i - 1))
                    bias = biash[:, bass.ds(2 * i + e, 1)]
                    for j in range(NCH):
                        last = nc.vector.scalar_tensor_tensor(out=zreg(zP[e], j), in0=region(0, j), scalar=bias,
                                                              in1=strict[:, 0:SEQ - j * P], op0=ALU.add, op1=ALU.add)
                    last.then_inc(s["dve"].sem, s["dve"].mark(f"z{e}"))
                    dve.wait_ge(s["dve"].sem, s["dve"].at(f"z{e}", i))
                    nc.vector.tensor_scalar(sP[e], zP[e], 40.0, None, ALU.min).then_inc(s["dve"].sem, s["dve"].mark(f"m{e}"))
                for e in range(2):
                    dve.wait_ge(s["act"].sem, s["act"].at(f"l{e}", i))
                    nc.vector.tensor_tensor(sP[e], sP[e], zP[e], ALU.max).then_inc(s["dve"].sem, s["dve"].mark(f"s{e}"))
                for e in range(2):
                    dve.wait_ge(s["pe"].sem, s["pe"].at(f"c{e}", i))
                    for j in range(NCH):
                        last = nc.vector.tensor_tensor(zreg(zP[e], j), zreg(zP[e], j), region(3, j), ALU.subtract)
                    last.then_inc(s["dve"].sem, s["dve"].mark(f"d{e}"))

        def pool_sbp(pool):
            s = spr
            pool.sem_inc(s["pool"].sem, s["pool"].n)
            with pool.Fori(0, SBC) as i:
                pool.wait_ge(s["pe"].sem, s["pe"].at("v1", i - 1))
                nc.gpsimd.tensor_copy(qst, mixT[:, bass.ds(i, 1), 0:SEQ].rearrange("p a n -> p (a n)"))
                nc.gpsimd.tensor_copy(kst, kvT[:, bass.ds(i, 1), 0:SEQ].rearrange("p a n -> p (a n)"))
                nc.gpsimd.tensor_copy(vstP, vtok[:, :, bass.ds(i * P, P)]).then_inc(s["pool"].sem, s["pool"].mark("st"))

        ssm = steps("sbs", dict(pe="z " + " ".join(f"t{u}" for u in range(5)) + " v r",
                                act="z0 z1 e0 l0 e1 l1 w0 w1 t0 t2 t4 o m",
                                dve="k0 k1 m0 m1 s0 c0 s1 c1 d0 d1 t1 t3", pool="q"))
        kpage = big[:, 0:PAGES * SBC * P].rearrange("p (c n) -> p c n", c=PAGES)
        vpage = big[:, PAGES * SBC * P:2 * PAGES * SBC * P].rearrange("p (c n) -> p c n", c=PAGES)
        k_in, v_in = sem("k_in"), sem("v_in")
        SROWS = [P, P // 2]
        PAST = PAGES * P
        zS = [xflat[0:SROWS[w], w * ZW:(w + 1) * ZW] for w in range(2)]
        sS = [membuf[0:SROWS[w], w * ZW:(w + 1) * ZW] for w in range(2)]
        TW = P + P // 2
        wT = membuf[:, 0:NC * TW].rearrange("p (c r) -> p c r", c=NC)
        oS = big[:, 12288:12288 + 2 * P]
        qs = big[:, 12288 + 2 * P:12288 + 2 * P + SBC * 32].rearrange("p (f x) -> p f x", f=SBC)
        SETS = [(0, 4), (4, SBC)]
        units_of = [(0, 2), (2, 4), (4, 6), (6, PAGES - 1), (PAGES - 1, NC)]

        def pe_sbs(pe):
            s = ssm
            pe.sem_inc(s["pe"].sem, s["pe"].n)
            with pe.Fori(0, DEC_B) as b:
                pe.wait_ge(k_in, b * (16 * PAGES) + 16 * PAGES)
                pe.wait_ge(s["pool"].sem, s["pool"].at("q", b))
                pe.wait_ge(s["act"].sem, s["act"].at("z1", b - 1))
                for w, (f0, f1) in enumerate(SETS):
                    for span in range(3):
                        for f in range(f0, f1):
                            g = f - f0
                            if span < 2:
                                rhs = kpage[:, 4 * span:4 * span + 4, f * P:(f + 1) * P]
                                dst = PB[32 * g:32 * g + 32, 2 * w + span, :].rearrange("p (c n) -> p c n", c=4)
                            else:
                                rhs, dst = kvT[:, f, SEQ:NT], PB[32 * g:32 * g + 32, 4, w * NS:(w + 1) * NS]
                            last = nc.tensor.matmul(dst, qs[:, f, :], rhs, start=True, stop=True)
                last.then_inc(s["pe"].sem, s["pe"].mark("z"))
                for u, (c0, c1) in enumerate(units_of):
                    if u >= 2:
                        e = "act" if u % 2 == 0 else "dve"
                        pe.wait_ge(s[e].sem, s[e].at(f"t{u - 2}", b))
                    elif u == 0:
                        pe.wait_ge(s["act"].sem, s["act"].at("w1", b))
                    for c in range(c0, c1):
                        n = P if c < PAGES else NS
                        for w in range(2):
                            o = (c - c0) * TW + w * P
                            last = nc.tensor.transpose(PB[0:n, 5 + u % 2, o:o + SROWS[w]], zS[w][:, c * P:c * P + n],
                                                       ident[0:SROWS[w], 0:SROWS[w]])
                    last.then_inc(s["pe"].sem, s["pe"].mark(f"t{u}"))
                pe.wait_ge(s["act"].sem, s["act"].at("t4", b))
                pe.wait_ge(s["dve"].sem, s["dve"].at("t3", b))
                pe.wait_ge(v_in, b * (16 * PAGES) + 16 * PAGES)
                for w, (f0, f1) in enumerate(SETS):
                    for c in range(NC):
                        for f in range(f0, f1):
                            g, n = f - f0, P if c < PAGES else NS
                            v = vpage[:, c, f * P:(f + 1) * P] if c < PAGES else vnew64[0:NS, f * P:(f + 1) * P]
                            last = nc.tensor.matmul(PB[32 * g:32 * g + 32, 7, w * P:(w + 1) * P],
                                                    wT[0:n, c, w * P + 32 * g:w * P + 32 * g + 32], v,
                                                    start=c == 0, stop=c == NC - 1)
                last.then_inc(s["pe"].sem, s["pe"].mark("v"))
                pe.wait_ge(s["act"].sem, s["act"].at("o", b))
                for w in range(2):
                    last = nc.tensor.transpose(PB[:, 5, w * P:w * P + SROWS[w]], oS[0:SROWS[w], w * P:(w + 1) * P],
                                               ident[0:SROWS[w], 0:SROWS[w]])
                last.then_inc(s["pe"].sem, s["pe"].mark("r"))

        def sbs_t_evac(u):
            c0, c1 = units_of[u]
            parts = [(c0, c1, P)] if c1 < NC else [(c0, PAGES, P), (PAGES, NC, NS)]
            return [(wT[0:n, a:b, :], PB[0:n, 5 + u % 2, (a - c0) * TW:(b - c0) * TW].rearrange("p (c r) -> p c r", c=b - a))
                    for a, b, n in parts]

        def act_sbs(act):
            s = ssm
            S_, mark = s["act"].sem, s["act"].mark
            act.sem_inc(S_, s["act"].n)
            with act.Fori(0, DEC_B) as b:
                wait = lambda e, name, it=b: act.wait_ge(s[e].sem, s[e].at(name, it))
                wait("pe", "z")
                for w in range(2):
                    r = SROWS[w]
                    nc.scalar.activation(zS[w][:, 0:PAST], PB[0:r, 2 * w:2 * w + 2, :].rearrange("p a n -> p (a n)"),
                                         ACT.Identity, bias=sbias[0:r, w:w + 1])
                    nc.scalar.activation(zS[w][:, PAST:ZW], PB[0:r, 4, w * NS:(w + 1) * NS], ACT.Identity,
                                         bias=sbias[0:r, w:w + 1]).then_inc(S_, mark(f"z{w}"))
                for w in range(2):
                    wait("dve", f"m{w}")
                    nc.scalar.activation(sS[w], sS[w], ACT.Exp).then_inc(S_, mark(f"e{w}"))
                    wait("act", f"e{w}")
                    nc.scalar.activation(sS[w], sS[w], ACT.Ln, bias=onec[0:SROWS[w], :]).then_inc(S_, mark(f"l{w}"))
                for w in range(2):
                    wait("dve", f"d{w}")
                    nc.scalar.activation(zS[w], zS[w], ACT.Exp).then_inc(S_, mark(f"w{w}"))
                for u in range(0, len(units_of), 2):
                    wait("pe", f"t{u}")
                    wait("dve", "d1")
                    for dst, src in sbs_t_evac(u):
                        last = nc.scalar.activation(dst, src, ACT.Copy)
                    last.then_inc(S_, mark(f"t{u}"))
                wait("pe", "v")
                nc.scalar.activation(oS[:, 0:P], PB[:, 7, 0:P], ACT.Copy)
                nc.scalar.activation(oS[0:P // 2, P:2 * P], PB[0:P // 2, 7, P:2 * P], ACT.Copy).then_inc(S_, mark("o"))
                wait("pe", "r")
                for e in range(2):
                    for w, (f0, f1) in enumerate(SETS):
                        src = PB[64 * e:64 * e + 64, 5, w * P:w * P + SROWS[w]].rearrange("p (g x) -> p g x", x=32)
                        last = nc.scalar.activation(mixT[64 * e:64 * e + 64, f0:f1, bass.ds(b * DEC_T + SEQ, DEC_T)],
                                                    src[:, :, 8 * e:8 * e + 8], ACT.Copy)
                last.then_inc(S_, mark("m"))

        def dve_sbs(dve):
            s = ssm
            S_, mark = s["dve"].sem, s["dve"].mark
            dve.sem_inc(S_, s["dve"].n)
            with dve.Fori(0, DEC_B) as b:
                wait = lambda e, name, it=b: dve.wait_ge(s[e].sem, s[e].at(name, it))
                for w in range(2):
                    wait("act", f"z{w}")
                    nc.vector.tensor_tensor(zS[w][:, PAST:ZW], zS[w][:, PAST:ZW],
                                            strict8[0:SROWS[w], bass.ds(b * NS, NS)], ALU.add).then_inc(S_, mark(f"k{w}"))
                wait("pe", "v", b - 1)
                for w in range(2):
                    wait("dve", f"k{w}")
                    nc.vector.tensor_scalar(sS[w], zS[w], 40.0, None, ALU.min).then_inc(S_, mark(f"m{w}"))
                for w in range(2):
                    wait("act", f"l{w}")
                    nc.vector.tensor_tensor(sS[w], sS[w], zS[w], ALU.max).then_inc(S_, mark(f"s{w}"))
                    wait("dve", f"s{w}")
                    back = sS[w][:, ::-1]
                    nc.vector.tensor_tensor_scan(back, back, back, 0.0, ALU.add, ALU.max).then_inc(S_, mark(f"c{w}"))
                for w in range(2):
                    wait("dve", f"c{w}")
                    nc.vector.tensor_tensor(zS[w], zS[w], sS[w], ALU.subtract).then_inc(S_, mark(f"d{w}"))
                for u in (1, 3):
                    wait("pe", f"t{u}")
                    for dst, src in sbs_t_evac(u):
                        last = nc.vector.tensor_copy(dst, src)
                    last.then_inc(S_, mark(f"t{u}"))

        def pool_sbs(pool):
            s = ssm
            pool.sem_inc(s["pool"].sem, s["pool"].n)
            with pool.Fori(0, DEC_B) as b:
                pool.wait_ge(s["pe"].sem, s["pe"].at("z", b - 1))
                nc.gpsimd.tensor_copy(qs[:, :, 0:QC], qblk[:, :, bass.ds(b, 1), :].rearrange("p f a x -> p f (a x)")).then_inc(
                    s["pool"].sem, s["pool"].mark("q"))

        def mem_place(layer, which):
            if which == 0:
                return lambda i, k: [(mkv[:, layer, 0, k, :], PB[:, k, 0:N_MEM])]
            return lambda i, k: [(mkv[:, layer, 1, :, k * P:(k + 1) * P], PB[:, k, 0:N_MEM].rearrange("p (t n) -> p t n", t=2))]

        def v_place(i, k):
            col = bass.ds((2 * i + k) * P, P)
            return [(vtok[:, :, col], PB[:, k, :].rearrange("p (t n) -> p t n", t=NCH)),
                    (vnew64[0:NS, col], PB[0:NS, 2 + k, 0:P])]

        @block.tensor
        def _(pe):
            mn = [bigv[:, 0:KD, :], bigv[:, KD:2 * KD, :]]
            pe.wait_ge(mem_loaded, MEM_LOADS)
            pe_stats(pe, "mem", N_MEM)
            pe_stats(pe, "mix_pre0")
            for layer in range(2):
                pe.wait_ge(normed, applied[f"mem{layer}"])
                pe_plain(pe, f"mem{layer}", mn[layer], N_MEM)
                pe_plain(pe, f"mem{layer}", mn[layer], N_MEM, swap=True, first=2)
            pe.wait_ge(loaded, LOADS)
            pe_tokens(pe)
            pe_split(pe, "in_a")
            dn_run(pe, "pe", dn_pe, lambda c: ())
            pe_mem(pe, 0)
            pe_split(pe, "out_a")
            pe_stats(pe, "mix_post0")
            for layer in range(2):
                if layer:
                    pe_stats(pe, "kv")
                    pe.wait_ge(normed, applied["kv"])
                    pe_plain(pe, "v", PLACE["k"][0], swap=True, count=SBC)
                    pe_split(pe, "k")
                    pe_split(pe, "in_b")
                    pe_mem(pe, 1)
                    pe.wait_ge(consts_b, 16)
                    pe_sbp(pe)
                    pe_sbs(pe)
                    pe_split(pe, "out_b")
                    pe_stats(pe, "mix_post1")
                pe_stats(pe, f"ffn_pre{layer}")
                pe_split(pe, f"up{layer}")
                pe_down(pe, f"down{layer}")
                pe_stats(pe, f"ffn_post{layer}")

        @block.scalar
        def _(act):
            act.sem_inc(gated, 2)
            nc.scalar.preload_act_table_set(EXP_LN)
            act.wait_ge(zeroed, 1)
            act.wait_ge(mem_loaded, MEM_LOADS)
            act_stats(act, "mem", mixT, N_MEM)
            act.wait_ge(loaded, LOADS)
            act_stats(act, "mix_pre0", hT)
            for layer in range(2):
                for which in range(2):
                    act_evac(act, f"mem{layer}", mem_place(layer, which), 2, first=2 * which, split=False, split_end=False)
                if layer == 0:
                    act_xhi(act, "in_a", normed_chunk(act, "mix_pre0"))
            for k in range(2):
                act_hi(act, "in_a", 0, k)
            act_tokens(act)
            act_conv(act, "in_a", DN_TAPS, QKV)
            act_evac(act, "in_a", chunked(bigv, QKV), DN_H, first=QKV, func=ACT.Silu)
            act_evac(act, "in_a", chunked(mq), 2, first=QKV + DN_H, scale=DH ** -0.5, split=False, split_end=False)
            act.wait_ge(conv_done, 2 + QKV)
            act.wait_ge(tail_kept, 2 + QKV)
            nc.scalar.preload_act_table_set(EXP_LN)
            dn_run(act, "act", dn_act, lambda c: (dn_cols(c),))
            act_mem(act, 0)
            for k in range(2):
                act_hi(act, "out_a", 0, k)
            act.wait_ge(dn_s["dve"].sem, dn_s["dve"].at("oz1"))
            act.wait_ge(ma[0][1]["act"].sem, ma[0][1]["act"].at("o1", 1))
            act_xhi(act, "out_a", lambda c: None)
            act_evac(act, "out_a", chunked(outv), KD)
            act_stats(act, "mix_post0", outv)
            for layer in range(2):
                if layer:
                    act_stats(act, "kv", hT, after="ffn_post0")
                    act_xhi(act, "k", normed_chunk(act, "kv"))
                    act_xhi(act, "in_b", normed_chunk(act, "mix_pre1"))
                    act_evac(act, "v", v_place, SBC, split=False)
                    act_evac(act, "k", chunked(kvT), SBC)
                    act_evac(act, "in_b", chunked(mixT), SBC, scale=DH ** -0.5)
                    act_evac(act, "in_b", chunked(mq), 2, first=SBC, scale=DH ** -0.5, split=False, split_end=False)
                    act_mem(act, 1)
                    act_sbp(act)
                    act_sbs(act)
                    for k in range(2):
                        act_hi(act, "out_b", 0, k)
                    act.wait_ge(ssm["act"].sem, ssm["act"].at("m", DEC_B - 1))
                    act_xhi(act, "out_b", lambda c: None)
                    act_evac(act, "out_b", chunked(outv), KD)
                    act_stats(act, "mix_post1", outv)
                    act.wait_ge(kv_stored, 16 * 3)
                act_stats(act, f"ffn_pre{layer}", hT, after=f"mix_post{layer}")
                act_xhi(act, f"up{layer}", normed_chunk(act, f"ffn_pre{layer}"))
                act.wait_ge(pads_zeroed, layer + 2)
                act_conv(act, f"up{layer}", FF_TAPS, 2 * FF)

                def gated_chunk(c):
                    y0 = 1 + conv_base[f"up{layer}"] // 2
                    act.wait_ge(y_ready, y0 + (c + 1 if c < 18 else FF))
                    if c == 2:
                        act.wait_ge(unit_done, UNIT0[f"down{layer}"])
                    if c == 18:
                        act.wait_ge(tail_kept, 2 + conv_base[f"up{layer}"] + 2 * FF)
                act_xhi(act, f"down{layer}", gated_chunk)
                act_down(act, f"down{layer}")
                nc.scalar.preload_act_table_set(EXP_LN)
                act_stats(act, f"ffn_post{layer}", downv)

        @block.vector
        def _(dve):
            dve.sem_inc(conv_done, 2)
            dve.sem_inc(y_ready, 1)
            mn = [bigv[:, 0:KD, :], bigv[:, KD:2 * KD, :]]
            dve.wait_ge(mem_loaded, MEM_LOADS)
            for layer in range(2):
                dve_apply(dve, "mem", f"mem{layer}", mixT, mn[layer], N_MEM)
            dve.wait_ge(loaded, LOADS)
            dve_apply(dve, "mix_pre0", "mix_pre0", hT, PLACE["in_a"][0])
            dve_tokens(dve)
            dve.wait_ge(pads_zeroed, 1)
            dve_conv(dve, "in_a", DN_TAPS, QKV)
            dve.wait_ge(evacuated, UNIT0["in_a"] + UNITS["in_a"])
            dve.wait_ge(gated, 2 + QKV)
            dn_run(dve, "dve", dn_dve, lambda c: (dn_cols(c), (lambda g: mixT[:, 3 * g:3 * g + 3, SEQ:NT]) if isinstance(c, int)
                                                 else (lambda g: mixT[:, 3 * g:3 * g + 3, bass.ds(c * P, P)])))
            dve_mem(dve, 0)
            dve_residual(dve, "mix_post0")
            for layer in range(2):
                if layer:
                    dve_apply(dve, "kv", "kv", hT, PLACE["k"][0])
                    dve_apply(dve, "kv", "mix_pre1", hT, PLACE["in_b"][0])
                    dve_mem(dve, 1)
                    dve.wait_ge(consts_b, 16)
                    dve_sbp(dve)
                    dve_sbs(dve)
                    dve_residual(dve, "mix_post1")
                dve_apply(dve, f"ffn_pre{layer}", f"ffn_pre{layer}", hT, PLACE[f"up{layer}"][0])
                dve_conv(dve, f"up{layer}", FF_TAPS, 2 * FF)
                x_lo(dve, nc.vector, f"down{layer}")
                dve_residual(dve, f"ffn_post{layer}")

        @block.gpsimd
        def _(pool):
            nc.gpsimd.memset(qmblk[:, :, :, :], 0.0)
            nc.gpsimd.memset(qblk[:, :, :, :], 0.0)
            nc.gpsimd.memset(epsc, EPS)
            nc.gpsimd.memset(onec, 1.0).then_inc(zeroed, 1)
            nc.gpsimd.memset(rawp[:, :, 0:DN_TAPS - 1], 0.0).then_inc(pads_zeroed, 1)
            pool.sem_inc(tail_kept, 2)
            pool.wait_ge(loaded, LOADS)
            pool.wait_ge(zeroed, 1)
            x_lo(pool, nc.gpsimd, "in_a")
            for k in range(2):
                pool_lo(pool, "in_a", 0, k)
            pool_conv(pool, "in_a", DN_TAPS, QKV)
            pool_los(pool, "in_a", QKV + 2, UNITS["in_a"] - QKV - 2)
            pool.wait_ge(tail_kept, 2 + QKV)
            pool.dma_start(d["o_dnconv"], cnew[:, 0:QKV * (DEC_B + 1) * (DN_TAPS - 1)]).then_inc(dnconv_out, 16)
            pool.wait_ge(pads_ready, QKV)
            pool.dma_start(cstate[:, :], d["ff_state"][0]).then_inc(state_in, 16)
            pool.wait_ge(rstd_ready, stat["mix_pre0"])
            pool.wait_ge(unit_done, UNIT0["out_a"])
            pool.wait_ge(gated, 2 + QKV)
            pool.wait_ge(conv_done, 2 + QKV)
            nc.gpsimd.memset(Sst[:, :, :], 0.0)
            nc.gpsimd.memset(WTm[:, :, :], 0.0).then_inc(po.sem, po.inc())
            pool.wait_ge(po.sem, po.value)
            dn_run(pool, "pool", dn_pool, lambda c: ((bigv[:, 2 * DN_H:3 * DN_H, SEQ:NT] if isinstance(c, int)
                                                      else bigv[:, 2 * DN_H:3 * DN_H, bass.ds(c * P, P)]),))
            pool.wait_ge(dn_s["dve"].sem, dn_s["dve"].at("oz1"))
            pool_mem(pool, 0)
            for k in range(2):
                pool_lo(pool, "out_a", 0, k)
            x_lo(pool, nc.gpsimd, "out_a")
            pool_los(pool, "out_a", 2, KD)
            for layer in range(2):
                if layer:
                    pool.dma_start(pconst[:, 0:P + SEQ + DEC_B * NS], d["c_sb"]).then_inc(consts_b, 16)
                    x_lo(pool, nc.gpsimd, "k")
                    x_lo(pool, nc.gpsimd, "in_b")
                    pool_los(pool, "k", 0, SBC + UNITS["in_b"])
                    pool.wait_ge(evacuated, UNIT0["in_b"] + UNITS["in_b"])
                    for e in range(2):
                        last = nc.gpsimd.tensor_copy(
                            qblk[64 * e:64 * e + 64, :, :, 8 * e:8 * e + 8],
                            mixT[64 * e:64 * e + 64, 0:SBC, SEQ:NT].rearrange("p c (b t) -> p c b t", b=DEC_B))
                    last.then_inc(po.sem, po.inc())
                    pool.wait_ge(po.sem, po.value)
                    pool_mem(pool, 1)
                    pool.wait_ge(ma[1][1]["pe"].sem, ma[1][1]["pe"].at("av", 1))
                    nc.gpsimd.memset(qs[:, :, QC:32], 0.0)
                    pool_sbp(pool)
                    pool_sbs(pool)
                    for k in range(2):
                        pool_lo(pool, "out_b", 0, k)
                    x_lo(pool, nc.gpsimd, "out_b")
                    pool_los(pool, "out_b", 2, KD)
                pool.wait_ge(hid, HID[f"mix_post{layer}"])
                if layer:
                    pool.wait_ge(kv_stored, 16 * 3)
                nc.gpsimd.memset(rawp[:, :, 0:FF_TAPS - 1], 0.0).then_inc(pads_zeroed, 1)
                pool.wait_ge(state_in, 16 * (layer + 1))
                pool.wait_ge(dnconv_out if layer == 0 else ffconv_out, 16)
                x_lo(pool, nc.gpsimd, f"up{layer}")
                pool_conv(pool, f"up{layer}", FF_TAPS, 2 * FF)
                pool.wait_ge(tail_kept, 2 + QKV + 2 * FF * (layer + 1))
                pool.dma_start(d["o_ffconv"][layer], cnew[:, :]).then_inc(ffconv_out, 16)
                if not layer:
                    pool.wait_ge(pads_ready, QKV + 2 * FF)
                    pool.dma_start(cstate[:, :], d["ff_state"][1]).then_inc(state_in, 16)
                pool_los(pool, f"down{layer}", 2, UNITS[f"down{layer}"] - 2)
            pool.wait_ge(ffconv_out, 32)

        @block.sync
        def _(sp):
            def load(s, dst, src):
                sp.dma_start(dst, src).then_inc(s, 16)
            load(mem_loaded, mixT[:, :, 0:N_MEM], d["memT"].rearrange("c p n -> p c n"))
            load(mem_loaded, common[:, :], d["c_common"])
            load(mem_loaded, gains[:, :, :], d["gains"])
            load(mem_loaded, alog, d["a_log"].to_broadcast([P, DN_H]))
            load(mem_loaded, dtb, d["dt_bias"].to_broadcast([P, DN_H]))
            load(mem_loaded, ogain, d["o_gain"])

            def feed(name, first=0, count=None):
                n = UNITS[name] if count is None else count

                def pair(i, first):
                    u0, s0 = UNIT0[name] + first, SPLIT0[name] + first
                    own = first > 0 or not isinstance(i, int)
                    for k in range(2):
                        if (name if own else AFTER.get(name)) in PLAIN:
                            sp.wait_ge(unit_done, 2 * i + (u0 + k - 1))
                        elif u0:
                            sp.wait_ge(lo_ready, 2 * i + (s0 + k - 1))
                        r = 2 * i + (u0 + k)
                        src = d["w8"][r] if isinstance(r, int) else d["w8"][bass.ds(r, 1), :, :].rearrange("a p n -> p (a n)")
                        sp.dma_start(ring[:, k, :], src).then_inc(w_full[k], 16)
                if first == 0:
                    pair(0, 0)
                    first, n = 2, n - 2
                if n == 2:
                    pair(0, first)
                elif n:
                    with sp.Fori(0, n // 2) as i:
                        pair(i, first)

            feed("mem0", count=2)
            load(loaded, hT[:, :, :], d["xT"].rearrange("c p n -> p c n"))
            load(loaded, pconst[:, :], d["c_dn"])
            load(loaded, dnw[:, :, :], d["dn_w"])
            load(loaded, cstate[:, 0:QKV * DEC_B * (DN_TAPS - 1)], d["dn_state"])
            load(loaded, wba[:, :, :], d["w_ba"])
            load(loaded, biash[:, :], d["sb_bias"].to_broadcast([P, SB_H]))
            load(loaded, ffw[:, :, :, :], d["ff_w"])
            load(loaded, pages[:, :], d["page_table"])
            load(loaded, sbias[:, :], d["sb_bias_rows"])
            feed("mem0", first=2, count=2)
            feed("mem1")
            feed("in_a")
            sp.wait_ge(evacuated, UNIT0["in_a"])
            store(sp, d["o_mkv"], mkv[:, :, :, :, :].rearrange("p l w c n -> p (l w c n)"))
            feed("out_a", count=2)
            sp.wait_ge(unit_done, UNIT0["out_a"])
            for h in range(2):
                sp.dma_start(S8[h], d["state_dn"][h]).then_inc(s8_in[h], 16)
            sp.wait_ge(dn_p["dve"].sem, dn_p["dve"].at("s5", NCH - 1))
            store(sp, d["o_dns_p"], Sst[:, :, :])
            for h in range(DN_H):
                sp.wait_ge(dn_s["dve"].sem, dn_s["dve"].at(f"sn{h}"))
                sp.dma_start(d["o_dns_s"][h], S8[h % 2]).then_inc(s8_out, 16)
                if h + 2 < DN_H:
                    sp.wait_ge(s8_out, 16 * (h + 1))
                    sp.dma_start(S8[h % 2], d["state_dn"][h + 2]).then_inc(s8_in[h % 2], 16)
            sp.wait_ge(s8_out, 16 * DN_H)

            def mem_load(layer, g):
                sp.dma_start(km[:, :, :, :].rearrange("p b c m -> p b (c m)"),
                             d["cache_mk"][layer, 4 * g:4 * g + 4].rearrange("b p n -> p b n")).then_inc(mem_in, 16)
                sp.dma_start(vm[:, :, :, :].rearrange("p b c m -> p b (c m)"),
                             d["cache_mv"][layer, 4 * g:4 * g + 4].rearrange("b p n -> p b n")).then_inc(mem_in, 16)
            mem_load(0, 0)
            sp.wait_ge(ma[0][1]["pe"].sem, ma[0][1]["pe"].at("av", 0))
            mem_load(0, 1)
            feed("out_a", first=2, count=KD - 2)
            feed("up0")
            feed("down0")
            feed("v")
            feed("k")

            def page_loads(b):
                at = [sp.value_load(pages[0:1, b * PAGES + j:b * PAGES + j + 1] if isinstance(b, int)
                                    else pages[0:1, bass.ds(b * PAGES + j, 1)],
                                    min_val=0, max_val=d["kpages"].shape[0] - 1) for j in range(PAGES)]
                for cache, dst, s, used in (("kpages", kpage, k_in, "z"), ("vpages", vpage, v_in, "v")):
                    if not isinstance(b, int):
                        sp.wait_ge(ssm["pe"].sem, ssm["pe"].at(used, b - 1))
                    for j in range(PAGES):
                        sp.dma_start(dst[:, j, :], d[cache][bass.ds(at[j], 1), :, :].rearrange("a p n -> p (a n)")).then_inc(s, 16)
            feed("in_b")
            sp.wait_ge(evacuated, UNIT0["in_b"])
            sp.dma_start(d["o_k"], kvT[:, :, :]).then_inc(kv_stored, 16)
            sp.dma_start(d["o_v"], vtok[:, :, :]).then_inc(kv_stored, 16)
            sp.dma_start(d["o_vs"], vnew64[0:NS, :]).then_inc(kv_stored, 16)
            sp.wait_ge(unit_done, UNIT0["out_b"])
            mem_load(1, 0)
            feed("out_b", count=2)
            page_loads(0)
            sp.wait_ge(ma[1][1]["pe"].sem, ma[1][1]["pe"].at("av", 0))
            mem_load(1, 1)
            with sp.Fori(1, DEC_B) as b:
                page_loads(b)
            feed("out_b", first=2, count=KD - 2)
            feed("up1")
            feed("down1")
            sp.wait_ge(hid, HID["ffn_post1"])
            store(sp, d["o_y"].rearrange("c p n -> p c n"), hT[:, :, :])
            sp.wait_ge(kv_stored, 16 * 3)
            sp.wait_ge(stored, n_stored[0])


def kernel(**inputs):
    from concourse.bacc import Bacc
    from concourse.bass_utils import run_bass_kernel_spmd

    x = {n: np.asarray(a) for n, a in inputs.items()}
    A = np.ascontiguousarray
    nu = D_MODEL // P

    def units(w):
        return w.reshape(nu, P, -1, P).transpose(2, 1, 0, 3).reshape(-1, P, nu * P)

    def down_units(w):
        r = w.reshape(FF, P, nu, P).transpose(2, 1, 0, 3)
        r = np.concatenate([r, np.zeros((nu, P, 3 * KD - FF, P), w.dtype)], 2)
        return r.reshape(nu, P, 3, KD * P).transpose(0, 2, 1, 3).reshape(-1, P, KD * P)

    def halves(a):
        return a.reshape(a.shape[:-1] + (2, FF, P)).swapaxes(-3, -2).reshape(a.shape)

    def chunks(a):
        r = a.reshape(a.shape[:-1] + (-1, P))
        return np.moveaxis(r, (-1, -2), (0, 1))

    def bias_rows(b):
        r = np.zeros((2, 4, 4, DEC_T), b.dtype)
        r[:, :, 0:2] = np.concatenate([b, np.zeros(4, b.dtype)]).reshape(2, 4, 2)[..., None]
        return A(r.reshape(2, P).T)

    zcols = (QKV + DN_H) * P
    wa, wb = x["w_in_a"][0], x["w_in_b"][0]
    parts = {"mem0": x["w_mem_kv"][0], "mem1": x["w_mem_kv"][1],
             "in_a": np.concatenate([wa[:, :zcols], wa[:, zcols + 2 * DN_H:]], 1), "out_a": x["w_out_a"][0],
             "up0": halves(x["ffn_w_up"][0]), "v": x["w_kv"][:, SBC * P:], "k": x["w_kv"][:, :SBC * P], "in_b": wb, "out_b": x["w_out_b"][0],
             "up1": halves(x["ffn_w_up"][1])}
    c_common, c_dn, c_sb = constants()
    n_phys = x["cache_k"].shape[0]
    gains_ = np.concatenate([x["mem_norm"], x["norm_mix_pre"], x["norm_mix_post"], x["norm_ffn_pre"], x["norm_ffn_post"],
                             x["kv_norm"][None]], 0)
    order = [0, 1, 2, 4, 6, 8, 10, 3, 5, 7, 9]
    arrays = {
        "xT": A(np.concatenate([x["x_prompt"].reshape(SEQ, -1), x["x_sample"].reshape(NS, -1)]).T.reshape(nu, P, NT)),
        "memT": A(x["mem_prompt"][0].T.reshape(nu, P, N_MEM)),
        "w8": np.concatenate([units(parts[n]) if n in parts else down_units(x["ffn_w_down"][int(n[-1])])
                              for n, _ in UNIT_PLAN]),
        "w_ba": A(wa[:, zcols:zcols + 2 * DN_H].reshape(nu, P, 2 * DN_H).transpose(1, 0, 2)),
        "gains": A(chunks(gains_[order]).transpose(0, 2, 1)),
        "a_log": A(x["dn_a_log"].reshape(1, DN_H)), "dt_bias": A(x["dn_dt_bias"].reshape(1, DN_H)),
        "o_gain": A(x["dn_o_gain"].reshape(P, 1)), "sb_bias": A(x["sb_bias"].reshape(1, SB_H)),
        "sb_bias_rows": bias_rows(x["sb_bias"].reshape(SB_H)),
        "dn_w": A(chunks(x["dn_conv_w"][0])),
        "ff_w": A(chunks(halves(np.concatenate([x["ffn_conv_w"], x["ffn_conv_b"][:, None]], 1))).transpose(0, 2, 1, 3)),
        "dn_state": A(chunks(x["state_dn_conv"][0]).reshape(P, -1)),
        "ff_state": A(np.stack([chunks(halves(x["state_ffn_conv"][l])).reshape(P, -1) for l in range(2)])),
        "state_dn": A(x["state_dn"][0].transpose(1, 2, 0, 3)),
        "cache_mk": A(x["cache_mem_k"].reshape(2, DEC_B, N_MEM, MEMC, P).transpose(0, 1, 4, 3, 2).reshape(2, DEC_B, P, -1)),
        "cache_mv": A(x["cache_mem_v"].reshape(2, DEC_B, 2, P, MEMC * P).transpose(0, 1, 3, 2, 4).reshape(2, DEC_B, P, -1)),
        "kpages": A(x["cache_k"].reshape(n_phys, P, SBC, P).transpose(0, 3, 2, 1).reshape(n_phys, P, SBC * P)),
        "vpages": A(x["cache_v"].reshape(n_phys, P, SBC * P)),
        "page_table": A(x["page_table"].reshape(1, -1)),
        "c_common": c_common, "c_dn": c_dn, "c_sb": c_sb,
    }
    outs = {"o_y": (nu, P, NT), "o_dns_p": (P, DN_H, P), "o_dns_s": (DN_H, P, DEC_B, P),
            "o_dnconv": (P, QKV * (DEC_B + 1) * (DN_TAPS - 1)), "o_ffconv": (2, P, 2 * FF * (DEC_B + 1) * (FF_TAPS - 1)),
            "o_k": (P, SBC, NT), "o_v": (P, NCH, SBC * P), "o_vs": (NS, SBC * P), "o_mkv": (P, 2 * 2 * 2 * N_MEM)}
    nc = Bacc("TRN2", target_bir_lowering=False, num_devices=1)
    d = {n: nc.dram_tensor(f"in_{n}", a.shape, mybir.dt.from_np(a.dtype), kind="ExternalInput").ap() for n, a in arrays.items()}
    d.update({n: nc.dram_tensor(n, s, F32, kind="ExternalOutput").ap() for n, s in outs.items()})
    build(nc, d)
    r = run_bass_kernel_spmd(nc, [{f"in_{n}": a for n, a in arrays.items()}], core_ids=[0]).results[0]

    y = r["o_y"].transpose(2, 0, 1).reshape(NT, D_MODEL)

    def unchunk(a, n, taps):
        a = a.reshape(P, n, DEC_B + 1, taps).transpose(2, 3, 1, 0)
        return a.reshape(DEC_B + 1, taps, n * P)

    def unhalve(a):
        return a.reshape(a.shape[:-1] + (FF, 2, P)).swapaxes(-3, -2).reshape(a.shape)

    dc = unchunk(r["o_dnconv"], QKV, DN_TAPS - 1)
    fc = np.stack([unhalve(unchunk(r["o_ffconv"][l], 2 * FF, FF_TAPS - 1)) for l in range(2)])
    k = r["o_k"].transpose(2, 1, 0).reshape(NT, SB_H, DH)
    vp = r["o_v"].transpose(1, 0, 2).reshape(1, SEQ, SB_H, DH)
    mkv = r["o_mkv"].reshape(P, 2, 2, 2, N_MEM)
    mk = mkv[:, :, 0].transpose(1, 3, 2, 0).reshape(2, 1, N_MEM, 4, DH)
    mv = mkv[:, :, 1].transpose(1, 2, 0, 3).reshape(2, 1, N_MEM, 4, DH)
    return (A(y[:SEQ]).reshape(1, SEQ, D_MODEL), A(y[SEQ:]).reshape(DEC_B, DEC_T, D_MODEL),
            A(r["o_dns_p"].transpose(1, 0, 2))[None, None], A(dc[0:1])[None], A(fc[:, 0:1]),
            A(k[:SEQ])[None], A(vp), A(mk), A(mv),
            A(r["o_dns_s"].transpose(2, 0, 1, 3))[None], A(dc[1:])[None], A(fc[:, 1:]),
            A(k[SEQ:]).reshape(DEC_B, DEC_T, SB_H, DH), A(r["o_vs"]).reshape(DEC_B, DEC_T, SB_H, DH))
```

```python
from contextlib import ExitStack

import numpy as np
import concourse.bass as bass
from concourse import mybir
from concourse.alu_op_type import AluOpType as ALU

ACT = mybir.ActivationFunctionType
F32 = mybir.dt.float32
F32R = mybir.dt.float32r
I32 = mybir.dt.int32
AX_X = mybir.AxisListType.X

P = 128
D_MODEL = 1024
KD = D_MODEL // P
SEQ = 512
DEC_B, DEC_T = 8, 8
NS = DEC_B * DEC_T
NT = SEQ + NS
HALF = NT // 2
DN_H = 6
QKV = 3 * DN_H
DN_TAPS, FF_TAPS = 4, 3
FF = 2816 // P
SB_H, DH = 12, 64
SBC = SB_H * DH // P
MEMC = 2
N_MEM = 256
PAGES = 8
NC = PAGES + 1
QC = 2 * DEC_T
ZW = PAGES * P + NS
SLOT = KD * P
THIRDS = [KD, KD, FF - 2 * KD]
NEG = -1.0e30
EPS = 1e-6
EXP_LN = "natural_log_exp_and_others"
SILU, GELU = "silu_and_others", "gelu_apprx_tanh_and_others"
NCH = SEQ // P
KVR = SBC * NT + NCH * SBC * P + SBC * P
ARENA = (QKV + DN_H + 2 * KD) * NT + KVR
CH = ARENA // NT
LEVELS = 7
LEVELS_S = 3


class Steps:

    def __init__(self, sem, names):
        self.sem, self.names, self.n, self.next = sem, names, len(names), 0

    def mark(self, name):
        assert self.names[self.next % self.n] == name, (name, self.names[self.next % self.n])
        self.next += 1
        return 1

    def at(self, name, turn=0):
        return (turn + 1) * self.n + self.names.index(name) + 1

    def skip(self, eng, turn, *names):
        for name in names:
            self.mark(name)
        before = self.at(names[0], turn) - 1
        if before:
            eng.wait_ge(self.sem, before)
        eng.sem_inc(self.sem, len(names))


def constants():
    s, t = np.arange(P)[:, None], np.arange(P)[None, :]
    same8 = s // 8 == t // 8
    f = lambda m: m.astype(np.float32)
    neg = lambda m: np.where(m, 0.0, NEG).astype(np.float32)
    levels = [f((s >> (l + 1) == t >> (l + 1)) & (((t >> l) & 1) == 1) & (((s >> l) & 1) == 0))
              for l in range(LEVELS)]
    common = np.concatenate([np.ones((P, P), np.float32), f(s == t)], 1)
    dn = np.concatenate(levels + [f(s <= t), neg(s <= t), f(same8 & (s <= t)), neg(same8 & (s <= t)), f(same8)], 1)
    b, col = np.arange(DEC_B)[None, :, None], np.arange(NS)[None, None, :]
    new = neg((col // DEC_T == b) & (col % DEC_T < s[:, :, None] % DEC_T)).reshape(P, -1)
    sb = np.concatenate([f(s >= t), neg(s < t), np.zeros((P, SEQ - P), np.float32), new], 1)
    return common, dn, sb


UNIT_PLAN = [("mem0", 4), ("mem1", 4), ("in_a", QKV + DN_H + MEMC), ("out_a", KD), ("up0", 2 * FF), ("down0", 3 * KD),
             ("k", SBC), ("v", SBC), ("in_b", SBC + MEMC), ("out_b", KD), ("up1", 2 * FF), ("down1", 3 * KD)]
UNITS = dict(UNIT_PLAN)
PLAIN = ("mem0", "mem1")
XSPLIT = [("in_a", KD), ("out_a", KD), ("up0", KD), ("down0", FF), ("k", KD), ("in_b", KD), ("out_b", KD), ("up1", KD),
          ("down1", FF)]
SHARED = ("in_a", "up0", "k", "up1")
EARLY = 5
UNIT0, SPLIT0, X0 = {}, {}, {}
_u = _s = 0
for _name, _n in UNIT_PLAN:
    UNIT0[_name], SPLIT0[_name] = _u, _s
    _u += _n
    _s += 0 if _name in PLAIN else _n
_x = 0
for _name, _n in XSPLIT:
    X0[_name] = _x
    _x += _n
XLO0, _x = {}, 0
for _name, _n in XSPLIT:
    XLO0[_name] = _x
    _x += EARLY if _name in SHARED else _n
X0["v"], XLO0["v"] = X0["k"], XLO0["k"]
AFTER = {b: a for (a, _), (b, _) in zip(UNIT_PLAN, UNIT_PLAN[1:])}
GAINS = ["mem0", "mem1", "mix_pre0", "mix_post0", "ffn_pre0", "ffn_post0", "kv", "mix_pre1", "mix_post1",
         "ffn_pre1", "ffn_post1"]


def build(nc, d):
    with ExitStack() as ctx:
        def sb(name, *shape, dt=F32):
            return ctx.enter_context(nc.sbuf_tensor(name, list(shape), dt))

        def sem(name):
            return ctx.enter_context(nc.semaphore(name))

        PB = ctx.enter_context(nc.psum_tensor("PB", [P, 8, 512], F32))
        hT = sb("hT", P, KD, NT)
        at = nc.sbuf_base
        arena = sb("arena", P, ARENA)
        BIG, MIX, XN = (QKV + DN_H), (QKV + DN_H) + KD, (QKV + DN_H) + 2 * KD
        big = arena[:, 0:BIG * NT]
        allv = arena[:, 0:CH * NT].rearrange("p (c n) -> p c n", n=NT)
        mixT, xnT = allv[:, BIG:MIX, :], allv[:, MIX:XN, :]
        ring = sb("ring", P, 2, SLOT)
        kvr = arena[:, XN * NT:ARENA]
        mb_at = nc.sbuf_base
        membuf = sb("membuf", P, 4 * SLOT)
        wparts = nc.alloc_sbuf_tensor_at("wparts", [P, 2, 2, SLOT], F32R, offset=mb_at)
        mkv = sb("mkv", P, 2, 2, 2, N_MEM)
        mq = sb("mq", P, MEMC, NT)
        qmblk = sb("qmblk", P, MEMC, DEC_B, 4 * DEC_T)
        qblk = sb("qblk", P, SBC, DEC_B, QC)
        common = sb("common", P, 2 * P)
        pconst = sb("pconst", P, 12 * P)
        gains = sb("gains", P, len(GAINS), KD)
        dnw = sb("dnw", P, QKV, DN_TAPS)
        ffw = sb("ffw", P, 2, 2 * FF, FF_TAPS + 1)
        cstate = sb("cstate", P, 2 * FF * DEC_B * 2)
        cnew = sb("cnew", P, 2 * FF * (DEC_B + 1) * 2)
        rstd = sb("rstd", P, NT)
        sqsum, sqone = sb("sqsum", P, NT)[:, :], sb("sqone", P, NT)[:, :]
        vstage = (sqsum, sqone)
        wba = sb("wba", P, KD, 2 * DN_H)
        tok = sb("tok", P, 9, NCH + 1, DN_H)
        small = sb("small", P, 48)
        sbias = sb("sbias", P, 2)
        biash = sb("biash", P, SB_H)
        pages = sb("pages", 1, DEC_B * PAGES, dt=I32)

        ones, ident = common[:, 0:P], common[:, P:2 * P]
        levelm = [pconst[:, l * P:(l + 1) * P] for l in range(LEVELS)]
        cumT, maskT, cum8, mask8, same8 = (pconst[:, (LEVELS + i) * P:(LEVELS + i + 1) * P] for i in range(5))
        suffix = pconst[:, 0:P]
        strict = pconst[:, P:P + SEQ]
        strict8 = pconst[:, P + SEQ:P + SEQ + DEC_B * NS]
        sq = allv[:, BIG - 2:BIG, :]
        A, R = slice(0, KD), slice(MIX, XN)
        M, U, Z = slice(BIG, MIX), slice(KD, 2 * KD), slice(2 * KD, BIG)
        PLACE = {"in_a": (Z, R, M), "out_a": (M, R, M), "k": (U, R, M), "in_b": (A, Z, A), "out_b": (M, R, M)}
        for layer in range(2):
            PLACE[f"up{layer}"] = (M, R, M)
            PLACE[f"down{layer}"] = (slice(0, FF), slice(FF, 2 * FF), slice(0, FF))
        parts = {(p.start, p.stop): nc.alloc_sbuf_tensor_at(f"parts{p.start}_{p.stop}", [P, p.stop - p.start, NT], F32R,
                                                            offset=at + 4 * NT * p.start)
                 for p in (A, R, M, Z, slice(0, FF), slice(FF, 2 * FF))}
        PLACE["v"] = PLACE["k"]
        PLACE = {n: (allv[:, x, :], parts[h.start, h.stop], parts[lo.start, lo.stop]) for n, (x, h, lo) in PLACE.items()}
        outv = allv[:, A, :]
        downv = allv[:, 2 * FF:2 * FF + KD, :]
        epsc, alog, dtb, ogain = small[:, 0:1], small[:, 1:7], small[:, 7:13], small[:, 13:14]
        nalog, vmax, vsum, vrec = small[:, 14:20], small[:, 20:24], small[:, 24:28], small[:, 28:32]
        onec = small[:, 32:33]

        rawp = kvr[:, 0:2 * (SEQ + 3)].rearrange("p (a n) -> p a n", a=2)
        o = 2 * (SEQ + 3)
        raws = kvr[:, o:o + 2 * DEC_B * 11].rearrange("p (a b n) -> p a b n", a=2, b=DEC_B)
        o += 2 * DEC_B * 11
        acc = kvr[:, o:o + 2 * NT].rearrange("p (a n) -> p a n", a=2)
        o += 2 * NT
        gate = kvr[:, o:o + NT]
        kvT = kvr[:, 0:SBC * NT].rearrange("p (c n) -> p c n", c=SBC)
        o = SBC * NT
        vtok = kvr[:, o:o + NCH * SBC * P].rearrange("p (t n) -> p t n", t=NCH)
        o += NCH * SBC * P
        vnew64 = kvr[:, o:o + SBC * P]

        w_full = [sem("w_full0"), sem("w_full1")]
        hi_ready, lo_ready, xhi, xlo, xlo_late = (sem(n) for n in ("hi_ready", "lo_ready", "xhi", "xlo", "xlo_late"))
        unit_done, evacuated = sem("unit_done"), sem("evacuated")
        mem_loaded, loaded, consts_b = sem("mem_loaded"), sem("loaded"), sem("consts_b")
        sq_ready, sq_summed, rstd_ready, normed = sem("sq_ready"), sem("sq_summed"), sem("rstd_ready"), sem("normed")
        dve_own, act_own, pool_own = sem("dve_own"), sem("act_own"), sem("pool_own")
        conv_done, tail_kept, gated = sem("conv_done"), sem("tail_kept"), sem("gated")
        y_ready, pads_ready, pads_zeroed = sem("y_ready"), sem("pads_ready"), sem("pads_zeroed")
        stored = sem("stored")
        state_in = sem("state_in")
        zeroed = sem("zeroed")
        tk_pe, tk_act, tk_dve = sem("tk_pe"), sem("tk_act"), sem("tk_dve")
        v_turned, v_read = sem("v_turned"), sem("v_read")
        kv_stored, mkv_stored, queries = sem("kv_stored"), sem("mkv_stored"), sem("queries")
        mem_in = [sem("mem_in0"), sem("mem_in1")]
        hid = sem("hid")
        n_stored = [0]

        def store(eng, out, src):
            eng.dma_start(out, src).then_inc(stored, 16)
            n_stored[0] += 16

        class Own:

            def __init__(self, s):
                self.sem, self.value = s, 0

            def inc(self):
                self.value += 1
                return 1

        dv, ac, po = Own(dve_own), Own(act_own), Own(pool_own)
        norm_no = [0]
        NORMS = ["mem", "mix_pre0", "mix_post0", "ffn_pre0", "ffn_post0", "kv", "mix_post1", "ffn_pre1", "ffn_post1"]
        APPLIES = ["mem0", "mem1", "mix_pre0", "mix_post0", "ffn_pre0", "ffn_post0", "kv", "mix_pre1",
                   "mix_post1", "ffn_pre1", "ffn_post1"]
        applied = {n: (i + 1) * KD for i, n in enumerate(APPLIES)}
        stat = {n: i + 1 for i, n in enumerate(NORMS)}
        SQUARES = [1 if "post" in n else KD for n in NORMS]
        squares = {n: sum(SQUARES[:i]) for i, n in enumerate(NORMS)}

        xflat = xnT[:, :, :].rearrange("p c n -> p (c n)")
        HW = DN_H * P

        def tile6(i):
            if i < 6:
                a = xflat[:, i * HW:(i + 1) * HW]
            else:
                a = kvr[:, (i - 6) * HW:(i - 5) * HW]
            return a.rearrange("p (h n) -> p h n", h=DN_H)

        (qn, kn, eg, ktk, vb, wk, gamT, LT, Tm, TT, M1, BT, WTn, qdec, Sst) = (tile6(i) for i in range(15))
        sqq, sqk, rq, rk = Tm, TT, M1, BT
        ug, ib = vb, wk
        vst = WTn
        vnew, osq, ro = BT, M1, Tm
        bigv = big[:, :].rearrange("p (c n) -> p c n", n=NT)
        S8 = [membuf[:, i * 1024:(i + 1) * 1024].rearrange("p (b n) -> p b n", b=DEC_B) for i in range(2)]
        WTm = membuf[:, 2048:2048 + DEC_B * NS].rearrange("p (b n) -> p b n", b=DEC_B)
        WTd = membuf[:, 2048:2048 + DEC_B * (NS + DEC_T)].rearrange("p (b n) -> p b n", b=DEC_B)[:, :, 0:DEC_T]
        vmask = membuf[0:NS, 2624:2624 + 1024].rearrange("p (b n) -> p b n", b=DEC_B)
        G = range(2)

        def heads(a, g, rows=P, T=P):
            return a[0:rows, 3 * g:3 * g + 3, 0:T]

        def bank(b, rows=P, T=P):
            return PB[0:rows, b, 0:3 * P].rearrange("p (h n) -> p h n", h=3)[:, :, 0:T]

        def steps(prefix, table):
            return {e: Steps(sem(f"{prefix}_{e}"), names.split()) for e, names in table.items()}

        def dn_table(n, sample):
            pe = "ss0 ss1 gb0 gb1 bb0 bb1 kk0 kk1 kq0 kq1 kt0 kt1 vt0 vt1 t00 t01 "
            for l in range(1, n):
                pe += f"m{l}_0 m{l}_1 "
                if l < n - 1:
                    pe += f"x{l}_0 "
                pe += f"xt{l}_0 "
                if l < n - 1:
                    pe += f"x{l}_1 "
                pe += f"xt{l}_1 "
            pe += "wt0 wt1 "
            if sample:
                pe += " ".join(f"vn{h} o{h} sa{h} sb{h}" for h in range(DN_H)) + " "
            else:
                pe += "vn0 vn1 o0 o1 s0 s1 "
            pe += "os0 os1"
            act = "sq0 sk0 sq1 sk1 lq0 lk0 lq1 lk1 rq0 rk0 rq1 rk1 eg0 eg1 ga0 ga1 t00 t01 "
            act += " ".join(f"m{l}_{g}" for l in range(1, n) for g in G) + " "
            if sample:
                act += " ".join(f"wt{h} vn{h}" for h in range(DN_H)) + " "
            else:
                act += "wt0 wt1 vn0 vn1 "
            act += "os0 os1 ol0 ol1 or0 or1"
            dve = "qn0 kn0 qn1 kn1 ga00 ga01 ga02 ga10 ga11 ga12 lt0 at0 lb0 lt1 at1 lb1 tt00 tt01 kd0 wk0 vb0 kd1 wk1 vb1 "
            for l in range(1, n):
                for g in G:
                    if l < n - 1:
                        dve += f"x{l}_{g} "
                    dve += f"xt{l}_{g} "
            if sample:
                dve += " ".join(f"vm{h} sd{h} sn{h}" for h in range(DN_H)) + " "
            else:
                dve += "s0 s1 s2 s3 s4 s5 "
            dve += "on0 on1 oz0 oz1"
            pool = "ug ib vst " + " ".join(f"bt{l}" for l in range(n)) + " qd"
            return dict(pe=pe, act=act, dve=dve, pool=pool)

        dn_p = steps("dn", dn_table(LEVELS, False))
        dn_s = steps("dns", dn_table(LEVELS_S, True))
        s8_in, s8_out = [sem("s8_in0"), sem("s8_in1")], sem("s8_out")
        dnconv_out, ffconv_out = sem("dnconv_out"), sem("ffconv_out")
        MEM_LOADS, LOADS = 16 * 6, 16 * 9

        tB, tG, tGc, tGl, tNg, tEd, tBg, tA, tX = (tok[:, i, :, :] for i in range(9))

        block = ctx.enter_context(nc.Block())

        def pe_busy(bank_, n):
            for _ in range(n):
                nc.tensor.matmul(PB[:, bank_, 0:2 * P], ones, common[:, :], start=True, stop=True)

        def pe_stats(pe, name, n=NT):
            j = stat[name] - 1
            if j:
                pe.wait_ge(rstd_ready, j)
            for k in range(SQUARES[j]):
                pe.wait_ge(sq_ready, squares[name] + k + 1)
                src = sqsum if "post" in name else sq[:, k % 2, :]
                for b, lo in enumerate(range(0, n, HALF)):
                    last = nc.tensor.matmul(PB[:, 4 + b, 0:min(n, HALF)], ones, src[:, lo:lo + min(n, HALF)],
                                            start=k == 0, stop=k == SQUARES[j] - 1)
                last.then_inc(sq_summed, 1)

        def act_stats(act, name, src, n=NT, after=None):
            for k in range(KD if src is not None else 0):
                if k >= 2:
                    act.wait_ge(sq_summed, squares[name] + k - 1)
                if after:
                    act.wait_ge(hid, HID[after] - KD + k + 1)
                nc.scalar.activation(sq[:, k % 2, 0:n], src[:, k, 0:n], ACT.Square).then_inc(sq_ready, 1)
            act.wait_ge(sq_summed, squares[name] + SQUARES[stat[name] - 1])
            before = {"mem": 0, "mix_pre0": applied["mem1"], "mix_post1": applied["mix_pre1"]}
            if name != "mem":
                act.wait_ge(normed, before.get(name, applied[name] - KD))
            for b, lo in enumerate(range(0, n, HALF)):
                last = nc.scalar.activation(rstd[:, lo:lo + min(n, HALF)], PB[:, 4 + b, 0:min(n, HALF)], ACT.Ln, bias=epsc,
                                            scale=1.0 / D_MODEL)
            last.then_inc(ac.sem, ac.inc())
            act.wait_ge(ac.sem, ac.value)
            nc.scalar.activation(rstd[:, 0:n], rstd[:, 0:n], ACT.Exp, scale=-0.5).then_inc(rstd_ready, 1)

        def dve_apply(dve, stat_name, name, src, dst, n=NT):
            dve.wait_ge(rstd_ready, stat[stat_name])
            g = GAINS.index(name)
            for k in range(KD):
                last = nc.vector.scalar_tensor_tensor(out=dst[:, k, 0:n], in0=src[:, k, 0:n],
                                                      scalar=gains[:, g, k:k + 1], in1=rstd[:, 0:n],
                                                      op0=ALU.mult, op1=ALU.mult)
                last.then_inc(normed, 1)

        HID = {n: (i + 1) * KD for i, n in enumerate(["mix_post0", "ffn_post0", "mix_post1", "ffn_post1"])}

        def dve_squares(dve, name, src):
            u0, per = UNIT0[name], UNITS[name] // KD
            base = dv.value
            nc.vector.memset(sqsum, 0.0)
            with dve.Fori(0, KD // 2) as i:
                for k in range(2):
                    dve.wait_ge(evacuated, 2 * per * i + (u0 + per * (k + 1)))
                    dve.wait_ge(dv.sem, 4 * i + (base + 2 * k))
                    nc.vector.tensor_tensor(sqone, row(src, 2 * i + k), row(src, 2 * i + k), ALU.mult).then_inc(dv.sem, 1)
                    dve.wait_ge(dv.sem, 4 * i + (base + 2 * k + 1))
                    nc.vector.tensor_tensor(sqsum, sqsum, sqone, ALU.add).then_inc(dv.sem, 1)
            dv.value = base + 2 * KD
            dve.wait_ge(dv.sem, dv.value)
            dve.sem_inc(sq_ready, 1)

        def dve_residual(dve, name):
            src = downv if name.startswith("ffn") else outv
            dve.wait_ge(rstd_ready, stat[name])
            for k in range(KD + 1):
                if k < KD:
                    nc.vector.scalar_tensor_tensor(out=src[:, k, :], in0=src[:, k, :],
                                                   scalar=gains[:, GAINS.index(name), k:k + 1], in1=rstd[:, :],
                                                   op0=ALU.mult, op1=ALU.mult).then_inc(normed, 1)
                if k:
                    dve.wait_ge(normed, applied[name] - KD + k)
                    nc.vector.tensor_tensor(hT[:, k - 1, :], hT[:, k - 1, :], src[:, k - 1, :], ALU.add).then_inc(hid, 1)

        def act_hi(act, name, i, k, first=0):
            u = UNIT0[name] + first + k
            act.wait_ge(w_full[k], 16 * i + (u // 2 + 1) * 16)
            act.wait_ge(unit_done, 2 * i + (u - 1))
            nc.scalar.activation(wparts[:, 0, k, :], ring[:, k, :], ACT.Copy).then_inc(hi_ready, 1)

        def pool_lo(pool, name, i, k, first=0):
            pool.wait_ge(hi_ready, 2 * i + (SPLIT0[name] + first + k + 1))
            nc.gpsimd.tensor_tensor(wparts[:, 1, k, :], ring[:, k, :], wparts[:, 0, k, :].bitcast(F32), ALU.subtract).then_inc(lo_ready, 1)

        def pool_los(pool, name, first, count):
            with pool.Fori(0, count // 2) as i:
                for k in range(2):
                    pool_lo(pool, name, i, k, first)

        def act_xhi(act, name, ready):
            x, h, _ = PLACE[name]
            for c in range(dict(XSPLIT)[name]):
                ready(c)
                nc.scalar.activation(h[:, c, :], x[:, c, :], ACT.Copy).then_inc(xhi, 1)

        def normed_chunk(act, name):
            return lambda c: act.wait_ge(normed, applied[name] - KD + c + 1)

        def x_lo(eng, ops, name, late=False):
            x, h, lo = PLACE[name]
            n = dict(XSPLIT)[name]
            for c in range(EARLY, n) if late else range(EARLY if name in SHARED else n):
                eng.wait_ge(xhi, X0[name] + c + 1)
                ops.tensor_tensor(lo[:, c, :], x[:, c, :], h[:, c, :].bitcast(F32), ALU.subtract).then_inc(
                    xlo_late if late else xlo, 1)

        def products(pe, name, dst, k, c, block, start, stop):
            _, h, lo = PLACE[name]
            shared = "k" if name == "v" else name
            if shared in SHARED and c >= EARLY:
                pe.wait_ge(xlo_late, SHARED.index(shared) * (KD - EARLY) + c - EARLY + 1)
            else:
                pe.wait_ge(xlo, XLO0[name] + c + 1)
            for part, x in ((0, h), (0, lo), (1, h)):
                for b in range(2):
                    last = nc.tensor.matmul(dst(b), wparts[:, part, k, block * P:(block + 1) * P],
                                            x[:, c, b * HALF:(b + 1) * HALF], start=start and part == 0 and x is h,
                                            stop=stop and part == 1)
            return last

        def pe_split(pe, name):
            u0, s0 = UNIT0[name], SPLIT0[name]

            def unit(i, k):
                pe.wait_ge(evacuated, 2 * i + (u0 + k - 1))
                pe.wait_ge(lo_ready, 2 * i + (s0 + k + 1))
                for c in range(KD):
                    last = products(pe, name, lambda b: PB[:, 2 * b + k, 0:HALF], k, c, c, c == 0, c == KD - 1)
                last.then_inc(unit_done, 1)

            def turn_v(i, k, first=False):
                pe.wait_ge(evacuated, 2 * i + (u0 + k + 1))
                if not first:
                    pe.wait_ge(v_read, 2 * i + k)
                for t in range(NCH + 1):
                    m = P if t < NCH else NS
                    last = nc.tensor.transpose(PB[0:m, 6 + t // NCH, t % NCH * P:(t % NCH + 1) * P],
                                               vstage[k][:, t * P:t * P + m], ident)
                last.then_inc(v_turned, 1)
            if name != "v":
                with pe.Fori(0, UNITS[name] // 2) as i:
                    for k in range(2):
                        unit(i, k)
            else:
                unit(0, 0)
                unit(0, 1)
                turn_v(0, 0, True)
                with pe.Fori(0, SBC // 2 - 1) as i:
                    unit(i + 1, 0)
                    turn_v(i, 1)
                    unit(i + 1, 1)
                    turn_v(i + 1, 0)
                turn_v(SBC // 2 - 1, 1)

        def pe_down(pe, name):
            u0, s0 = UNIT0[name], SPLIT0[name]
            pe.wait_ge(evacuated, u0)
            with pe.Fori(0, KD // 2) as i:
                for m in range(2):
                    for third, blocks in enumerate(THIRDS):
                        w = 3 * m + third
                        if third == 0:
                            pe.wait_ge(evacuated, 6 * i + (u0 + 3 * m - 3))
                        pe.wait_ge(lo_ready, 6 * i + (s0 + w + 1))
                        for j in range(blocks):
                            c = KD * third + j
                            last = products(pe, name, lambda b: PB[:, 2 * b + m, 0:HALF], w % 2, c, j, c == 0, c == FF - 1)
                        last.then_inc(unit_done, 1)

        def pe_plain(pe, name, x, swap=False, first=0):
            u0 = UNIT0[name] + first
            for k in range(2):
                if u0 + k >= 2:
                    pe.wait_ge(evacuated, u0 + k - 1)
                pe.wait_ge(w_full[k], (u0 // 2 + 1) * 16)
                for t in range(N_MEM // P if swap else 1):
                    for c in range(KD):
                        w = ring[:, k, c * P:(c + 1) * P]
                        if swap:
                            last = nc.tensor.matmul(PB[:, k, t * P:(t + 1) * P], x[:, c, t * P:(t + 1) * P], w,
                                                    start=c == 0, stop=c == KD - 1)
                        else:
                            last = nc.tensor.matmul(PB[:, k, 0:N_MEM], w, x[:, c, 0:N_MEM], start=c == 0, stop=c == KD - 1)
                last.then_inc(unit_done, 1)

        def act_evac(act, name, place, count, first=0, scale=1.0, func=ACT.Copy, split=True, split_end=True):
            u0 = UNIT0[name] + first

            def turn(i, ahead):
                for k in range(2):
                    act.wait_ge(unit_done, 2 * i + (u0 + k + 1))
                    for dst, src in place(i, k):
                        last = nc.scalar.activation(dst, src, func, scale=scale)
                    last.then_inc(evacuated, 1)
                    if ahead:
                        act_hi(act, name, i, k, first + 2)
            whole = count // 2 if split == split_end else count // 2 - 1
            if whole > 1:
                with act.Fori(0, whole) as i:
                    turn(i, split)
            elif whole:
                turn(0, split)
            if whole < count // 2:
                turn(whole, split_end)

        def row(a, c, lo=0, hi=NT):
            if isinstance(c, int):
                return a[:, c, lo:hi]
            return a[:, bass.ds(c, 1), lo:hi].rearrange("p a n -> p (a n)")

        def chunked(a, first=0):
            return lambda i, k: [(row(a, 2 * i + (first + k), b * HALF, (b + 1) * HALF), PB[:, 2 * b + k, 0:HALF])
                                 for b in range(2)]

        def act_down(act, name):
            u0 = UNIT0[name]

            def turn(i, end):
                for m in range(2):
                    for third in range(3):
                        w = 3 * m + third
                        act.wait_ge(unit_done, 6 * i + (u0 + w + 1))
                        if third == 2:
                            for b in range(2):
                                last = nc.scalar.activation(row(downv, 2 * i + m, b * HALF, (b + 1) * HALF),
                                                            PB[:, 2 * b + m, 0:HALF], ACT.Copy)
                            last.then_inc(evacuated, 3)
                        if not (end and w >= 4):
                            act_hi(act, name, 3 * i, w % 2, w // 2 * 2 + 2)
            with act.Fori(0, KD // 2 - 1) as i:
                turn(i, False)
            turn(KD // 2 - 1, name == "down1")

        conv_base = {"in_a": 0, "up0": QKV, "up1": QKV + 2 * FF}

        def scalar_of(a, c, j):
            return a[:, bass.ds(c, 1), j:j + 1].rearrange("p a b -> p (a b)")

        def act_conv(act, name, taps, units):
            pad, u0, cb = taps - 1, UNIT0[name], conv_base[name]
            with act.Fori(0, units // 2) as i:
                for k in range(2):
                    act.wait_ge(unit_done, 2 * i + (u0 + k + 1))
                    act.wait_ge(conv_done, 2 * i + (cb + k + 1))
                    act.wait_ge(tail_kept, 2 * i + (cb + k + 1))
                    nc.scalar.activation(rawp[:, k, pad:pad + HALF], PB[:, k, 0:HALF], ACT.Copy)
                    nc.scalar.activation(rawp[:, k, pad + HALF:pad + SEQ], PB[:, 2 + k, 0:SEQ - HALF], ACT.Copy)
                    nc.scalar.activation(raws[:, k, :, pad:pad + DEC_T],
                                         PB[:, 2 + k, SEQ - HALF:HALF].rearrange("p (b t) -> p b t", b=DEC_B),
                                         ACT.Copy).then_inc(evacuated, 1)
                    act_hi(act, name, i, k, 2)
                if name == "in_a":
                    for k in range(2):
                        act.wait_ge(conv_done, 2 * i + (cb + k + 3))
                        nc.scalar.activation(row(bigv, 2 * i + k), acc[:, k, :], ACT.Silu).then_inc(gated, 1)
                else:
                    act.wait_ge(conv_done, 2 * i + (cb + 3))
                    act.wait_ge(y_ready, i + (cb // 2 + 1))
                    nc.scalar.activation(gate, acc[:, 0, :], ACT.Gelu_apprx_tanh,
                                         bias=scalar_of(ffw[:, int(name[-1]), :, :], 2 * i, FF_TAPS)).then_inc(gated, 2)

        def dve_conv(dve, name, taps, units):
            cb, u0 = conv_base[name], UNIT0[name]
            wts = dnw if name == "in_a" else ffw[:, int(name[-1]), :, :]
            base = dv.value
            with dve.Fori(0, units // 2) as i:
                own = 0
                for k in range(2):
                    dve.wait_ge(evacuated, 2 * i + (u0 + k + 1))
                    dve.wait_ge(pads_ready, 2 * i + (cb + k + 1))
                    dve.wait_ge(gated, 2 * i + (cb + k + 1))
                    dve.wait_ge(y_ready, i + (cb // 2 + 1))
                    for tap in range(taps):
                        w = scalar_of(wts, 2 * i + k, tap)
                        xp, xs = rawp[:, k, tap:tap + SEQ], raws[:, k, :, tap:tap + DEC_T]
                        ap_, as_ = acc[:, k, 0:SEQ], acc[:, k, SEQ:NT].rearrange("p (b t) -> p b t", b=DEC_B)
                        if tap == 0:
                            nc.vector.tensor_scalar(ap_, xp, w, None, ALU.mult)
                            last = nc.vector.tensor_scalar(as_, xs, w, None, ALU.mult)
                        else:
                            dve.wait_ge(dv.sem, i * (2 * (taps - 1)) + (base + own))
                            nc.vector.scalar_tensor_tensor(out=ap_, in0=xp, scalar=w, in1=ap_, op0=ALU.mult, op1=ALU.add)
                            last = nc.vector.scalar_tensor_tensor(out=as_, in0=xs, scalar=w, in1=as_, op0=ALU.mult,
                                                                  op1=ALU.add)
                        if tap < taps - 1:
                            last.then_inc(dv.sem, 1)
                            own += 1
                    last.then_inc(conv_done, 1)
                if name != "in_a":
                    dve.wait_ge(gated, 2 * i + (cb + 3))
                    dve.wait_ge(conv_done, 2 * i + (cb + 4))
                    nc.vector.scalar_tensor_tensor(out=row(bigv, i), in0=acc[:, 1, :],
                                                   scalar=scalar_of(ffw[:, int(name[-1]), :, :], 2 * i + 1, FF_TAPS),
                                                   in1=gate, op0=ALU.add, op1=ALU.mult).then_inc(y_ready, 1)
                else:
                    dve.sem_inc(y_ready, 1)
            dv.value = base + (units // 2) * (2 * (taps - 1))

        def pool_conv(pool, name, taps, units):
            pad, cb, u0 = taps - 1, conv_base[name], UNIT0[name]
            st = cstate[:, 0:units * DEC_B * pad].rearrange("p (c b n) -> p c b n", c=units, b=DEC_B)
            ne = cnew[:, 0:units * (DEC_B + 1) * pad].rearrange("p (c b n) -> p c b n", c=units, b=DEC_B + 1)
            with pool.Fori(0, units // 2) as i:
                for k in range(2):
                    pool.wait_ge(conv_done, 2 * i + (cb + k + 1))
                    pool.wait_ge(tail_kept, 2 * i + (cb + k + 1))
                    nc.gpsimd.tensor_copy(raws[:, k, :, 0:pad],
                                          st[:, bass.ds(2 * i + k, 1), :, :].rearrange("p a b n -> p (a b) n")).then_inc(pads_ready, 1)
                for k in range(2):
                    pool_lo(pool, name, i, k, 2)
                    pool.wait_ge(evacuated, 2 * i + (u0 + k + 1))
                    nc.gpsimd.tensor_copy(ne[:, bass.ds(2 * i + k, 1), 0:1, :].rearrange("p a b n -> p (a b n)"),
                                          rawp[:, k, SEQ:SEQ + pad])
                    nc.gpsimd.tensor_copy(ne[:, bass.ds(2 * i + k, 1), 1:, :].rearrange("p a b n -> p (a b) n"),
                                          raws[:, k, :, DEC_T:DEC_T + pad]).then_inc(tail_kept, 1)

        TILES = [(P, 0, NCH), (NS, NCH, NCH + 1)]
        baP = PB[:, 6, 0:(NCH + 1) * 2 * DN_H].rearrange("p (t x) -> p t x", x=2 * DN_H)

        def pe_tokens(pe):
            pe.wait_ge(normed, applied["mix_pre0"])
            for t in range(NCH + 1):
                m = min(P, NT - t * P)
                for c in range(KD):
                    last = nc.tensor.matmul(baP[0:m, t, :], PLACE["in_a"][0][:, c, t * P:t * P + m], wba[:, c, :],
                                            start=c == 0, stop=c == KD - 1)
            last.then_inc(tk_pe, 1)

        def pe_sums(pe):
            pe.wait_ge(tk_dve, 3)
            for i, (m, a, b) in enumerate(TILES):
                w = (b - a) * DN_H
                rhs = tG[0:m, a:b, :].rearrange("p t h -> p (t h)")
                nc.tensor.matmul(PB[0:m, 7, 32 * i:32 * i + w], (cumT, cum8)[i][0:m, 0:m], rhs, start=True, stop=True)
                last = nc.tensor.matmul(PB[0:m, 7, 64 + 32 * i:64 + 32 * i + w], (ones, same8)[i][0:m, 0:m], rhs,
                                        start=True, stop=True)
            last.then_inc(tk_pe, 1)

        def act_tokens(act):
            act.wait_ge(tk_pe, 1)
            for m, a, b in TILES:
                nc.scalar.activation(tB[0:m, a:b, :], baP[0:m, a:b, 0:DN_H], ACT.Exp, scale=-1.0)
            nc.scalar.activation(nalog, alog, ACT.Exp).then_inc(tk_act, 1)
            act.wait_ge(tk_dve, 2)
            for m, a, b in TILES:
                last = nc.scalar.activation(tX[0:m, a:b, :], tX[0:m, a:b, :], ACT.Exp)
            last.then_inc(tk_act, 1)
            act.wait_ge(tk_act, 2)
            for m, a, b in TILES:
                last = nc.scalar.activation(tX[0:m, a:b, :], tX[0:m, a:b, :], ACT.Ln, bias=onec[0:m, :])
            last.then_inc(tk_act, 1)

        def act_sums(act):
            act.wait_ge(tk_dve, 4)
            for m, a, b in TILES:
                nc.scalar.activation(tEd[0:m, a:b, :], tEd[0:m, a:b, :], ACT.Exp)
                last = nc.scalar.activation(tBg[0:m, a:b, :], tGc[0:m, a:b, :], ACT.Exp)
            last.then_inc(tk_act, 1)

        def dve_tokens(dve):
            def heads_of(x, m, n):
                return x[0:m, :].unsqueeze(1).to_broadcast([m, n, DN_H])
            dve.wait_ge(tk_act, 1)
            for m, a, b in TILES:
                nc.vector.tensor_scalar(tB[0:m, a:b, :], tB[0:m, a:b, :], 1.0, None, ALU.add)
                last = nc.vector.tensor_tensor(tA[0:m, a:b, :], baP[0:m, a:b, DN_H:], heads_of(dtb, m, b - a), ALU.add)
            last.then_inc(tk_dve, 1)
            dve.wait_ge(tk_dve, 1)
            for m, a, b in TILES:
                nc.vector.reciprocal(tB[0:m, a:b, :], tB[0:m, a:b, :])
                fl = lambda x: x[0:m, a:b, :].rearrange("p t h -> p (t h)")
                last = nc.vector.scalar_tensor_tensor(out=fl(tX), in0=fl(tA), scalar=-1.0, in1=fl(tA), op0=ALU.mult,
                                                      op1=ALU.min)
            last.then_inc(tk_dve, 1)
            dve.wait_ge(tk_act, 3)
            for m, a, b in TILES:
                fl = lambda x: x[0:m, a:b, :].rearrange("p t h -> p (t h)")
                last = nc.vector.scalar_tensor_tensor(out=fl(tX), in0=fl(tA), scalar=0.0, in1=fl(tX), op0=ALU.max,
                                                      op1=ALU.add)
            last.then_inc(dv.sem, dv.inc())
            dve.wait_ge(dv.sem, dv.value)
            for m, a, b in TILES:
                nc.vector.tensor_tensor(tG[0:m, a:b, :], tX[0:m, a:b, :], heads_of(nalog, m, b - a), ALU.mult)
                last = nc.vector.tensor_scalar(tX[0:m, a:b, :], tX[0:m, a:b, :], -1.0, None, ALU.mult)
            last.then_inc(dv.sem, dv.inc())
            dve.wait_ge(dv.sem, dv.value)
            for m, a, b in TILES:
                last = nc.vector.tensor_tensor(tG[0:m, a:b, :], tX[0:m, a:b, :], heads_of(nalog, m, b - a), ALU.mult)
            last.then_inc(tk_dve, 1)

        def dve_sums(dve):
            dve.wait_ge(tk_pe, 2)
            for i, (m, a, b) in enumerate(TILES):
                w = (b - a) * DN_H
                fl = lambda x: x[0:m, a:b, :].rearrange("p t h -> p (t h)")
                nc.vector.tensor_copy(fl(tGc), PB[0:m, 7, 32 * i:32 * i + w])
                last = nc.vector.tensor_scalar(fl(tNg), PB[0:m, 7, 32 * i:32 * i + w], -1.0, None, ALU.mult)
            last.then_inc(dv.sem, dv.inc())
            dve.wait_ge(dv.sem, dv.value)
            for i, (m, a, b) in enumerate(TILES):
                w = (b - a) * DN_H
                fl = lambda x: x[0:m, a:b, :].rearrange("p t h -> p (t h)")
                last = nc.vector.tensor_tensor(fl(tEd), PB[0:m, 7, 64 + 32 * i:64 + 32 * i + w], fl(tGc), ALU.subtract)
            last.then_inc(tk_dve, 1)
            dve.wait_ge(tk_act, 4)
            for m, a, b in TILES:
                last = nc.vector.tensor_tensor(tBg[0:m, a:b, :], tBg[0:m, a:b, :], tB[0:m, a:b, :], ALU.mult)
            last.then_inc(tk_dve, 1)

        def tile_of(i, rows_, c, h0, h1):
            if isinstance(c, int):
                return tok[0:rows_, i, c, h0:h1]
            return tok[0:rows_, i, bass.ds(c, 1), h0:h1].rearrange("p a h -> p (a h)")

        def dn_pe(pe, s, c, before, levels, T, sample):
            c = 0 if sample else c
            wait = lambda e, name: pe.wait_ge(s[e].sem, s[e].at(name, c))
            mark = s["pe"].mark
            S_ = s["pe"].sem
            bs, bt = before
            pe.wait_ge(bs["dve"].sem, bs["dve"].at("oz1", bt))
            pe.wait_ge(bs["act"].sem, bs["act"].at("or1", bt))
            for g in G:
                wait("act", f"sk{g}")
                nc.tensor.matmul(bank(g, P, T), ones, heads(sqq, g, P, T), start=True, stop=True)
                nc.tensor.matmul(bank(2 + g, P, T), ones, heads(sqk, g, P, T), start=True,
                                 stop=True).then_inc(S_, mark(f"ss{g}"))
            wait("pool", "ug")
            for g in G:
                nc.tensor.matmul(bank(4 + g, P, T), ones[0:T, :], heads(ug, g, T, T), start=True,
                                 stop=True).then_inc(S_, mark(f"gb{g}"))
            wait("pool", "ib")
            for g in G:
                nc.tensor.matmul(bank(6 + g, T, T), ones[0:T, 0:T], heads(ib, g, T, T), start=True,
                                 stop=True).then_inc(S_, mark(f"bb{g}"))
            for g in G:
                wait("dve", f"kn{g}")
                for h in range(3):
                    kh = kn[:, 3 * g + h, 0:T]
                    last = nc.tensor.matmul(bank(g, T, T)[:, h, :], kh, kh, start=True, stop=True)
                last.then_inc(S_, mark(f"kk{g}"))
            for g in G:
                for h in range(3):
                    last = nc.tensor.matmul(bank(2 + g, T, T)[:, h, :], kn[:, 3 * g + h, 0:T], qn[:, 3 * g + h, 0:T],
                                            start=True, stop=True)
                last.then_inc(S_, mark(f"kq{g}"))
            for g in G:
                wait("act", f"eg{g}")
                wait("dve", f"ga{g}2")
                for h in range(3):
                    last = nc.tensor.transpose(bank(4 + g, T, P)[:, h, :], kn[:, 3 * g + h, 0:T], ident)
                last.then_inc(S_, mark(f"kt{g}"))
            wait("pool", "vst")
            for g in G:
                wait("dve", f"lb{g}")
                for h in range(3):
                    last = nc.tensor.transpose(bank(6 + g, T, P)[:, h, :], vst[:, 3 * g + h, 0:T], ident)
                last.then_inc(S_, mark(f"vt{g}"))
            for g in G:
                wait("dve", f"tt0{g}")
                for h in range(3):
                    last = nc.tensor.transpose(bank(g, T, T)[:, h, :], TT[0:T, 3 * g + h, 0:T], ident[0:T, 0:T])
                last.then_inc(S_, mark(f"t0{g}"))
            for l in range(1, levels):
                wait("pool", f"bt{l}")
                for g in G:
                    if l == 1:
                        wait("act", f"t0{g}")
                    else:
                        wait("dve", f"x{l - 1}_{g}")
                    for h in range(3 * g, 3 * g + 3):
                        last = nc.tensor.matmul(bank(g, T, T)[:, h - 3 * g, :], BT[0:T, h, 0:T], Tm[0:T, h, 0:T],
                                                start=True, stop=True)
                    last.then_inc(S_, mark(f"m{l}_{g}"))
                for g in G:
                    wait("act", f"m{l}_{g}")
                    wait("dve", f"wk{g}" if l == 1 else f"xt{l - 1}_{g}")
                    if l < levels - 1:
                        for h in range(3 * g, 3 * g + 3):
                            last = nc.tensor.matmul(bank(2 + g, T, T)[:, h - 3 * g, :], TT[0:T, h, 0:T], M1[0:T, h, 0:T],
                                                    start=True, stop=True)
                        last.then_inc(S_, mark(f"x{l}_{g}"))
                    for h in range(3 * g, 3 * g + 3):
                        last = nc.tensor.matmul(bank(4 + g, T, T)[:, h - 3 * g, :], M1[0:T, h, 0:T], TT[0:T, h, 0:T],
                                                start=True, stop=True)
                    last.then_inc(S_, mark(f"xt{l}_{g}"))
            for g in G:
                wait("dve", f"xt{levels - 1}_{g}")
                for h in range(3):
                    last = nc.tensor.matmul(bank(g, P, T)[:, h, :], wk[0:T, 3 * g + h, :], TT[0:T, 3 * g + h, 0:T],
                                            start=True, stop=True)
                last.then_inc(S_, mark(f"wt{g}"))
            if not sample:
                for g in G:
                    wait("act", f"wt{g}")
                    for h in range(3 * g, 3 * g + 3):
                        dst = bank(2 + g)[:, h - 3 * g, :]
                        nc.tensor.matmul(dst, TT[:, h, :], vb[:, h, :], start=True, stop=False)
                        last = nc.tensor.matmul(dst, WTn[:, h, :], Sst[:, h, :], start=False, stop=True)
                    last.then_inc(S_, mark(f"vn{g}"))
                wait("pool", "qd")
                for g in G:
                    wait("act", f"vn{g}")
                    for h in range(3 * g, 3 * g + 3):
                        dst = bank(4 + g)[:, h - 3 * g, :]
                        nc.tensor.matmul(dst, Sst[:, h, :], qdec[:, h, :], start=True, stop=False)
                        last = nc.tensor.matmul(dst, vnew[:, h, :], gamT[:, h, :], start=False, stop=True)
                    last.then_inc(S_, mark(f"o{g}"))
                for g in G:
                    wait("dve", f"vb{g}")
                    for h in range(3 * g, 3 * g + 3):
                        last = nc.tensor.matmul(bank(6 + g)[:, h - 3 * g, :], ktk[:, h, :], vnew[:, h, :],
                                                start=True, stop=True)
                    last.then_inc(S_, mark(f"s{g}"))
            else:
                wait("pool", "qd")
                wait("dve", "vb1")
                for h in range(DN_H):
                    S8h = S8[h % 2]
                    wait("act", f"wt{h}")
                    pe.wait_ge(s8_in[h % 2], 16 * (h // 2 + 1))
                    if h >= 2:
                        wait("act", f"vn{h - 2}")
                    dst = PB[0:T, 2 + h % 2, 0:P]
                    nc.tensor.matmul(dst, TT[0:T, h, 0:T], vb[0:T, h, :], start=True, stop=False)
                    for b in range(DEC_B):
                        last = nc.tensor.matmul(dst, WTm[:, b, :], S8h[:, b, :], start=False, stop=b == DEC_B - 1)
                    last.then_inc(S_, mark(f"vn{h}"))
                    wait("act", f"vn{h}")
                    dst = bank(4 + h // 3, P, T)[:, h % 3, :]
                    nc.tensor.matmul(dst, vnew[0:T, h, :], gamT[0:T, h, 0:T], start=True, stop=False)
                    for b in range(DEC_B):
                        last = nc.tensor.matmul(dst[:, 8 * b:8 * b + 8], S8h[:, b, :], qdec[:, h, 8 * b:8 * b + 8],
                                                start=False, stop=b == DEC_B - 1)
                    last.then_inc(S_, mark(f"o{h}"))
                    wait("dve", f"vm{h}")
                    if h:
                        wait("dve", f"sn{h - 1}")
                    for half in range(2):
                        nc.tensor.matmul(PB[:, 6 + half, :], ktk[0:T, h, :],
                                         vmask[:, 4 * half:4 * half + 4, :].rearrange("p b n -> p (b n)"),
                                         start=True, stop=True).then_inc(S_, mark(f"s{'ab'[half]}{h}"))
            for g in G:
                wait("act", f"os{g}")
                nc.tensor.matmul(bank(g, P, T), ones, heads(osq, g, P, T), start=True, stop=True).then_inc(S_, mark(f"os{g}"))
            pe_busy(2, 7)

        def dn_act(act, s, c, before, levels, T, sample, cols):
            c = 0 if sample else c
            wait = lambda e, name: act.wait_ge(s[e].sem, s[e].at(name, c))
            mark, S_ = s["act"].mark, s["act"].sem
            bs, bt = before
            act.wait_ge(bs["pe"].sem, bs["pe"].at("os1", bt))
            act.wait_ge(bs["dve"].sem, bs["dve"].at("on1", bt))
            for g in G:
                nc.scalar.activation(heads(sqq, g, P, T), cols(0, g), ACT.Square).then_inc(S_, mark(f"sq{g}"))
                nc.scalar.activation(heads(sqk, g, P, T), cols(1, g), ACT.Square).then_inc(S_, mark(f"sk{g}"))
            for g in G:
                wait("pe", f"ss{g}")
                nc.scalar.activation(heads(rq, g, P, T), bank(g, P, T), ACT.Ln, bias=epsc).then_inc(S_, mark(f"lq{g}"))
                nc.scalar.activation(heads(rk, g, P, T), bank(2 + g, P, T), ACT.Ln, bias=epsc).then_inc(S_, mark(f"lk{g}"))
            for g in G:
                wait("act", f"lk{g}")
                nc.scalar.activation(heads(rq, g, P, T), heads(rq, g, P, T), ACT.Exp, scale=-0.5).then_inc(S_, mark(f"rq{g}"))
                nc.scalar.activation(heads(rk, g, P, T), heads(rk, g, P, T), ACT.Exp, scale=-0.5).then_inc(S_, mark(f"rk{g}"))
            for g in G:
                wait("pe", f"gb{g}")
                nc.scalar.activation(heads(eg, g, P, T), bank(4 + g, P, T), ACT.Exp).then_inc(S_, mark(f"eg{g}"))
            for g in G:
                wait("dve", f"ga{g}2")
                nc.scalar.activation(heads(gamT, g, T, T), heads(gamT, g, T, T), ACT.Exp).then_inc(S_, mark(f"ga{g}"))
            for g in G:
                wait("pe", f"t0{g}")
                nc.scalar.activation(heads(Tm, g, T, T), bank(g, T, T), ACT.Copy).then_inc(S_, mark(f"t0{g}"))
            for l in range(1, levels):
                for g in G:
                    wait("pe", f"m{l}_{g}")
                    nc.scalar.activation(heads(M1, g, T, T), bank(g, T, T), ACT.Copy).then_inc(S_, mark(f"m{l}_{g}"))
            if not sample:
                for g in G:
                    wait("pe", f"wt{g}")
                    nc.scalar.activation(heads(WTn, g, P, T), bank(g, P, T), ACT.Copy, scale=-1.0).then_inc(S_, mark(f"wt{g}"))
                for g in G:
                    wait("pe", f"vn{g}")
                    nc.scalar.activation(heads(vnew, g, T, P), bank(2 + g, T, P), ACT.Copy).then_inc(S_, mark(f"vn{g}"))
            else:
                for h in range(DN_H):
                    wait("pe", "wt1" if h == 0 else f"vn{h - 1}")
                    nc.scalar.activation(WTd, bank(h // 3, P, T)[:, h % 3, :].rearrange("p (b t) -> p b t", b=DEC_B),
                                         ACT.Copy, scale=-1.0).then_inc(S_, mark(f"wt{h}"))
                    wait("pe", f"vn{h}")
                    nc.scalar.activation(vnew[0:T, h, :], PB[0:T, 2 + h % 2, 0:P], ACT.Copy).then_inc(S_, mark(f"vn{h}"))
            for g in G:
                wait("pe", f"o{3 * g + 2}" if sample else f"o{g}")
                nc.scalar.activation(heads(osq, g, P, T), bank(4 + g, P, T), ACT.Square).then_inc(S_, mark(f"os{g}"))
            for g in G:
                wait("pe", f"os{g}")
                nc.scalar.activation(heads(ro, g, P, T), bank(g, P, T), ACT.Ln, bias=epsc, scale=1.0 / P).then_inc(S_, mark(f"ol{g}"))
            for g in G:
                wait("act", f"ol{g}")
                nc.scalar.activation(heads(ro, g, P, T), heads(ro, g, P, T), ACT.Exp, scale=-0.5).then_inc(S_, mark(f"or{g}"))

        def dn_dve(dve, s, c, before, levels, T, sample, cols, out):
            ct, c = c, 0 if sample else c
            wait = lambda e, name: dve.wait_ge(s[e].sem, s[e].at(name, c))
            mark, S_ = s["dve"].mark, s["dve"].sem
            bs, bt = before
            dve.wait_ge(bs["pe"].sem, bs["pe"].at("os1", bt))
            mask = (mask8 if sample else maskT)[0:T, 0:T]
            for g in G:
                wait("act", f"rk{g}")
                nc.vector.scalar_tensor_tensor(out=heads(qn, g, P, T), in0=cols(0, g), scalar=float(P) ** -0.5,
                                               in1=heads(rq, g, P, T), op0=ALU.mult, op1=ALU.mult).then_inc(S_, mark(f"qn{g}"))
                nc.vector.tensor_tensor(heads(kn, g, P, T), cols(1, g), heads(rk, g, P, T), ALU.mult).then_inc(S_, mark(f"kn{g}"))
            for g in G:
                wait("act", f"eg{g}")
                for h in range(3):
                    nc.vector.scalar_tensor_tensor(out=gamT[0:T, 3 * g + h, 0:T], in0=bank(4 + g, T, T)[:, h, :],
                                                   scalar=tile_of(4, T, ct, 3 * g + h, 3 * g + h + 1),
                                                   in1=mask, op0=ALU.add, op1=ALU.add).then_inc(S_, mark(f"ga{g}{h}"))
            for g in G:
                wait("pe", f"kk{g}")
                wait("act", f"ga{g}")
                nc.vector.tensor_tensor(heads(LT, g, T, T), bank(g, T, T), heads(gamT, g, T, T), ALU.mult).then_inc(S_, mark(f"lt{g}"))
                wait("pe", f"kq{g}")
                wait("dve", f"lt{g}")
                nc.vector.tensor_tensor(heads(gamT, g, T, T), bank(2 + g, T, T), heads(gamT, g, T, T), ALU.mult).then_inc(S_, mark(f"at{g}"))
                wait("pe", f"bb{g}")
                nc.vector.tensor_tensor(heads(LT, g, T, T), heads(LT, g, T, T), bank(6 + g, T, T), ALU.mult).then_inc(S_, mark(f"lb{g}"))
            wait("pool", "bt0")
            for g in G:
                nc.vector.tensor_tensor(heads(TT, g, T, T), ident[0:T, 0:T].unsqueeze(1).to_broadcast([T, 3, T]),
                                        heads(BT, g, T, T), ALU.subtract).then_inc(S_, mark(f"tt0{g}"))

            def bc(i, g):
                return tile_of(i, T, ct, 3 * g, 3 * g + 3).unsqueeze(2).to_broadcast([T, 3, P])
            for g in G:
                wait("pe", f"kt{g}")
                nc.vector.tensor_tensor(heads(ktk, g, T, P), bank(4 + g, T, P), bc(5, g), ALU.mult).then_inc(S_, mark(f"kd{g}"))
                nc.vector.tensor_tensor(heads(wk, g, T, P), bank(4 + g, T, P), bc(6, g), ALU.mult).then_inc(S_, mark(f"wk{g}"))
                wait("pe", f"vt{g}")
                nc.vector.tensor_tensor(heads(vb, g, T, P), bank(6 + g, T, P), bc(0, g), ALU.mult).then_inc(S_, mark(f"vb{g}"))
            for l in range(1, levels):
                for g in G:
                    if l < levels - 1:
                        wait("pe", f"x{l}_{g}")
                        if l > 1:
                            wait("dve", f"x{l - 1}_{g}")
                        nc.vector.tensor_tensor(heads(Tm, g, T, T), heads(Tm, g, T, T), bank(2 + g, T, T),
                                                ALU.subtract).then_inc(S_, mark(f"x{l}_{g}"))
                    wait("pe", f"xt{l}_{g}")
                    wait("dve", f"tt0{g}" if l == 1 else f"xt{l - 1}_{g}")
                    nc.vector.tensor_tensor(heads(TT, g, T, T), heads(TT, g, T, T), bank(4 + g, T, T),
                                            ALU.subtract).then_inc(S_, mark(f"xt{l}_{g}"))
            if not sample:
                for h in range(DN_H):
                    g = h // 3
                    wait("pe", f"s{g}")
                    nc.vector.scalar_tensor_tensor(out=Sst[:, h, :], in0=Sst[:, h, :], scalar=eg[:, h, T - 1:T],
                                                   in1=bank(6 + g)[:, h % 3, :], op0=ALU.mult, op1=ALU.add).then_inc(S_, mark(f"s{h}"))
            else:
                for h in range(DN_H):
                    wait("act", f"vn{h}")
                    if h:
                        wait("pe", f"sb{h - 1}")
                    nc.vector.tensor_tensor(vmask, vnew[0:T, h, :].unsqueeze(1).to_broadcast([T, DEC_B, P]),
                                            same8[0:T, 0:T:DEC_T].unsqueeze(2).to_broadcast([T, DEC_B, P]),
                                            ALU.mult).then_inc(S_, mark(f"vm{h}"))
                    wait("pe", f"o{h}")
                    nc.vector.tensor_tensor(S8[h % 2], S8[h % 2],
                                            eg[:, h, DEC_T - 1:T:DEC_T].unsqueeze(2).to_broadcast([P, DEC_B, P]),
                                            ALU.mult).then_inc(S_, mark(f"sd{h}"))
                    wait("pe", f"sb{h}")
                    wait("dve", f"sd{h}")
                    nc.vector.tensor_tensor(S8[h % 2].rearrange("p b n -> p (b n)"), S8[h % 2].rearrange("p b n -> p (b n)"),
                                            PB[:, 6:8, :].rearrange("p a n -> p (a n)"), ALU.add).then_inc(S_, mark(f"sn{h}"))
            for g in G:
                wait("act", f"or{g}")
                nc.vector.scalar_tensor_tensor(out=heads(qn, g, P, T), in0=bank(4 + g, P, T), scalar=ogain,
                                               in1=heads(ro, g, P, T), op0=ALU.mult, op1=ALU.mult).then_inc(S_, mark(f"on{g}"))
            for g in G:
                wait("dve", f"on{g}")
                nc.vector.tensor_tensor(out(g), heads(qn, g, P, T), cols(3, g), ALU.mult).then_inc(S_, mark(f"oz{g}"))

        def dn_pool(pool, s, c, before, levels, T, sample, vcols):
            ct, c = c, 0 if sample else c
            wait = lambda e, name: pool.wait_ge(s[e].sem, s[e].at(name, c))
            mark, S_ = s["pool"].mark, s["pool"].sem
            bs, bt = before
            pool.wait_ge(bs["pe"].sem, bs["pe"].at("os1", bt))
            cum = (cum8 if sample else cumT)[0:T, 0:T]

            def six(m, i):
                return (m.unsqueeze(1).to_broadcast([T, DN_H, T]), tile_of(i, T, ct, 0, DN_H).unsqueeze(2).to_broadcast([T, DN_H, T]))
            a, b = six(cum, 1)
            nc.gpsimd.tensor_tensor(ug[0:T, :, 0:T], a, b, ALU.mult).then_inc(S_, mark("ug"))
            a, b = six(ident[0:T, 0:T], 0)
            nc.gpsimd.tensor_tensor(ib[0:T, :, 0:T], a, b, ALU.mult).then_inc(S_, mark("ib"))
            nc.gpsimd.tensor_copy(vst[:, :, 0:T], vcols).then_inc(S_, mark("vst"))
            for l in range(levels):
                if l == 0:
                    wait("dve", "lb1")
                elif l == 1:
                    wait("dve", "tt01")
                else:
                    wait("pe", f"m{l - 1}_1")
                nc.gpsimd.tensor_tensor(BT[0:T, :, 0:T], LT[0:T, :, 0:T],
                                        levelm[l][0:T, 0:T].unsqueeze(1).to_broadcast([T, DN_H, T]),
                                        ALU.mult).then_inc(S_, mark(f"bt{l}"))
            wait("act", "eg1")
            wait("dve", "qn1")
            nc.gpsimd.tensor_tensor(qdec[:, :, 0:T], qn[:, :, 0:T], eg[:, :, 0:T], ALU.mult).then_inc(S_, mark("qd"))

        def dn_cols(c):
            def f(part, g):
                r = bigv[:, DN_H * part + 3 * g:DN_H * part + 3 * g + 3, :]
                return r[:, :, SEQ:NT] if isinstance(c, int) else r[:, :, bass.ds(c * P, P)]
            return f

        def dn_run(eng, e, fn, extra):
            eng.sem_inc(dn_p[e].sem, dn_p[e].n)
            eng.sem_inc(dn_s[e].sem, dn_s[e].n)
            with eng.Fori(0, NCH) as c:
                fn(eng, dn_p, c, (dn_p, c - 1), LEVELS, P, False, *extra(c))
            fn(eng, dn_s, NCH, (dn_p, NCH - 1), LEVELS_S, NS, True, *extra(NCH))

        ma = {}
        for layer in range(2):
            ma[layer] = (steps(f"map{layer}", dict(
                pe="tr sc av", act="tc e0 e1 e2 e3 o", dve="mx rc pn", pool="st")),
                steps(f"mas{layer}", dict(pe="sc tr av tv", act="e0 e1 tc oc o0 o1", dve="mx rc pn", pool="qz")))
        xs_ = xflat
        prob = xs_[:, 0:1024].rearrange("p (h m) -> p h m", h=4)
        probT = xs_[:, 1024:2048].rearrange("p (x t) -> p x t", x=8)
        mqst = xs_[:, 2048:2048 + MEMC * P].rearrange("p (c t) -> p c t", c=MEMC)
        memkv = [(a[:, 0:2048].rearrange("p (b c m) -> p b c m", b=4, c=MEMC),
                  a[:, 2048:4096].rearrange("p (b c f) -> p b c f", b=4, c=2)) for a in (membuf, big[:, 7168:11264])]

        def pe_mem(pe, layer):
            sp_, ss_ = ma[layer]
            mk, mv = mkv[:, layer, 0, :, :], mkv[:, layer, 1, :, :]
            s, S = sp_, sp_["pe"]

            def scores(t):
                pe.wait_ge(s["pool"].sem, s["pool"].at("st", t))
                for x in range(4):
                    e, f = x // 2, x % 2
                    last = nc.tensor.matmul(PB[:, e, f * N_MEM:(f + 1) * N_MEM], mqst[64 * e:64 * e + 64, f, :],
                                            mk[64 * e:64 * e + 64, f, :], start=True, stop=True)
                last.then_inc(S.sem, S.mark("sc"))

            def turn(t, end):
                pe.wait_ge(s["dve"].sem, s["dve"].at("pn", t))
                for x in range(8):
                    last = nc.tensor.transpose(PB[:, 2 + x // 4, (x % 4) * P:(x % 4 + 1) * P],
                                               prob[:, x // 2, (x % 2) * P:(x % 2 + 1) * P], ident)
                last.then_inc(S.sem, S.mark("tr"))
                if end:
                    S.skip(pe, t, "sc")
                else:
                    scores(t + 1)
                pe.wait_ge(s["act"].sem, s["act"].at("tc", t))
                for x in range(4):
                    e, f = x // 2, x % 2
                    h = 2 * f + e
                    for mc in range(2):
                        last = nc.tensor.matmul(PB[64 * e:64 * e + 64, 6, f * P:(f + 1) * P],
                                                mv[:, mc, h * DH:(h + 1) * DH], probT[:, 2 * x + mc, :],
                                                start=mc == 0, stop=mc == 1)
                last.then_inc(S.sem, S.mark("av"))
                if not end:
                    pe_busy(7, 8)
            S.skip(pe, -1, "tr")
            scores(0)
            S.skip(pe, -1, "av")
            with pe.Fori(0, NCH - 1) as t:
                turn(t, False)
            turn(NCH - 1, True)
            s = ss_
            pe.sem_inc(s["pe"].sem, s["pe"].n)
            pe.wait_ge(s["pool"].sem, s["pool"].at("qz"))
            pe.wait_ge(sp_["act"].sem, sp_["act"].at("o", NCH - 1))
            for g in G:
                pe.wait_ge(mem_in[g], 32 * (layer + 1))
                for b in range(4):
                    for f in range(MEMC):
                        last = nc.tensor.matmul(PB[32 * b:32 * b + 32, g, 0:N_MEM], qmblk[:, f, 4 * g + b, :],
                                                memkv[g][0][:, b, f, :], start=f == 0, stop=f == MEMC - 1)
            last.then_inc(s["pe"].sem, s["pe"].mark("sc"))
            pe.wait_ge(s["dve"].sem, s["dve"].at("pn"))
            for x in range(4):
                last = nc.tensor.transpose(PB[:, 2, x * P:(x + 1) * P], prob[:, x // 2, x % 2 * P:(x % 2 + 1) * P], ident)
            last.then_inc(s["pe"].sem, s["pe"].mark("tr"))
            pe.wait_ge(s["act"].sem, s["act"].at("tc"))
            for g in G:
                for mc in range(2):
                    for b in range(4):
                        last = nc.tensor.matmul(PB[32 * b:32 * b + 32, 4 + g, 0:MEMC * P],
                                                probT[:, 2 * g + mc, 32 * b:32 * b + 32], memkv[g][1][:, b, mc, :],
                                                start=mc == 0, stop=mc == 1)
            last.then_inc(s["pe"].sem, s["pe"].mark("av"))
            pe.wait_ge(s["act"].sem, s["act"].at("oc"))
            for x in range(4):
                last = nc.tensor.transpose(PB[:, 6, x * P:(x + 1) * P], prob[:, 2 + x // 2, x % 2 * P:(x % 2 + 1) * P], ident)
            last.then_inc(s["pe"].sem, s["pe"].mark("tv"))

        def act_mem(act, layer):
            s, ss_ = ma[layer]
            S = s["act"]

            def turn(t, now, after):
                if now:
                    act.wait_ge(s["pe"].sem, s["pe"].at("tr", t))
                    nc.scalar.activation(probT[:, :, :], PB[:, 2:4, :].rearrange("p a (x t) -> p (a x) t", t=P),
                                         ACT.Copy).then_inc(S.sem, S.mark("tc"))
                else:
                    S.skip(act, t, "tc")
                if after:
                    act.wait_ge(s["dve"].sem, s["dve"].at("mx", t + 1))
                    for h in range(4):
                        nc.scalar.activation(prob[:, h, :], PB[:, h // 2, (h % 2) * N_MEM:(h % 2 + 1) * N_MEM], ACT.Exp,
                                             bias=vmax[:, h:h + 1], accum_out=vsum[:, h:h + 1]).then_inc(S.sem, S.mark(f"e{h}"))
                else:
                    S.skip(act, t, "e0", "e1", "e2", "e3")
                if now:
                    act.wait_ge(s["pe"].sem, s["pe"].at("av", t))
                    nc.scalar.activation(mixT[:, 6:8, bass.ds(t * P, P)], PB[:, 6, 0:2 * P].rearrange("p (f t) -> p f t", f=2),
                                         ACT.Copy).then_inc(S.sem, S.mark("o"))
                else:
                    S.skip(act, t, "o")
            turn(-1, False, True)
            with act.Fori(0, NCH - 1) as t:
                turn(t, True, True)
            turn(NCH - 1, True, False)
            s = ss_
            act.sem_inc(s["act"].sem, s["act"].n)
            act.wait_ge(s["dve"].sem, s["dve"].at("mx"))
            for g in G:
                nc.scalar.activation(prob[:, g, :], PB[:, g, 0:N_MEM], ACT.Exp, bias=vmax[:, g:g + 1],
                                     accum_out=vsum[:, g:g + 1]).then_inc(s["act"].sem, s["act"].mark(f"e{g}"))
            act.wait_ge(s["pe"].sem, s["pe"].at("tr"))
            nc.scalar.activation(probT[:, 0:4, :], PB[:, 2, :].rearrange("p (x t) -> p x t", x=4),
                                 ACT.Copy).then_inc(s["act"].sem, s["act"].mark("tc"))
            act.wait_ge(s["pe"].sem, s["pe"].at("av"))
            nc.scalar.activation(prob[:, 2:4, :], PB[:, 4:6, 0:N_MEM], ACT.Copy).then_inc(s["act"].sem, s["act"].mark("oc"))
            act.wait_ge(s["pe"].sem, s["pe"].at("tv"))
            for e in range(2):
                for f in range(MEMC):
                    h = 2 * f + e
                    src = PB[64 * e:64 * e + 64, 6, :].rearrange("p (g f b x) -> p g f b x", g=2, f=MEMC, b=4)
                    last = nc.scalar.activation(
                        mixT[64 * e:64 * e + 64, 6 + f, SEQ:NT].rearrange("p (g b t) -> p g b t", g=2, b=4),
                        src[:, :, f, :, 8 * h:8 * h + 8], ACT.Copy)
                last.then_inc(s["act"].sem, s["act"].mark(f"o{e}"))

        def dve_mem(dve, layer):
            s, ss_ = ma[layer]
            dve.sem_inc(s["dve"].sem, s["dve"].n)
            with dve.Fori(0, NCH) as t:
                dve.wait_ge(s["pe"].sem, s["pe"].at("sc", t - 1))
                nc.vector.tensor_reduce(vmax, PB[:, 0:2, :].rearrange("p a (e m) -> p (a e) m", e=2), AX_X, ALU.max,
                                        negate=True).then_inc(s["dve"].sem, s["dve"].mark("mx"))
                dve.wait_ge(s["act"].sem, s["act"].at("e3", t - 1))
                nc.vector.reciprocal(vrec, vsum).then_inc(s["dve"].sem, s["dve"].mark("rc"))
                dve.wait_ge(s["dve"].sem, s["dve"].at("rc", t))
                nc.vector.tensor_tensor(prob, prob, vrec.unsqueeze(2).to_broadcast([P, 4, N_MEM]),
                                        ALU.mult).then_inc(s["dve"].sem, s["dve"].mark("pn"))
            s = ss_
            dve.sem_inc(s["dve"].sem, s["dve"].n)
            dve.wait_ge(s["pe"].sem, s["pe"].at("sc"))
            nc.vector.tensor_reduce(vmax[:, 0:2], PB[:, 0:2, 0:N_MEM], AX_X, ALU.max, negate=True).then_inc(
                s["dve"].sem, s["dve"].mark("mx"))
            dve.wait_ge(s["act"].sem, s["act"].at("e1"))
            nc.vector.reciprocal(vrec[:, 0:2], vsum[:, 0:2]).then_inc(s["dve"].sem, s["dve"].mark("rc"))
            dve.wait_ge(s["dve"].sem, s["dve"].at("rc"))
            nc.vector.tensor_tensor(prob[:, 0:2, :], prob[:, 0:2, :], vrec[:, 0:2].unsqueeze(2).to_broadcast([P, 2, N_MEM]),
                                    ALU.mult).then_inc(s["dve"].sem, s["dve"].mark("pn"))

        def pool_mem(pool, layer):
            s, ss_ = ma[layer]
            pool.sem_inc(s["pool"].sem, s["pool"].n)
            pool.sem_inc(ss_["pool"].sem, ss_["pool"].n)
            nc.gpsimd.tensor_copy(mqst, mq[:, :, 0:P]).then_inc(s["pool"].sem, s["pool"].mark("st"))
            pool.wait_ge(s["pool"].sem, s["pool"].at("st", 0))
            if layer:
                for e in range(2):
                    nc.gpsimd.tensor_copy(qblk[64 * e:64 * e + 64, :, :, 8 * e:8 * e + 8],
                                          mixT[64 * e:64 * e + 64, 0:SBC, SEQ:NT].rearrange("p c (b t) -> p c b t", b=DEC_B))
            for h in range(4):
                e = h % 2
                last = nc.gpsimd.tensor_copy(qmblk[64 * e:64 * e + 64, h // 2, :, 8 * h:8 * h + 8],
                                             mq[64 * e:64 * e + 64, h // 2, SEQ:NT].rearrange("p (b t) -> p b t", b=DEC_B))
            last.then_inc(ss_["pool"].sem, ss_["pool"].mark("qz"))
            pool.wait_ge(ss_["pool"].sem, ss_["pool"].at("qz"))
            with pool.Fori(1, NCH) as t:
                pool.wait_ge(s["pe"].sem, s["pe"].at("sc", t - 2))
                nc.gpsimd.tensor_copy(mqst, mq[:, :, bass.ds(t * P, P)]).then_inc(s["pool"].sem, s["pool"].mark("st"))

        spr = steps("sbp", dict(
            pe="c0 c1 v0 z v1", act="e0 l0 e1 l1 w0 w1 o",
            dve="z0 m0 s0 z1 m1 s1 d0 d1", pool="v qk"))
        zoff = [0, 512, 896, 1152]
        sbs = xs_[:, 0:4608]
        zP = [sbs[:, 0:1280], sbs[:, 1280:2560]]
        sP = [sbs[:, 2560:3840], membuf[:, 0:1280]]
        qst, kst = membuf[:, 1280:1792], membuf[:, 1792:2304]
        vstP = membuf[:, 2304:2816].rearrange("p (j n) -> p j n", j=NCH)
        zb = [(0, 0), (1, 0), (2, 0), (2, 256)]

        def region(e, j):
            b, c = zb[j]
            return PB[:, 3 * (1 - e) + b, c:c + SEQ - j * P]

        def zreg(a, j, lo=0):
            return a[:, zoff[j] + lo:zoff[j] + SEQ - j * P]

        def pe_sbp(pe):
            s = spr["pe"]

            def scores(i):
                pe.wait_ge(spr["pool"].sem, spr["pool"].at("qk", i - 1))
                for j in range(NCH):
                    for e in range(2):
                        last = nc.tensor.matmul(region(e, j), kst[64 * e:64 * e + 64, j * P:(j + 1) * P],
                                                qst[64 * e:64 * e + 64, j * P:SEQ], start=True, stop=True)
                last.then_inc(s.sem, s.mark("z"))

            def turn(i, end):
                for e in range(2):
                    pe.wait_ge(spr["dve"].sem, spr["dve"].at(f"s{e}", i))
                    for j in range(NCH):
                        r = region(e, j)
                        nc_after = list(range(j + 1, NCH))
                        last = nc.tensor.matmul(r, suffix, zreg(sP[e], j), start=True, stop=not nc_after)
                        for jj in nc_after:
                            last = nc.tensor.matmul(r[:, (jj - j) * P:], ones, zreg(sP[e], jj), start=False,
                                                    stop=jj == NCH - 1)
                    last.then_inc(s.sem, s.mark(f"c{e}"))
                for e in range(2):
                    pe.wait_ge(spr["act"].sem, spr["act"].at(f"w{e}", i))
                    if e == 0:
                        pe.wait_ge(spr["pool"].sem, spr["pool"].at("v", i))
                    for j in range(NCH):
                        last = nc.tensor.matmul(PB[64 * e:64 * e + 64, 6, j * P:SEQ], vstP[:, j, 64 * e:64 * e + 64],
                                                zreg(zP[e], j), start=j == 0, stop=j == NCH - 1)
                    last.then_inc(s.sem, s.mark(f"v{e}"))
                    if e == 0 and end:
                        s.skip(pe, i, "z")
                    elif e == 0:
                        pe.wait_ge(spr["dve"].sem, spr["dve"].at("d1", i))
                        scores(i + 1)
                if not end:
                    pe_busy(7, 14)
            s.skip(pe, -1, "c0", "c1", "v0")
            scores(0)
            s.skip(pe, -1, "v1")
            with pe.Fori(0, SBC - 1) as i:
                turn(i, False)
            turn(SBC - 1, True)

        def act_sbp(act):
            s = spr
            act.sem_inc(s["act"].sem, s["act"].n)
            with act.Fori(0, SBC) as i:
                for e in range(2):
                    act.wait_ge(s["dve"].sem, s["dve"].at(f"m{e}", i))
                    nc.scalar.activation(sP[e], sP[e], ACT.Exp).then_inc(s["act"].sem, s["act"].mark(f"e{e}"))
                    act.wait_ge(s["act"].sem, s["act"].at(f"e{e}", i))
                    nc.scalar.activation(sP[e], sP[e], ACT.Ln, bias=onec).then_inc(s["act"].sem, s["act"].mark(f"l{e}"))
                for e in range(2):
                    act.wait_ge(s["dve"].sem, s["dve"].at(f"d{e}", i))
                    nc.scalar.activation(zP[e], zP[e], ACT.Exp).then_inc(s["act"].sem, s["act"].mark(f"w{e}"))
                act.wait_ge(s["pe"].sem, s["pe"].at("v1", i))
                nc.scalar.activation(mixT[:, bass.ds(i, 1), 0:SEQ].rearrange("p a n -> p (a n)"), PB[:, 6, :],
                                     ACT.Copy).then_inc(s["act"].sem, s["act"].mark("o"))

        def dve_sbp(dve):
            s = spr
            dve.sem_inc(s["dve"].sem, s["dve"].n)
            with dve.Fori(0, SBC) as i:
                for e in range(2):
                    dve.wait_ge(s["pe"].sem, s["pe"].at("v1" if e else "z", i - 1))
                    bias = biash[:, bass.ds(2 * i + e, 1)]
                    for j in range(NCH):
                        last = nc.vector.scalar_tensor_tensor(out=zreg(zP[e], j), in0=region(e, j), scalar=bias,
                                                              in1=strict[:, 0:SEQ - j * P], op0=ALU.add, op1=ALU.add)
                    last.then_inc(s["dve"].sem, s["dve"].mark(f"z{e}"))
                    dve.wait_ge(s["dve"].sem, s["dve"].at(f"z{e}", i))
                    nc.vector.tensor_scalar(sP[e], zP[e], 40.0, None, ALU.min).then_inc(s["dve"].sem, s["dve"].mark(f"m{e}"))
                    dve.wait_ge(s["act"].sem, s["act"].at(f"l{e}", i))
                    nc.vector.tensor_tensor(sP[e], sP[e], zP[e], ALU.max).then_inc(s["dve"].sem, s["dve"].mark(f"s{e}"))
                for e in range(2):
                    dve.wait_ge(s["pe"].sem, s["pe"].at(f"c{e}", i))
                    for j in range(NCH):
                        last = nc.vector.tensor_tensor(zreg(zP[e], j), zreg(zP[e], j), region(e, j), ALU.subtract)
                    last.then_inc(s["dve"].sem, s["dve"].mark(f"d{e}"))

        def pool_sbp(pool):
            s = spr["pool"]

            def queries_keys(i):
                nc.gpsimd.tensor_copy(qst, row(mixT, i, 0, SEQ))
                nc.gpsimd.tensor_copy(kst, row(kvT, i, 0, SEQ)).then_inc(s.sem, s.mark("qk"))

            def values(i):
                pool.wait_ge(spr["pe"].sem, spr["pe"].at("v1", i - 1))
                nc.gpsimd.tensor_copy(vstP, vtok[:, :, bass.ds(i * P, P)]).then_inc(s.sem, s.mark("v"))
            s.skip(pool, -1, "v")
            queries_keys(0)
            with pool.Fori(0, SBC - 1) as i:
                values(i)
                queries_keys(i + 1)
            values(SBC - 1)
            s.skip(pool, SBC - 1, "qk")

        ssm = steps("sbs", dict(pe="t0 t1 z t2 t3 t4 v r", act="t0 z0 t2 z1 t4 e0 l0 e1 l1 w0 w1 o m",
                                dve="t1 k0 m0 t3 k1 m1 s0 c0 s1 c1 d0 d1", pool="q"))
        kpage = big[:, 0:PAGES * SBC * P].rearrange("p (c n) -> p c n", c=PAGES)
        vpage = big[:, PAGES * SBC * P:2 * PAGES * SBC * P].rearrange("p (c n) -> p c n", c=PAGES)
        k_in, v_in = sem("k_in"), sem("v_in")
        SROWS = [P, P // 2]
        PAST = PAGES * P
        zSb = [[xflat[0:SROWS[w], (2 * x + w) * ZW:(2 * x + w + 1) * ZW] for w in range(2)] for x in range(2)]
        sS = [membuf[0:SROWS[w], w * ZW:(w + 1) * ZW] for w in range(2)]
        TW = P + P // 2
        wT = membuf[:, 2 * ZW:2 * ZW + NC * TW].rearrange("p (c r) -> p c r", c=NC)
        oS = big[:, 12288:12288 + 2 * P]
        qs = big[:, 12288 + 2 * P:12288 + 2 * P + SBC * 32].rearrange("p (f x) -> p f x", f=SBC)
        SETS = [(0, 4), (4, SBC)]
        units_of = [(0, 2), (2, 4), (4, 6), (6, PAGES - 1), (PAGES - 1, NC)]

        def sbs_run(eng, turn):
            turn(-1, 1, False, True)
            with eng.Fori(0, DEC_B // 2 - 1) as i:
                for x in range(2):
                    turn(2 * i + x, x, True, True)
            turn(DEC_B - 2, 0, True, True)
            turn(DEC_B - 1, 1, True, False)

        def pe_sbs(pe):
            s, S = ssm, ssm["pe"]

            def transpose(b, x, u):
                c0, c1 = units_of[u]
                for c in range(c0, c1):
                    n = P if c < PAGES else NS
                    for w in range(2):
                        o = (c - c0) * TW + w * P
                        last = nc.tensor.transpose(PB[0:n, 5 + u % 2, o:o + SROWS[w]], zSb[x][w][:, c * P:c * P + n],
                                                   ident[0:SROWS[w], 0:SROWS[w]])
                last.then_inc(S.sem, S.mark(f"t{u}"))

            def turn(b, x, now, after):
                if now:
                    pe.wait_ge(s["act"].sem, s["act"].at("w1", b - 1))
                    transpose(b, x, 0)
                    transpose(b, x, 1)
                else:
                    S.skip(pe, b, "t0", "t1")
                if after:
                    pe.wait_ge(k_in, b * (16 * PAGES) + 32 * PAGES)
                    pe.wait_ge(s["pool"].sem, s["pool"].at("q", b))
                    for w, (f0, f1) in enumerate(SETS):
                        for span in range(3):
                            for f in range(f0, f1):
                                g = f - f0
                                if span < 2:
                                    rhs = kpage[:, 4 * span:4 * span + 4, f * P:(f + 1) * P]
                                    dst = PB[32 * g:32 * g + 32, 2 * w + span, :].rearrange("p (c n) -> p c n", c=4)
                                else:
                                    rhs, dst = kvT[:, f, SEQ:NT], PB[32 * g:32 * g + 32, 4, w * NS:(w + 1) * NS]
                                last = nc.tensor.matmul(dst, qs[:, f, :], rhs, start=True, stop=True)
                    last.then_inc(S.sem, S.mark("z"))
                else:
                    S.skip(pe, b, "z")
                if not now:
                    return S.skip(pe, b, "t2", "t3", "t4", "v", "r")
                for u in (2, 3, 4):
                    e = "act" if u % 2 == 0 else "dve"
                    pe.wait_ge(s[e].sem, s[e].at(f"t{u - 2}", b))
                    transpose(b, x, u)
                pe.wait_ge(s["act"].sem, s["act"].at("t4", b))
                pe.wait_ge(s["dve"].sem, s["dve"].at("t3", b))
                pe.wait_ge(v_in, b * (16 * PAGES) + 16 * PAGES)
                for w, (f0, f1) in enumerate(SETS):
                    for c in range(NC):
                        for f in range(f0, f1):
                            g, n = f - f0, P if c < PAGES else NS
                            v = vpage[:, c, f * P:(f + 1) * P] if c < PAGES else vnew64[0:NS, f * P:(f + 1) * P]
                            last = nc.tensor.matmul(PB[32 * g:32 * g + 32, 7, w * P:(w + 1) * P],
                                                    wT[0:n, c, w * P + 32 * g:w * P + 32 * g + 32], v,
                                                    start=c == 0, stop=c == NC - 1)
                last.then_inc(S.sem, S.mark("v"))
                pe.wait_ge(s["act"].sem, s["act"].at("o", b))
                for w in range(2):
                    last = nc.tensor.transpose(PB[:, 7, (2 + w) * P:(2 + w) * P + SROWS[w]], oS[0:SROWS[w], w * P:(w + 1) * P],
                                               ident[0:SROWS[w], 0:SROWS[w]])
                last.then_inc(S.sem, S.mark("r"))
            sbs_run(pe, turn)

        def sbs_t_evac(u):
            c0, c1 = units_of[u]
            parts = [(c0, c1, P)] if c1 < NC else [(c0, PAGES, P), (PAGES, NC, NS)]
            return [(wT[0:n, a:b, :], PB[0:n, 5 + u % 2, (a - c0) * TW:(b - c0) * TW].rearrange("p (c r) -> p c r", c=b - a))
                    for a, b, n in parts]

        def act_sbs(act):
            s, S = ssm, ssm["act"]

            def turn(b, x, now, after):
                zn = zSb[1 - x]
                wait = lambda e, name: act.wait_ge(s[e].sem, s[e].at(name, b))

                def transposed(u):
                    if not now:
                        return S.skip(act, b, f"t{u}")
                    wait("pe", f"t{u}")
                    for dst, src in sbs_t_evac(u):
                        last = nc.scalar.activation(dst, src, ACT.Copy)
                    last.then_inc(S.sem, S.mark(f"t{u}"))

                def scores(w):
                    if not after:
                        return S.skip(act, b, f"z{w}")
                    r = SROWS[w]
                    wait("pe", "z")
                    nc.scalar.activation(zn[w][:, 0:PAST], PB[0:r, 2 * w:2 * w + 2, :].rearrange("p a n -> p (a n)"),
                                         ACT.Identity, bias=sbias[0:r, w:w + 1])
                    nc.scalar.activation(zn[w][:, PAST:ZW], PB[0:r, 4, w * NS:(w + 1) * NS], ACT.Identity,
                                         bias=sbias[0:r, w:w + 1]).then_inc(S.sem, S.mark(f"z{w}"))
                transposed(0)
                scores(0)
                transposed(2)
                scores(1)
                transposed(4)
                for w in range(2):
                    if not after:
                        S.skip(act, b, f"e{w}", f"l{w}")
                        continue
                    wait("dve", f"m{w}")
                    nc.scalar.activation(sS[w], sS[w], ACT.Exp).then_inc(S.sem, S.mark(f"e{w}"))
                    wait("act", f"e{w}")
                    nc.scalar.activation(sS[w], sS[w], ACT.Ln, bias=onec[0:SROWS[w], :]).then_inc(S.sem, S.mark(f"l{w}"))
                for w in range(2):
                    if not after:
                        S.skip(act, b, f"w{w}")
                        continue
                    wait("dve", f"d{w}")
                    nc.scalar.activation(zn[w], zn[w], ACT.Exp).then_inc(S.sem, S.mark(f"w{w}"))
                if now:
                    wait("pe", "v")
                    nc.scalar.activation(oS[:, 0:P], PB[:, 7, 0:P], ACT.Copy)
                    nc.scalar.activation(oS[0:P // 2, P:2 * P], PB[0:P // 2, 7, P:2 * P], ACT.Copy).then_inc(S.sem, S.mark("o"))
                    wait("pe", "r")
                    for e in range(2):
                        for w, (f0, f1) in enumerate(SETS):
                            src = PB[64 * e:64 * e + 64, 7, (2 + w) * P:(2 + w) * P + SROWS[w]].rearrange("p (g x) -> p g x", x=32)
                            last = nc.scalar.activation(mixT[64 * e:64 * e + 64, f0:f1, bass.ds(b * DEC_T + SEQ, DEC_T)],
                                                        src[:, :, 8 * e:8 * e + 8], ACT.Copy)
                    last.then_inc(S.sem, S.mark("m"))
                else:
                    S.skip(act, b, "o", "m")
            sbs_run(act, turn)

        def dve_sbs(dve):
            s, S = ssm, ssm["dve"]

            def turn(b, x, now, after):
                zn = zSb[1 - x]
                wait = lambda e, name: dve.wait_ge(s[e].sem, s[e].at(name, b))
                for w, u in enumerate((1, 3)):
                    if now:
                        wait("pe", f"t{u}")
                        for dst, src in sbs_t_evac(u):
                            last = nc.vector.tensor_copy(dst, src)
                        last.then_inc(S.sem, S.mark(f"t{u}"))
                    else:
                        S.skip(dve, b, f"t{u}")
                    if not after:
                        S.skip(dve, b, f"k{w}", f"m{w}")
                        continue
                    wait("act", f"z{w}")
                    nc.vector.tensor_tensor(zn[w][:, PAST:ZW], zn[w][:, PAST:ZW],
                                            strict8[0:SROWS[w], bass.ds((b + 1) * NS, NS)], ALU.add).then_inc(
                                                S.sem, S.mark(f"k{w}"))
                    wait("dve", f"k{w}")
                    nc.vector.tensor_scalar(sS[w], zn[w], 40.0, None, ALU.min).then_inc(S.sem, S.mark(f"m{w}"))
                if not after:
                    return S.skip(dve, b, "s0", "c0", "s1", "c1", "d0", "d1")
                for w in range(2):
                    wait("act", f"l{w}")
                    nc.vector.tensor_tensor(sS[w], sS[w], zn[w], ALU.max).then_inc(S.sem, S.mark(f"s{w}"))
                    wait("dve", f"s{w}")
                    back = sS[w][:, ::-1]
                    nc.vector.tensor_tensor_scan(back, back, back, 0.0, ALU.add, ALU.max).then_inc(S.sem, S.mark(f"c{w}"))
                for w in range(2):
                    wait("dve", f"c{w}")
                    nc.vector.tensor_tensor(zn[w], zn[w], sS[w], ALU.subtract).then_inc(S.sem, S.mark(f"d{w}"))
            sbs_run(dve, turn)

        def pool_sbs(pool):
            S = ssm["pool"]

            def queries(b):
                nc.gpsimd.tensor_copy(qs[:, :, 0:QC], qblk[:, :, bass.ds(b, 1), :].rearrange("p f a x -> p f (a x)")).then_inc(
                    S.sem, S.mark("q"))
            queries(0)
            with pool.Fori(0, DEC_B - 1) as b:
                pool.wait_ge(ssm["pe"].sem, ssm["pe"].at("z", b - 1))
                queries(b + 1)

        def mem_place(layer, which):
            if which == 0:
                return lambda i, k: [(mkv[:, layer, 0, k, :], PB[:, k, 0:N_MEM])]
            return lambda i, k: [(mkv[:, layer, 1, :, k * P:(k + 1) * P], PB[:, k, 0:N_MEM].rearrange("p (t n) -> p t n", t=2))]

        def v_place(i, k):
            return [(vstage[k][:, b * HALF:(b + 1) * HALF], PB[:, 2 * b + k, 0:HALF]) for b in range(2)]

        def dve_v(dve):
            with dve.Fori(0, SBC) as u:
                col = bass.ds(u * P, P)
                dve.wait_ge(v_turned, u + 1)
                nc.vector.tensor_copy(vtok[:, :, col], PB[:, 6, :].rearrange("p (t n) -> p t n", t=NCH))
                nc.vector.tensor_copy(vnew64[0:NS, col], PB[0:NS, 7, 0:P]).then_inc(v_read, 1)

        @block.tensor
        def _(pe):
            mn = [bigv[:, 0:KD, :], bigv[:, KD:2 * KD, :]]
            pe.wait_ge(mem_loaded, MEM_LOADS)
            pe_stats(pe, "mem", N_MEM)
            for layer in range(2):
                if layer:
                    pe_stats(pe, "mix_pre0")
                pe.wait_ge(normed, applied[f"mem{layer}"])
                pe_plain(pe, f"mem{layer}", mn[layer])
                pe_plain(pe, f"mem{layer}", mn[layer], swap=True, first=2)
            pe.wait_ge(loaded, LOADS)
            pe_tokens(pe)
            pe_split(pe, "in_a")
            pe_sums(pe)
            dn_run(pe, "pe", dn_pe, lambda c: ())
            pe_mem(pe, 0)
            pe_split(pe, "out_a")
            pe_stats(pe, "mix_post0")
            for layer in range(2):
                if layer:
                    pe_stats(pe, "kv")
                    pe_split(pe, "k")
                    pe_split(pe, "v")
                    pe_split(pe, "in_b")
                    pe_mem(pe, 1)
                    pe.wait_ge(consts_b, 16)
                    pe_sbp(pe)
                    pe_sbs(pe)
                    pe_split(pe, "out_b")
                    pe_stats(pe, "mix_post1")
                pe_stats(pe, f"ffn_pre{layer}")
                pe_split(pe, f"up{layer}")
                pe_down(pe, f"down{layer}")
                pe_stats(pe, f"ffn_post{layer}")

        @block.scalar
        def _(act):
            act.sem_inc(gated, 2)
            nc.scalar.preload_act_table_set(EXP_LN)
            act.wait_ge(zeroed, 1)
            act.wait_ge(mem_loaded, MEM_LOADS)
            act_stats(act, "mem", mixT, N_MEM)
            for layer in range(2):
                for which in range(2):
                    act_evac(act, f"mem{layer}", mem_place(layer, which), 2, first=2 * which, split=False, split_end=False)
                if layer == 0:
                    act.wait_ge(loaded, LOADS)
                    act_stats(act, "mix_pre0", hT)
                    act_xhi(act, "in_a", normed_chunk(act, "mix_pre0"))
            for k in range(2):
                act_hi(act, "in_a", 0, k)
            act_tokens(act)
            nc.scalar.preload_act_table_set(SILU)
            act_conv(act, "in_a", DN_TAPS, QKV)
            act_evac(act, "in_a", chunked(bigv, QKV), DN_H, first=QKV, func=ACT.Silu)
            act_evac(act, "in_a", chunked(mq), 2, first=QKV + DN_H, scale=DH ** -0.5, split=False, split_end=False)
            nc.scalar.preload_act_table_set(EXP_LN)
            act_sums(act)
            act.wait_ge(conv_done, 2 + QKV)
            act.wait_ge(tail_kept, 2 + QKV)
            dn_run(act, "act", dn_act, lambda c: (dn_cols(c),))
            act_mem(act, 0)
            act_hi(act, "out_a", 0, 0)
            act.wait_ge(dn_s["dve"].sem, dn_s["dve"].at("oz1"))
            act.wait_ge(ma[0][1]["act"].sem, ma[0][1]["act"].at("o1"))
            act_xhi(act, "out_a", lambda c: None)
            act_hi(act, "out_a", 0, 1)
            act_evac(act, "out_a", chunked(outv), KD)
            act_stats(act, "mix_post0", None)
            for layer in range(2):
                if layer:
                    act_stats(act, "kv", hT, after="ffn_post0")
                    act_xhi(act, "k", normed_chunk(act, "kv"))
                    act_evac(act, "k", chunked(kvT), SBC)
                    act_xhi(act, "in_b", normed_chunk(act, "mix_pre1"))
                    act_evac(act, "v", v_place, SBC)
                    act_evac(act, "in_b", chunked(mixT), SBC, scale=DH ** -0.5)
                    act_evac(act, "in_b", chunked(mq), 2, first=SBC, scale=DH ** -0.5, split=False, split_end=False)
                    act_mem(act, 1)
                    act_sbp(act)
                    act_sbs(act)
                    act_hi(act, "out_b", 0, 0)
                    act.wait_ge(ssm["act"].sem, ssm["act"].at("m", DEC_B - 1))
                    act_xhi(act, "out_b", lambda c: None)
                    act_hi(act, "out_b", 0, 1)
                    act_evac(act, "out_b", chunked(outv), KD)
                    act_stats(act, "mix_post1", None)
                    act.wait_ge(kv_stored, 16 * 3)
                act_stats(act, f"ffn_pre{layer}", hT, after=f"mix_post{layer}")
                act_xhi(act, f"up{layer}", normed_chunk(act, f"ffn_pre{layer}"))
                act.wait_ge(pads_zeroed, layer + 2)
                nc.scalar.preload_act_table_set(GELU)
                act_conv(act, f"up{layer}", FF_TAPS, 2 * FF)

                def gated_chunk(c):
                    y0 = 1 + conv_base[f"up{layer}"] // 2
                    act.wait_ge(y_ready, y0 + (c + 1 if c < 18 else FF))
                    if c == 2:
                        act.wait_ge(unit_done, UNIT0[f"down{layer}"])
                    if c == 18:
                        act.wait_ge(tail_kept, 2 + conv_base[f"up{layer}"] + 2 * FF)
                act_xhi(act, f"down{layer}", gated_chunk)
                act_down(act, f"down{layer}")
                nc.scalar.preload_act_table_set(EXP_LN)
                act_stats(act, f"ffn_post{layer}", None)

        @block.vector
        def _(dve):
            dve.sem_inc(conv_done, 2)
            dve.sem_inc(y_ready, 1)
            mn = [bigv[:, 0:KD, :], bigv[:, KD:2 * KD, :]]
            dve.wait_ge(mem_loaded, MEM_LOADS)
            for layer in range(2):
                dve_apply(dve, "mem", f"mem{layer}", mixT, mn[layer], N_MEM)
            dve.wait_ge(loaded, LOADS)
            dve_apply(dve, "mix_pre0", "mix_pre0", hT, PLACE["in_a"][0])
            x_lo(dve, nc.vector, "in_a", late=True)
            dve_tokens(dve)
            dve.wait_ge(pads_zeroed, 1)
            dve_conv(dve, "in_a", DN_TAPS, QKV)
            dve_sums(dve)
            dve.wait_ge(evacuated, UNIT0["in_a"] + UNITS["in_a"])
            dve.wait_ge(gated, 2 + QKV)
            dn_run(dve, "dve", dn_dve, lambda c: (dn_cols(c), (lambda g: mixT[:, 3 * g:3 * g + 3, SEQ:NT]) if isinstance(c, int)
                                                 else (lambda g: mixT[:, 3 * g:3 * g + 3, bass.ds(c * P, P)])))
            dve_mem(dve, 0)
            x_lo(dve, nc.vector, "out_a")
            dve_squares(dve, "out_a", outv)
            dve_residual(dve, "mix_post0")
            for layer in range(2):
                if layer:
                    dve_apply(dve, "kv", "kv", hT, PLACE["k"][0])
                    x_lo(dve, nc.vector, "k", late=True)
                    dve_apply(dve, "kv", "mix_pre1", hT, PLACE["in_b"][0])
                    dve_v(dve)
                    dve_mem(dve, 1)
                    dve.wait_ge(consts_b, 16)
                    dve_sbp(dve)
                    dve_sbs(dve)
                    x_lo(dve, nc.vector, "out_b")
                    dve_squares(dve, "out_b", outv)
                    dve_residual(dve, "mix_post1")
                dve_apply(dve, f"ffn_pre{layer}", f"ffn_pre{layer}", hT, PLACE[f"up{layer}"][0])
                x_lo(dve, nc.vector, f"up{layer}", late=True)
                dve_conv(dve, f"up{layer}", FF_TAPS, 2 * FF)
                x_lo(dve, nc.vector, f"down{layer}")
                dve_squares(dve, f"down{layer}", downv)
                dve_residual(dve, f"ffn_post{layer}")

        @block.gpsimd
        def _(pool):
            nc.gpsimd.memset(qmblk[:, :, :, :], 0.0)
            nc.gpsimd.memset(qblk[:, :, :, :], 0.0)
            nc.gpsimd.memset(epsc, EPS)
            nc.gpsimd.memset(onec, 1.0).then_inc(zeroed, 1)
            nc.gpsimd.memset(rawp[:, :, 0:DN_TAPS - 1], 0.0).then_inc(pads_zeroed, 1)
            pool.sem_inc(tail_kept, 2)
            pool.wait_ge(loaded, LOADS)
            pool.wait_ge(zeroed, 1)
            x_lo(pool, nc.gpsimd, "in_a")
            for k in range(2):
                pool_lo(pool, "in_a", 0, k)
            pool_conv(pool, "in_a", DN_TAPS, QKV)
            pool_los(pool, "in_a", QKV + 2, UNITS["in_a"] - QKV - 2)
            pool.wait_ge(tail_kept, 2 + QKV)
            pool.dma_start(d["o_dnconv"], cnew[:, 0:QKV * (DEC_B + 1) * (DN_TAPS - 1)]).then_inc(dnconv_out, 16)
            pool.wait_ge(pads_ready, QKV)
            pool.dma_start(cstate[:, :], d["ff_state"][0]).then_inc(state_in, 16)
            pool.wait_ge(rstd_ready, stat["mix_pre0"])
            pool.wait_ge(unit_done, UNIT0["out_a"])
            pool.wait_ge(gated, 2 + QKV)
            pool.wait_ge(conv_done, 2 + QKV)
            nc.gpsimd.memset(Sst[:, :, :], 0.0)
            nc.gpsimd.memset(WTm[:, :, :], 0.0).then_inc(po.sem, po.inc())
            pool.wait_ge(po.sem, po.value)
            dn_run(pool, "pool", dn_pool, lambda c: ((bigv[:, 2 * DN_H:3 * DN_H, SEQ:NT] if isinstance(c, int)
                                                      else bigv[:, 2 * DN_H:3 * DN_H, bass.ds(c * P, P)]),))
            pool.wait_ge(dn_s["dve"].sem, dn_s["dve"].at("oz1"))
            pool_mem(pool, 0)
            for k in range(2):
                pool_lo(pool, "out_a", 0, k)
            pool_los(pool, "out_a", 2, KD)
            for layer in range(2):
                if layer:
                    pool.dma_start(pconst[:, 0:P + SEQ + DEC_B * NS], d["c_sb"]).then_inc(consts_b, 16)
                    x_lo(pool, nc.gpsimd, "k")
                    pool_los(pool, "k", 2, SBC)
                    x_lo(pool, nc.gpsimd, "in_b")
                    pool_los(pool, "v", 2, SBC - 2 + UNITS["in_b"])
                    pool.wait_ge(evacuated, UNIT0["in_b"] + UNITS["in_b"])
                    pool.wait_ge(v_read, SBC)
                    pool_mem(pool, 1)
                    pool.wait_ge(ma[1][1]["pe"].sem, ma[1][1]["pe"].at("av"))
                    nc.gpsimd.memset(qs[:, :, QC:32], 0.0)
                    pool_sbp(pool)
                    pool_sbs(pool)
                    for k in range(2):
                        pool_lo(pool, "out_b", 0, k)
                    pool_los(pool, "out_b", 2, KD)
                pool.wait_ge(hid, HID[f"mix_post{layer}"])
                if layer:
                    pool.wait_ge(kv_stored, 16 * 3)
                nc.gpsimd.memset(rawp[:, :, 0:FF_TAPS - 1], 0.0).then_inc(pads_zeroed, 1)
                pool.wait_ge(state_in, 16 * (layer + 1))
                pool.wait_ge(dnconv_out if layer == 0 else ffconv_out, 16)
                x_lo(pool, nc.gpsimd, f"up{layer}")
                pool_conv(pool, f"up{layer}", FF_TAPS, 2 * FF)
                pool.wait_ge(tail_kept, 2 + QKV + 2 * FF * (layer + 1))
                pool.dma_start(d["o_ffconv"][layer], cnew[:, :]).then_inc(ffconv_out, 16)
                if not layer:
                    pool.wait_ge(pads_ready, QKV + 2 * FF)
                    pool.dma_start(cstate[:, :], d["ff_state"][1]).then_inc(state_in, 16)
                pool_los(pool, f"down{layer}", 2, UNITS[f"down{layer}"] - 2 * layer)
            pool.wait_ge(ffconv_out, 32)

        @block.sync
        def _(sp):
            def load(s, dst, src):
                sp.dma_start(dst, src).then_inc(s, 16)
            load(mem_loaded, mixT[:, :, 0:N_MEM], d["memT"].rearrange("c p n -> p c n"))
            load(mem_loaded, common[:, :], d["c_common"])
            load(mem_loaded, gains[:, :, :], d["gains"])
            load(mem_loaded, alog, d["a_log"].to_broadcast([P, DN_H]))
            load(mem_loaded, dtb, d["dt_bias"].to_broadcast([P, DN_H]))
            load(mem_loaded, ogain, d["o_gain"])

            def feed(name, first=0, count=None):
                n = UNITS[name] if count is None else count

                def pair(i, first):
                    u0, s0 = UNIT0[name] + first, SPLIT0[name] + first
                    own = first > 0 or not isinstance(i, int)
                    for k in range(2):
                        if (name if own else AFTER.get(name)) in PLAIN:
                            sp.wait_ge(unit_done, 2 * i + (u0 + k - 1))
                        elif u0:
                            sp.wait_ge(lo_ready, 2 * i + (s0 + k - 1))
                        r = 2 * i + (u0 + k)
                        src = d["w8"][r] if isinstance(r, int) else d["w8"][bass.ds(r, 1), :, :].rearrange("a p n -> p (a n)")
                        sp.dma_start(ring[:, k, :], src).then_inc(w_full[k], 16)
                if first == 0:
                    pair(0, 0)
                    first, n = 2, n - 2
                if n == 2:
                    pair(0, first)
                elif n:
                    with sp.Fori(0, n // 2) as i:
                        pair(i, first)

            feed("mem0", count=2)
            load(loaded, hT[:, :, :], d["xT"].rearrange("c p n -> p c n"))
            load(loaded, pconst[:, :], d["c_dn"])
            load(loaded, dnw[:, :, :], d["dn_w"])
            load(loaded, cstate[:, 0:QKV * DEC_B * (DN_TAPS - 1)], d["dn_state"])
            load(loaded, wba[:, :, :], d["w_ba"])
            load(loaded, biash[:, :], d["sb_bias"].to_broadcast([P, SB_H]))
            load(loaded, ffw[:, :, :, :], d["ff_w"])
            load(loaded, pages[:, :], d["page_table"])
            load(loaded, sbias[:, :], d["sb_bias_rows"])
            feed("mem0", first=2, count=2)
            feed("mem1")
            feed("in_a")
            sp.wait_ge(evacuated, UNIT0["in_a"])
            store(sp, d["o_mkv"], mkv[:, :, :, :, :].rearrange("p l w c n -> p (l w c n)"))
            feed("out_a", count=2)
            sp.wait_ge(unit_done, UNIT0["out_a"])
            for h in range(2):
                sp.dma_start(S8[h], d["state_dn"][h]).then_inc(s8_in[h], 16)
            sp.wait_ge(dn_p["dve"].sem, dn_p["dve"].at("s5", NCH - 1))
            store(sp, d["o_dns_p"], Sst[:, :, :])
            for h in range(DN_H):
                sp.wait_ge(dn_s["dve"].sem, dn_s["dve"].at(f"sn{h}"))
                sp.dma_start(d["o_dns_s"][h], S8[h % 2]).then_inc(s8_out, 16)
                if h + 2 < DN_H:
                    sp.wait_ge(s8_out, 16 * (h + 1))
                    sp.dma_start(S8[h % 2], d["state_dn"][h + 2]).then_inc(s8_in[h % 2], 16)
            sp.wait_ge(s8_out, 16 * DN_H)

            def mem_load(layer, g):
                km, vm = memkv[g]
                sp.dma_start(km[:, :, :, :].rearrange("p b c m -> p b (c m)"),
                             d["cache_mk"][layer, 4 * g:4 * g + 4].rearrange("b p n -> p b n")).then_inc(mem_in[g], 16)
                sp.dma_start(vm[:, :, :, :].rearrange("p b c m -> p b (c m)"),
                             d["cache_mv"][layer, 4 * g:4 * g + 4].rearrange("b p n -> p b n")).then_inc(mem_in[g], 16)
            mem_load(0, 0)
            sp.wait_ge(dn_s["dve"].sem, dn_s["dve"].at("oz1"))
            mem_load(0, 1)
            feed("out_a", first=2, count=KD - 2)
            feed("up0")
            feed("down0")
            feed("k")
            feed("v")

            def page_loads(b, cache, dst, signal, used=None, turn=0):
                at = [sp.value_load(pages[0:1, b * PAGES + j:b * PAGES + j + 1] if isinstance(b, int)
                                    else pages[0:1, bass.ds(b * PAGES + j, 1)],
                                    min_val=0, max_val=d[cache].shape[0] - 1) for j in range(PAGES)]
                if used:
                    sp.wait_ge(ssm["pe"].sem, ssm["pe"].at(used, turn))
                for j in range(PAGES):
                    sp.dma_start(dst[:, j, :], d[cache][bass.ds(at[j], 1), :, :].rearrange("a p n -> p (a n)")).then_inc(
                        signal, 16)
            feed("in_b")
            sp.wait_ge(evacuated, UNIT0["in_b"])
            sp.wait_ge(v_read, SBC)
            sp.dma_start(d["o_k"], kvT[:, :, :]).then_inc(kv_stored, 16)
            sp.dma_start(d["o_v"], vtok[:, :, :]).then_inc(kv_stored, 16)
            sp.dma_start(d["o_vs"], vnew64[0:NS, :]).then_inc(kv_stored, 16)
            sp.wait_ge(unit_done, UNIT0["out_b"])
            mem_load(1, 0)
            mem_load(1, 1)
            feed("out_b", count=2)
            page_loads(0, "kpages", kpage, k_in)
            sp.wait_ge(ma[1][1]["pe"].sem, ma[1][1]["pe"].at("av"))
            page_loads(0, "vpages", vpage, v_in)
            page_loads(1, "kpages", kpage, k_in, "z", -1)
            with sp.Fori(1, DEC_B - 1) as b:
                page_loads(b + 1, "kpages", kpage, k_in, "z", b - 1)
                page_loads(b, "vpages", vpage, v_in, "v", b - 1)
            page_loads(DEC_B - 1, "vpages", vpage, v_in, "v", DEC_B - 2)
            feed("out_b", first=2, count=KD - 2)
            feed("up1")
            feed("down1")
            for k in range(0, KD, 2):
                sp.wait_ge(hid, HID["ffn_post1"] - KD + k + 2)
                store(sp, d["o_y"][k:k + 2].rearrange("c p n -> p c n"), hT[:, k:k + 2, :])
            sp.wait_ge(kv_stored, 16 * 3)
            sp.wait_ge(stored, n_stored[0])


def kernel(**inputs):
    from concourse.bacc import Bacc
    from concourse.bass_utils import run_bass_kernel_spmd

    x = {n: np.asarray(a) for n, a in inputs.items()}
    A = np.ascontiguousarray
    nu = D_MODEL // P

    def units(w):
        return w.reshape(nu, P, -1, P).transpose(2, 1, 0, 3).reshape(-1, P, nu * P)

    def down_units(w):
        r = w.reshape(FF, P, nu, P).transpose(2, 1, 0, 3)
        r = np.concatenate([r, np.zeros((nu, P, 3 * KD - FF, P), w.dtype)], 2)
        return r.reshape(nu, P, 3, KD * P).transpose(0, 2, 1, 3).reshape(-1, P, KD * P)

    def halves(a):
        return a.reshape(a.shape[:-1] + (2, FF, P)).swapaxes(-3, -2).reshape(a.shape)

    def chunks(a):
        r = a.reshape(a.shape[:-1] + (-1, P))
        return np.moveaxis(r, (-1, -2), (0, 1))

    def bias_rows(b):
        r = np.zeros((2, 4, 4, DEC_T), b.dtype)
        r[:, :, 0:2] = np.concatenate([b, np.zeros(4, b.dtype)]).reshape(2, 4, 2)[..., None]
        return A(r.reshape(2, P).T)

    zcols = (QKV + DN_H) * P
    wa, wb = x["w_in_a"][0], x["w_in_b"][0]
    parts = {"mem0": x["w_mem_kv"][0], "mem1": x["w_mem_kv"][1],
             "in_a": np.concatenate([wa[:, :zcols], wa[:, zcols + 2 * DN_H:]], 1), "out_a": x["w_out_a"][0],
             "up0": halves(x["ffn_w_up"][0]), "v": x["w_kv"][:, SBC * P:], "k": x["w_kv"][:, :SBC * P], "in_b": wb, "out_b": x["w_out_b"][0],
             "up1": halves(x["ffn_w_up"][1])}
    c_common, c_dn, c_sb = constants()
    n_phys = x["cache_k"].shape[0]
    gains_ = np.concatenate([x["mem_norm"], x["norm_mix_pre"], x["norm_mix_post"], x["norm_ffn_pre"], x["norm_ffn_post"],
                             x["kv_norm"][None]], 0)
    order = [0, 1, 2, 4, 6, 8, 10, 3, 5, 7, 9]
    arrays = {
        "xT": A(np.concatenate([x["x_prompt"].reshape(SEQ, -1), x["x_sample"].reshape(NS, -1)]).T.reshape(nu, P, NT)),
        "memT": A(x["mem_prompt"][0].T.reshape(nu, P, N_MEM)),
        "w8": np.concatenate([units(parts[n]) if n in parts else down_units(x["ffn_w_down"][int(n[-1])])
                              for n, _ in UNIT_PLAN]),
        "w_ba": A(wa[:, zcols:zcols + 2 * DN_H].reshape(nu, P, 2 * DN_H).transpose(1, 0, 2)),
        "gains": A(chunks(gains_[order]).transpose(0, 2, 1)),
        "a_log": A(x["dn_a_log"].reshape(1, DN_H)), "dt_bias": A(x["dn_dt_bias"].reshape(1, DN_H)),
        "o_gain": A(x["dn_o_gain"].reshape(P, 1)), "sb_bias": A(x["sb_bias"].reshape(1, SB_H)),
        "sb_bias_rows": bias_rows(x["sb_bias"].reshape(SB_H)),
        "dn_w": A(chunks(x["dn_conv_w"][0])),
        "ff_w": A(chunks(halves(np.concatenate([x["ffn_conv_w"], x["ffn_conv_b"][:, None]], 1))).transpose(0, 2, 1, 3)),
        "dn_state": A(chunks(x["state_dn_conv"][0]).reshape(P, -1)),
        "ff_state": A(np.stack([chunks(halves(x["state_ffn_conv"][l])).reshape(P, -1) for l in range(2)])),
        "state_dn": A(x["state_dn"][0].transpose(1, 2, 0, 3)),
        "cache_mk": A(x["cache_mem_k"].reshape(2, DEC_B, N_MEM, MEMC, P).transpose(0, 1, 4, 3, 2).reshape(2, DEC_B, P, -1)),
        "cache_mv": A(x["cache_mem_v"].reshape(2, DEC_B, 2, P, MEMC * P).transpose(0, 1, 3, 2, 4).reshape(2, DEC_B, P, -1)),
        "kpages": A(x["cache_k"].reshape(n_phys, P, SBC, P).transpose(0, 3, 2, 1).reshape(n_phys, P, SBC * P)),
        "vpages": A(x["cache_v"].reshape(n_phys, P, SBC * P)),
        "page_table": A(x["page_table"].reshape(1, -1)),
        "c_common": c_common, "c_dn": c_dn, "c_sb": c_sb,
    }
    outs = {"o_y": (nu, P, NT), "o_dns_p": (P, DN_H, P), "o_dns_s": (DN_H, P, DEC_B, P),
            "o_dnconv": (P, QKV * (DEC_B + 1) * (DN_TAPS - 1)), "o_ffconv": (2, P, 2 * FF * (DEC_B + 1) * (FF_TAPS - 1)),
            "o_k": (P, SBC, NT), "o_v": (P, NCH, SBC * P), "o_vs": (NS, SBC * P), "o_mkv": (P, 2 * 2 * 2 * N_MEM)}
    nc = Bacc("TRN2", target_bir_lowering=False, num_devices=1)
    d = {n: nc.dram_tensor(f"in_{n}", a.shape, mybir.dt.from_np(a.dtype), kind="ExternalInput").ap() for n, a in arrays.items()}
    d.update({n: nc.dram_tensor(n, s, F32, kind="ExternalOutput").ap() for n, s in outs.items()})
    build(nc, d)
    r = run_bass_kernel_spmd(nc, [{f"in_{n}": a for n, a in arrays.items()}], core_ids=[0]).results[0]

    y = r["o_y"].transpose(2, 0, 1).reshape(NT, D_MODEL)

    def unchunk(a, n, taps):
        a = a.reshape(P, n, DEC_B + 1, taps).transpose(2, 3, 1, 0)
        return a.reshape(DEC_B + 1, taps, n * P)

    def unhalve(a):
        return a.reshape(a.shape[:-1] + (FF, 2, P)).swapaxes(-3, -2).reshape(a.shape)

    dc = unchunk(r["o_dnconv"], QKV, DN_TAPS - 1)
    fc = np.stack([unhalve(unchunk(r["o_ffconv"][l], 2 * FF, FF_TAPS - 1)) for l in range(2)])
    k = r["o_k"].transpose(2, 1, 0).reshape(NT, SB_H, DH)
    vp = r["o_v"].transpose(1, 0, 2).reshape(1, SEQ, SB_H, DH)
    mkv = r["o_mkv"].reshape(P, 2, 2, 2, N_MEM)
    mk = mkv[:, :, 0].transpose(1, 3, 2, 0).reshape(2, 1, N_MEM, 4, DH)
    mv = mkv[:, :, 1].transpose(1, 2, 0, 3).reshape(2, 1, N_MEM, 4, DH)
    return (A(y[:SEQ]).reshape(1, SEQ, D_MODEL), A(y[SEQ:]).reshape(DEC_B, DEC_T, D_MODEL),
            A(r["o_dns_p"].transpose(1, 0, 2))[None, None], A(dc[0:1])[None], A(fc[:, 0:1]),
            A(k[:SEQ])[None], A(vp), A(mk), A(mv),
            A(r["o_dns_s"].transpose(2, 0, 1, 3))[None], A(dc[1:])[None], A(fc[:, 1:]),
            A(k[SEQ:]).reshape(DEC_B, DEC_T, SB_H, DH), A(r["o_vs"]).reshape(DEC_B, DEC_T, SB_H, DH))
```
